# Optimizing a Trainium2 kernel written in Bass

```python
import math
import jax, jax.numpy as jnp
from jax import lax
import numpy as np

D_MODEL = 1024
BATCH = 1
SEQ = 128
DEPTH = 1
DEC_BATCH = 1
DEC_SEQ = 1024
PAST_LEN = 256

GRID_W = 64
D_SSM = 512
D_POOL = 256
D_CONV = 256
D_MIX = D_SSM + D_POOL + D_CONV
D_IN = D_SSM + D_POOL + 2 * D_CONV
SSM_GROUP = 16
N_SSM_GROUPS = D_SSM // SSM_GROUP
SSM_STATE = 64
POOL_WINDOWS = (2, 4, 8, 16)
N_POOL_GROUPS = len(POOL_WINDOWS)
POOL_GROUP = D_POOL // N_POOL_GROUPS
CONV_WIDTH = 31
D_FF = int(math.ceil(8 * D_MODEL / 3 / 256)) * 256
EPS = 1e-6
F32 = jnp.float32

kernel_name = 'hybrid_s5_pool_conformer_diffusion_step'

def _rmsnorm(x, g):
    xf = x.astype(F32)
    y = xf * lax.rsqrt(jnp.mean(xf * xf, axis=-1, keepdims=True) + EPS)
    return (y * g.astype(F32)).astype(x.dtype)

def _adaln(cond, w, b):
    return jax.nn.silu(cond) @ w + b

def _grid_pos_embed(rows, width, d):
    q = d // 4
    omega = 1.0 / (10000.0 ** (jnp.arange(q, dtype=F32) / q))
    t = jnp.arange(rows * width)
    r = (t // width).astype(F32)[:, None] * omega[None]
    cl = (t % width).astype(F32)[:, None] * omega[None]
    return jnp.concatenate([jnp.sin(r), jnp.cos(r), jnp.sin(cl), jnp.cos(cl)], axis=-1)

def _diag_scan(bu, lam_bar, h0, reverse):
    idx = -1 if reverse else 0
    bu = bu.at[:, idx].add(lam_bar[None] * h0)
    a = jnp.broadcast_to(lam_bar, bu.shape)

    def combine(e1, e2):
        a1, b1 = e1
        a2, b2 = e2
        return a1 * a2, a2 * b1 + b2

    _, h = lax.associative_scan(combine, (a, bu), axis=1, reverse=reverse)
    return h

def _ssm_mixer(u, h0_f, h0_b, p, l):
    Bn, L, _ = u.shape
    uf = u.astype(F32)
    ug = uf.reshape(Bn, L, N_SSM_GROUPS, SSM_GROUP).astype(jnp.complex64)
    y = uf * p['ssm_d'][l].astype(F32)
    finals = []
    for di, (h0, rev) in enumerate(((h0_f, False), (h0_b, True))):
        lam = lax.complex(p['ssm_lam_re'][l, di].astype(F32), p['ssm_lam_im'][l, di].astype(F32))
        dt = jnp.exp(p['ssm_log_dt'][l, di].astype(F32))[:, None]
        lam_bar = jnp.exp(lam * dt)
        bmat = lax.complex(p['ssm_b_re'][l, di].astype(F32), p['ssm_b_im'][l, di].astype(F32))
        b_bar = ((lam_bar - 1.0) / lam)[..., None] * bmat
        bu = jnp.einsum('blgh,gph->blgp', ug, b_bar)
        h = _diag_scan(bu, lam_bar, h0, rev)
        cmat = lax.complex(p['ssm_c_re'][l, di].astype(F32), p['ssm_c_im'][l, di].astype(F32))
        y = y + jnp.einsum('blgp,ghp->blgh', h, cmat).real.reshape(Bn, L, D_SSM)
        finals.append(h[:, 0] if rev else h[:, -1])
    y = jax.nn.gelu(y)
    y = y * jax.nn.sigmoid(y @ p['ssm_w_glu'][l].astype(F32) + p['ssm_b_glu'][l].astype(F32))
    return y.astype(u.dtype), finals

def _pool_mixer(u, p, l):
    Bn, L, _ = u.shape
    uf = u.astype(F32)
    csum = jnp.concatenate([jnp.zeros((Bn, 1, D_POOL), F32), jnp.cumsum(uf, axis=1)], axis=1)
    t = np.arange(L)
    outs = []
    for gi, w in enumerate(POOL_WINDOWS):
        lo = np.maximum(t - w // 2, 0)
        hi = np.minimum(t + w // 2, L)
        cnt = jnp.asarray((hi - lo).astype(np.float32))[None, :, None]
        sl = slice(gi * POOL_GROUP, (gi + 1) * POOL_GROUP)
        seg = csum[:, :, sl]
        outs.append((seg[:, hi] - seg[:, lo]) / cnt - uf[:, :, sl])
    pooled = jnp.stack(outs, axis=2)
    y = jnp.einsum('blgc,gcd->blgd', pooled, p['pool_w'][l].astype(F32)).reshape(Bn, L, D_POOL)
    return (y * p['pool_scale'][l].astype(F32)).astype(u.dtype)

def _conv_mixer(u, p, l):
    a, g = jnp.split(u, 2, axis=-1)
    v = a * jax.nn.sigmoid(g)
    filt = p['conv_dw_w'][l].astype(v.dtype)[:, None, :]
    pad = CONV_WIDTH // 2
    v = lax.conv_general_dilated(v, filt, window_strides=(1,), padding=[(pad, pad)],
                                 dimension_numbers=('NWC', 'WIO', 'NWC'),
                                 feature_group_count=D_CONV) + p['conv_dw_b'][l]
    vf = v.astype(F32)
    mu = jnp.mean(vf, axis=-1, keepdims=True)
    var = jnp.mean(jnp.square(vf - mu), axis=-1, keepdims=True)
    vn = (vf - mu) * lax.rsqrt(var + EPS) * p['conv_ln_g'][l].astype(F32) + p['conv_ln_b'][l].astype(F32)
    return jax.nn.silu(vn).astype(u.dtype)

def _layer(x, mod, l, h0_f, h0_b, p):
    sh1, sc1, g1, sh2, sc2, g2 = jnp.split(mod[:, None, :].astype(x.dtype), 6, axis=-1)
    h = _rmsnorm(x, p['norm1_g'][l]) * (1.0 + sc1) + sh1
    z = h @ p['w_in'][l]
    u_ssm = z[..., :D_SSM]
    u_pool = z[..., D_SSM:D_SSM + D_POOL]
    u_conv = z[..., D_SSM + D_POOL:]
    y_ssm, finals = _ssm_mixer(u_ssm, h0_f, h0_b, p, l)
    y_pool = _pool_mixer(u_pool, p, l)
    y_conv = _conv_mixer(u_conv, p, l)
    y = jnp.concatenate([y_ssm, y_pool, y_conv], axis=-1) @ p['w_out'][l]
    x = x + g1 * y
    h2 = _rmsnorm(x, p['norm2_g'][l]) * (1.0 + sc2) + sh2
    f = (jax.nn.silu(h2 @ p['ffn_w1'][l]) * (h2 @ p['ffn_w3'][l])) @ p['ffn_w2'][l]
    return x + g2 * f, finals

def setup_inputs(seed: int = 0) -> dict:
    key = jax.random.key(seed)
    ks = iter(jax.random.split(key, 48))

    def nrm(shape, s):
        return jax.random.normal(next(ks), shape, F32) * s

    G, P, H = N_SSM_GROUPS, SSM_STATE, SSM_GROUP
    lam_im0 = jnp.broadcast_to(math.pi * jnp.arange(P, dtype=F32), (DEPTH, 2, G, P))
    return {
        'x_prompt': nrm((BATCH, SEQ, D_MODEL), 1.0),
        'x_sample': nrm((DEC_BATCH, DEC_SEQ, D_MODEL), 1.0),
        'state_ssm_re': nrm((DEC_BATCH, DEPTH, 2, G, P), 0.5),
        'state_ssm_im': nrm((DEC_BATCH, DEPTH, 2, G, P), 0.5),
        'c': nrm((DEC_BATCH, D_MODEL), 1.0),
        'c_ctx': nrm((D_MODEL,), 1.0),
        'ada_w': nrm((DEPTH, D_MODEL, 6 * D_MODEL), 0.5 * D_MODEL ** -0.5),
        'ada_b': nrm((DEPTH, 6 * D_MODEL), 0.01),
        'norm1_g': 1.0 + nrm((DEPTH, D_MODEL), 0.05),
        'w_in': nrm((DEPTH, D_MODEL, D_IN), D_MODEL ** -0.5),
        'ssm_lam_re': -0.5 + nrm((DEPTH, 2, G, P), 0.01),
        'ssm_lam_im': lam_im0 + nrm((DEPTH, 2, G, P), 0.01),
        'ssm_log_dt': jax.random.uniform(next(ks), (DEPTH, 2, G), F32, math.log(1e-3), math.log(1e-1)),
        'ssm_b_re': nrm((DEPTH, 2, G, P, H), (2 * H) ** -0.5),
        'ssm_b_im': nrm((DEPTH, 2, G, P, H), (2 * H) ** -0.5),
        'ssm_c_re': nrm((DEPTH, 2, G, H, P), (2 * P) ** -0.5 * 2.0),
        'ssm_c_im': nrm((DEPTH, 2, G, H, P), (2 * P) ** -0.5 * 2.0),
        'ssm_d': nrm((DEPTH, D_SSM), 1.0),
        'ssm_w_glu': nrm((DEPTH, D_SSM, D_SSM), D_SSM ** -0.5),
        'ssm_b_glu': nrm((DEPTH, D_SSM), 0.01),
        'pool_w': nrm((DEPTH, N_POOL_GROUPS, POOL_GROUP, POOL_GROUP), POOL_GROUP ** -0.5),
        'pool_scale': 1.0 + nrm((DEPTH, D_POOL), 0.1),
        'conv_dw_w': nrm((DEPTH, CONV_WIDTH, D_CONV), CONV_WIDTH ** -0.5),
        'conv_dw_b': nrm((DEPTH, D_CONV), 0.01),
        'conv_ln_g': 1.0 + nrm((DEPTH, D_CONV), 0.05),
        'conv_ln_b': nrm((DEPTH, D_CONV), 0.01),
        'w_out': nrm((DEPTH, D_MIX, D_MODEL), D_MIX ** -0.5),
        'norm2_g': 1.0 + nrm((DEPTH, D_MODEL), 0.05),
        'ffn_w1': nrm((DEPTH, D_MODEL, D_FF), D_MODEL ** -0.5),
        'ffn_w3': nrm((DEPTH, D_MODEL, D_FF), D_MODEL ** -0.5),
        'ffn_w2': nrm((DEPTH, D_FF, D_MODEL), D_FF ** -0.5),
        'final_g': 1.0 + nrm((D_MODEL,), 0.05),
    }

def reference(x_prompt, x_sample, state_ssm_re, state_ssm_im, c, c_ctx, ada_w, ada_b, norm1_g, w_in,
              ssm_lam_re, ssm_lam_im, ssm_log_dt, ssm_b_re, ssm_b_im, ssm_c_re, ssm_c_im, ssm_d,
              ssm_w_glu, ssm_b_glu, pool_w, pool_scale, conv_dw_w, conv_dw_b, conv_ln_g, conv_ln_b,
              w_out, norm2_g, ffn_w1, ffn_w3, ffn_w2, final_g):
    p = {'norm1_g': norm1_g, 'w_in': w_in, 'ssm_lam_re': ssm_lam_re, 'ssm_lam_im': ssm_lam_im,
         'ssm_log_dt': ssm_log_dt, 'ssm_b_re': ssm_b_re, 'ssm_b_im': ssm_b_im, 'ssm_c_re': ssm_c_re,
         'ssm_c_im': ssm_c_im, 'ssm_d': ssm_d, 'ssm_w_glu': ssm_w_glu, 'ssm_b_glu': ssm_b_glu,
         'pool_w': pool_w, 'pool_scale': pool_scale, 'conv_dw_w': conv_dw_w, 'conv_dw_b': conv_dw_b,
         'conv_ln_g': conv_ln_g, 'conv_ln_b': conv_ln_b, 'w_out': w_out, 'norm2_g': norm2_g,
         'ffn_w1': ffn_w1, 'ffn_w3': ffn_w3, 'ffn_w2': ffn_w2}

    xc = x_prompt
    bc = x_prompt.shape[0]
    h0 = jnp.zeros((bc, N_SSM_GROUPS, SSM_STATE), jnp.complex64)
    per_layer = []
    for l in range(DEPTH):
        mod_ctx = _adaln(c_ctx[None, :], ada_w[l], ada_b[l])
        xc, (hf, hb) = _layer(xc, mod_ctx, l, h0, h0, p)
        per_layer.append(jnp.stack([hf, hb], axis=1))
    st = jnp.stack(per_layer, axis=1)
    new_state_ssm_re = st.real
    new_state_ssm_im = st.imag
    y_prompt = _rmsnorm(xc, final_g)

    L = x_sample.shape[1]
    rows = L // GRID_W
    xs = x_sample + _grid_pos_embed(rows, GRID_W, D_MODEL).astype(x_sample.dtype)[None]
    for l in range(DEPTH):
        mod = _adaln(c, ada_w[l], ada_b[l])
        h0_f = lax.complex(state_ssm_re[:, l, 0].astype(F32), state_ssm_im[:, l, 0].astype(F32))
        h0_b = lax.complex(state_ssm_re[:, l, 1].astype(F32), state_ssm_im[:, l, 1].astype(F32))
        xs, _ = _layer(xs, mod, l, h0_f, h0_b, p)
    y_sample = _rmsnorm(xs, final_g)

    return (y_prompt, y_sample, new_state_ssm_re, new_state_ssm_im)


_drawn_inputs = setup_inputs


def setup_inputs(seed=0):
    import zlib

    import numpy as np

    out = dict(_drawn_inputs(seed))
    spreads = {}
    factors = {'ada_b': 3.022,
     'ssm_lam_re': 19.568,
     'ssm_b_glu': 64.0,
     'pool_scale': 3.943,
     'conv_dw_b': 8.0,
     'conv_ln_g': 8.0,
     'conv_ln_b': 58.898,
     'norm2_g': 4.03,
     'state_ssm_re': 4.513,
     'state_ssm_im': 4.593,
     'ssm_c_re': 4.225,
     'ssm_c_im': 4.206}
    for name, (base, spread) in spreads.items():
        noise = np.random.default_rng([zlib.crc32(name.encode()), seed]).standard_normal(out[name].shape)
        drawn = base * np.exp(spread * noise) if base else spread * noise
        out[name] = __import__('jax').numpy.asarray(drawn.astype(out[name].dtype))
    for name, factor in factors.items():
        out[name] = (out[name] * factor).astype(out[name].dtype)
    return out
```

```python
from contextlib import ExitStack

import numpy as np
import concourse.bass as bass
from concourse import mybir

F32 = mybir.dt.float32
F32R = mybir.dt.float32r
ACT = mybir.ActivationFunctionType
ALU = mybir.AluOpType

P = 128
D = 1024
KT = D // P
LAT, CTX = 1024, 128
T = LAT + CTX
NB, BW = 3, 384
NT = T // P
GRID_W = 64
D_IN = 1280
DFF = 2816
EPS = 1e-6

CH = 8
G, NS, HD = 32, 64, 16
Q = G
NPAIR = G // 2
LC, CC = LAT // CH, CTX // CH
UC = LC + 1 + CC
SLOTS = UC + 1
BSH = CC + 1
NPOW = CH + 1

FB = 2
NFB = DFF // P // FB
TWO_PI = 6.283185307179586
TP1 = 6.28125
TP2 = float(np.float32(TWO_PI - TP1))
TP3 = float(TWO_PI - TP1 - np.float32(TWO_PI - TP1))
ROUND = 12582912.0

V_N1, V_N2, V_GB, V_PS, V_CB, V_LG, V_LB, V_CX, V_CC = 0, 8, 16, 20, 22, 24, 26, 28, 36
VR = 44
TAPS = 31
PAD = TAPS // 2
VL = PAD + LAT + PAD + CTX + PAD
VO = LAT + PAD + CTX
VCTX = LAT + PAD
PZ = 8
PL = PZ + LAT + PZ + CTX + PZ


def view(t, off, dims, p0=0, n=P):
    full = t[:]
    ps = full.ap[0][0]
    return bass.AP(tensor=full.tensor, offset=full.offset + p0 * ps + off, ap=[[ps, n]] + [list(d) for d in dims])


def dview(ap, off, dims):
    return bass.AP(tensor=ap.tensor, offset=ap.offset + off, ap=[list(d) for d in dims])


def build(nc, A, O):
    ctx = ExitStack()

    def at(name, shape, off, dt=F32):
        n = int(np.prod(shape[1:])) * 4
        assert off % 32 == 0 and off + n <= LIMIT, (name, off + n)
        return nc.alloc_sbuf_tensor_at(name, shape, dt, offset=off)

    LIMIT = 229368
    O_NT = 16512
    O_WB = O_NT + 2 * KT * T * 4
    O_UZ = O_WB + 2 * Q * P * 4
    O_ST = O_UZ + 18560
    O_WS = O_ST + 2 * Q * SLOTS * 4
    O_BC = O_WS + 24576
    O_C = O_BC + 16384

    cur = [O_C]

    def const(name, shape, dt=F32):
        n = int(np.prod(shape[1:])) * 4
        t = at(name, shape, cur[0], dt)
        cur[0] += (n + 31) // 32 * 32
        return t

    ident = const("ident", [P, P])
    onesm = const("onesm", [P, P])
    X_TAP = VR
    X_LRE, X_LIM, X_HRE, X_HIM, X_DT = (VR + 2 * TAPS + Q * i for i in range(5))
    NPV = VR + 2 * TAPS + 5 * Q
    pv = const("pv", [P, NPV])
    dcol = const("dcol", [32, NPAIR])
    condT = const("condT", [P, KT, 32])
    modc = const("modc", [P, 48, 2])
    gsc = const("gsc", [P, 2, KT, 2])
    O_POW = cur[0]
    powr = const("powr", [P, NPOW, Q])
    powi = const("powi", [P, NPOW, Q])
    a8i = const("a8i", [P, 2, Q])
    ss = const("ss", [P, 2 * NT])
    rstd = const("rstd", [P, NT])
    ss2 = const("ss2", [P, 2 * NT])
    rstd2 = const("rstd2", [P, NT])
    var = const("var", [P, NT])
    var2 = const("var2", [P, NT])
    edge = const("edge", [P, 34])
    scT = const("scT", [P, 3, 2, Q])
    dsel = const("dsel", [32, NPAIR, HD])
    a8r = const("a8r", [P, Q])

    nt_hi = at("nt_hi", [P, KT, T], O_NT, F32R)
    nt_lo = at("nt_lo", [P, KT, T], O_NT + KT * T * 4, F32R)
    raw = [at(f"raw{i}", [32, 2 * HD * NS], O_WB + i * 8192) for i in range(4)]
    xt = [at(f"xt{i}", [P, D], O_UZ + i * 4096) for i in range(4)]
    posc = at("posc", [P, 512], O_UZ + 16384)
    posr = [at(f"posr{i}", [P, 512], O_BC + 8192 + i * 2048) for i in range(2)]
    o = O_ST
    wbt_tmp = [at(f"wbt_tmp{i}", [P, 4, P], o + 2048 * i) for i in range(2)]
    o += 4096
    wbt = [[at(f"wbt{s}{r}", [P, 4, P], o + 2048 * (2 * s + r)) for r in range(2)] for s in range(2)]
    o += 8192
    NC = NPOW * HD
    wct_tmp = [at(f"wct_tmp{i}", [P, 4, NC], o + 2304 * i) for i in range(2)]
    o += 4608
    wct = [[at(f"wct{s}{r}", [P, 4, NC], o + 2304 * (2 * s + r)) for r in range(2)] for s in range(2)]
    o += 9216
    prm = at("prm", [P, 16, Q], o)
    o += 2048
    hf = [at(f"hf{i}", [P, 512], o + 2048 * i) for i in range(2)]
    o += 4096
    arow = [at("arow0", [P, 512], o), at("arow1", [P, 512], O_WS + 20480), at("arow2", [P, 512], O_POW)]
    abias = [at("abias0", [P, 512], o + 2048)] + [at("abias1", [P, 512], O_WS + 18432)] * 2
    o += 4096
    assert o <= O_WS
    o = O_BC + 12288
    rows = at("rows", [VR, P], o)
    rtap = at("rtap", [2 * TAPS, P], o + 512)
    rlam = at("rlam", [Q, 5, P], o + 1024)
    dn = at("dn", [NPAIR, 2 * HD], o + 3584)
    ldt = at("ldt", [Q, 2], o + 3712)
    assert o + 3744 <= O_C
    wb = at("wb", [P, 2, Q, P], O_WB)
    u8 = [at(f"u8{i}", [P, 8, UC], O_UZ + 4640 * i) for i in range(2)]
    zp = [at(f"zp{i}", [P, CH, UC], O_UZ + 9280 + 4640 * i) for i in range(2)]
    st = at("st", [P, 2 * Q * SLOTS], O_ST)
    wst = [at(f"wst{i}", [P, KT, P], O_WS + 4096 * i) for i in range(2)]
    w_hi = [at(f"w_hi{i}", [P, KT, P], O_WS + 8192 + 8192 * i, F32R) for i in range(2)]
    w_lo = [at(f"w_lo{i}", [P, KT, P], O_WS + 12288 + 8192 * i, F32R) for i in range(2)]
    ad0 = [at(f"ad0{i}", [P, 2048], O_WS + 8192 + 8192 * i) for i in range(2)]
    bb = at("bb", [P, 2, Q, HD], O_BC)
    cc = at("cc", [P, 2, Q, HD], O_BC + 4096)
    bblk = at("bblk", [P, 2, Q, 32], O_BC + 8192)
    pu = at("pu", [P, 2, PL], O_WB)
    psum_w = at("psum_w", [P, 2, PL], O_WB + 9408)
    vp = at("vp", [P, 2, VL], O_WB + 18816)
    cacc = at("cacc", [P, 2, VO], O_UZ)
    sig = at("sig", [P, 2, T], O_UZ + 9344)
    wpool = at("wpool", [P, 2, P], O_WB + 28416)
    fin = at("fin", [Q, 2, P], O_WB + 29440)
    scC = at("scC", [P, 3, 2, Q], O_WB + 30464)
    u9 = [at(f"u9{i}", [P, 8, UC], O_WB + 9408 + 4640 * i) for i in range(2)]
    wc = at("wc", [P, 2, Q, NC], O_NT)
    toep = at("toep", [P, G, P], O_NT + 36864)
    kb = at("kb", [32, NPAIR, 15 * HD], O_NT + 53248)
    ad1 = [at(f"ad1{i}", [P, 2048], O_NT + 53248 + 8192 * i) for i in range(2)]
    yT = at("yT", [P, 4, CH * UC], O_NT + 53248)
    yb = [at(f"yb{i}", [P, 8, UC], O_WB + 4640 * i) for i in range(2)]
    ymp = at("ymp", [P, 4, T], O_WS)
    yms = at("yms", [P, 4, T], O_ST)
    wglu = at("wglu", [P, 4, 512], O_NT)
    gsig = at("gsig", [P, CH * UC], O_NT + 8192)
    wo = [at("wo1", [P, 4, D], O_BC), at("wo2", [P, 4, D], O_ST + 18432)]
    lnw = at("lnw", [P, 2, VO], O_WB + 18816)
    o = O_WB
    xr = [at(f"xr{i}", [P, D], o + 4096 * i) for i in range(3)]
    o += 12288
    g1b = at("g1b", [P, 2, D], o)
    o += 8192
    posr2 = [at(f"posr2{i}", [P, 512], o + 2048 * i) for i in range(2)]
    posc2 = at("posc2", [P, 512], o + 4096)
    o += 6144
    xn2 = at("xn2", [P, D], o)
    assert o + 4096 <= O_UZ
    tg = at("tg", [P, 512], O_UZ)
    h2f = at("h2f", [P, KT, P], O_UZ + 2048)
    o = O_NT + 2 * KT * T * 4
    f_hi = at("f_hi", [P, FB, T], o, F32R)
    f_lo = at("f_lo", [P, FB, T], o + FB * T * 4, F32R)
    o += 2 * FB * T * 4
    sa = [at(f"sa{i}", [P, BW], o + 1536 * i) for i in range(2)]
    fv = [at(f"fv{i}", [P, BW], o + 3072 + 1536 * i) for i in range(2)]
    o += 6144
    fst = [at(f"fst{i}", [P, D], o + 4096 * i) for i in range(3)]
    o += 12288
    acc = at("acc", [P, NT, D], o)
    o += NT * D * 4
    f13h = [at(f"f13h{i}", [P, 2, KT, P], o + 16384 * i, F32R) for i in range(2)]
    f13l = [at(f"f13l{i}", [P, 2, KT, P], o + 8192 + 16384 * i, F32R) for i in range(2)]
    o += 32768
    f2h = at("f2h", [P, FB, D], o, F32R)
    f2l = at("f2l", [P, FB, D], o + 8192, F32R)
    assert o + 16384 <= O_C, o + 16384 - O_C
    o = O_NT
    g2b = at("g2b", [P, 2, D], o)
    fgb = at("fgb", [P, D], o + 8192)
    xe = [at(f"xe{i}", [P, D], o + 12288 + 4096 * i) for i in range(3)]
    te = [at(f"te{i}", [P, D], o + 24576 + 4096 * i) for i in range(2)]

    PS = [nc.alloc_psum_tensor(f"bank{i}", [P, 512], F32) for i in range(8)]
    z_dram = nc.dram_tensor("z_dram", [512, CH, UC], F32).ap()
    y_dram = nc.dram_tensor("y_dram", [512, CH, UC], F32).ap()
    wc_dram = nc.dram_tensor("wc_dram", [P, 2, Q, NC], F32).ap()
    kb_dram = nc.dram_tensor("kb_dram", [32, NPAIR, 15 * HD], F32).ap()
    x2_dram = nc.dram_tensor("x2_dram", [T, D], F32).ap()


    sems = {}

    def sem(name):
        if name not in sems:
            sems[name] = nc.alloc_semaphore(name)
        return sems[name]

    ZB = [4, 5, 6]
    VB = [2, 3, 7]
    GB = [(0, 3 * UC), (3 * UC, 3 * UC), (6 * UC, 2 * UC)]
    XG = [range(0, 4), range(4, 8), range(8, 9)]

    def x_tile(i):
        return dview(A["x_sample"], i * P * D, [[D, P], [1, D]]) if i < 8 else dview(A["x_prompt"], 0, [[D, P], [1, D]])

    def pos_tile(i):
        return dview(A["pos_rows"], 2 * i * 512, [[512, 2], [0, GRID_W], [1, 512]])

    pos_cols2 = dview(A["pos_cols"], 0, [[0, 2], [512, GRID_W], [1, 512]])

    def piece_count(n, c):
        return 16 * (c // 3 + 1) + (n - c) // 6 * 32 if isinstance(n, int) else (n - c) * 16 // 3 + 16 * (c // 3 + 1)

    def piece(c):
        c2 = c - 6 if c >= 6 else c
        if c2 < 4:
            return (f13h[c2 // 2][:, c2 % 2, :, :], f13l[c2 // 2][:, c2 % 2, :, :],
                    fst[c % 3][:, :].rearrange("p (k n) -> p k n", n=P))
        return f2h[:, c2 - 4, :], f2l[:, c2 - 4, :], fst[c % 3][:, :]

    block = ctx.enter_context(nc.Block())

    def y_out(sp, i):
        sp.wait_ge(sem("y_made"), i + 1)
        dst = dview(O[1], i * P * D, [[D, P], [1, D]]) if i < 8 else dview(O[0], 0, [[D, P], [1, D]])
        sp.dma_start(dst, xe[i % 3][:, :]).then_inc(sem(f"tile_out{i % 3}"), 16)

    @block.sync
    def _(sp):
        def x_in(i):
            sp.dma_start(xt[i % 4][:, :], x_tile(i)).then_inc(sem(f"x{i % 4}_in"), 16)
            if i < 8:
                if i >= 2:
                    sp.wait_ge(sem("pos_added"), i - 1)
                sp.dma_start(posr[i % 2][:, :], pos_tile(i)).then_inc(sem(f"posr{i % 2}_in"), 16)

        def ada_bias(a):
            for q in range(4):
                sp.dma_start(abias[a][32 * q:32 * q + 32, :],
                             dview(A["ada_b"], a * 2048 + q * 512, [[0, 32], [1, 512]])).then_inc(sem(f"ada_bias{a}_in"), 16)

        def ada_in(slots, n):
            a, k = n // KT, n % KT
            sp.dma_start(slots[k % 2][:, :],
                         dview(A["ada_w"], k * P * 6 * D + a * 2048, [[6 * D, P], [1, 2048]])).then_inc(sem(f"ada{k % 2}_in"), 16)

        def w_in_load(i):
            sp.dma_start(wst[i % 2][:, :, :], dview(A["w_in"], i * P, [[D_IN, P], [P * D_IN, KT], [1, P]])).then_inc(sem(f"w_in{i % 2}_in"), 16)

        for name, r0, n in (("norm1_g", V_N1, 8), ("norm2_g", V_N2, 8), ("ssm_b_glu", V_GB, 4), ("pool_scale", V_PS, 2),
                            ("conv_dw_b", V_CB, 2), ("conv_ln_g", V_LG, 2), ("conv_ln_b", V_LB, 2),
                            ("c_ctx", V_CX, 8), ("c", V_CC, 8)):
            sp.dma_start(rows[r0:r0 + n, :], dview(A[name], 0, [[P, n], [1, P]])).then_inc(sem("vectors_in"), 16)
        sp.dma_start(rtap[:, :], dview(A["conv_dw_w"], 0, [[P, 2 * TAPS], [1, P]])).then_inc(sem("vectors_in"), 16)
        for i, name in enumerate(("ssm_lam_re", "ssm_lam_im", "state_ssm_re", "state_ssm_im")):
            sp.dma_start(rlam[:, i, :], dview(A[name], 0, [[P, Q], [1, P]])).then_inc(sem("vectors_in"), 16)
        sp.dma_start(dn[:, :], dview(A["ssm_d"], 0, [[32, NPAIR], [1, 32]])).then_inc(sem("vectors_in"), 16)
        sp.dma_start(ldt[:, :], dview(A["ssm_log_dt"], 0, [[2, Q], [1, 2]])).then_inc(sem("log_dt_in"), 16)
        ada_in(ad0, 0)
        ada_in(ad0, 1)
        sp.dma_start(posc[:, :], pos_cols2).then_inc(sem("posc_in"), 16)
        ada_bias(0)
        for i in range(2):
            x_in(i)
        for i, name in enumerate(("ssm_b_re", "ssm_b_im", "ssm_c_re", "ssm_c_im")):
            if i < 2:
                sp.dma_start(raw[i][:, :], dview(A[name], 0, [[2048, Q], [1, 2048]])).then_inc(sem("raws_in"), 16)
            else:
                for par in range(2):
                    sp.dma_start(view(raw[i], par * NS, [[P, HD], [1, NS]], 0, Q),
                                 dview(A[name], par * HD * NS, [[2048, Q], [NS, HD], [1, NS]])).then_inc(sem("raws_in"), 16)
        x_in(2)
        x_in(3)
        sp.dma_start(edge[:, :], A["pool_edges"]).then_inc(sem("edges_in"), 16)
        for n in range(2, KT):
            sp.wait_ge(sem("ada_tile"), n - 1)
            ada_in(ad0, n)
        w_in_load(0)
        w_in_load(1)
        for i in range(4, NT):
            sp.wait_ge(sem("xT_bank"), 8 * (i // 4))
            x_in(i)
        for i in range(10):
            if i + 2 < 10:
                sp.wait_ge(sem("w_in_lo"), i + 1)
                w_in_load(i + 2)
            if i < 4:
                sp.wait_ge(sem("z_evac"), NB * (i + 1))
                sp.wait_ge(sem("zero_column"), 2)
                sp.dma_start(dview(z_dram, i * P * CH * UC, [[CH * UC, P], [1, CH * UC]]),
                             view(zp[i % 2], 0, [[1, CH * UC]])).then_inc(sem("z_out"), 16)
                sp.wait_ge(sem("z_out"), 16 * (i + 1))
                if i >= 2:
                    sp.wait_ge(sem("v_done"), 8 * (i - 1))
                for s in range(CH):
                    sp.dma_start(u8[i % 2][16 * s:16 * s + 16, :, :],
                                 dview(z_dram, i * P * CH * UC + s * UC, [[CH * UC, 16], [16 * CH * UC, 8], [1, UC]])).then_inc(sem(f"u{i}_in"), 16)
        sp.wait_ge(sem("wpool_zero"), 1)
        for g in range(4):
            h = 64 * (g % 2)
            sp.dma_start(wpool[h:h + 64, g // 2, h:h + 64], dview(A["pool_w"], g * 4096, [[64, 64], [1, 64]])).then_inc(sem("wpool_in"), 16)
        sp.wait_ge(sem("z_done"), 30)
        for s in range(2):
            sp.wait_ge(sem(f"wc_out{s}"), 128)
        sp.dma_start(wc[:, :, :, :], wc_dram).then_inc(sem("wc_in"), 16)
        for a in (1, 2):
            if a == 2:
                sp.wait_ge(sem("ada_bank"), 2)
            ada_bias(a)
            for n in range(KT * a, KT * a + KT):
                if n >= KT + 2:
                    sp.wait_ge(sem("ada_tile"), n - 1)
                ada_in(ad1, n)
        sp.wait_ge(sem("kb_evac"), 8)
        sp.dma_start(kb_dram, kb[:, :, :]).then_inc(sem("kb_out"), 16)
        sp.wait_ge(sem("kb_out"), 16)
        RK = NPAIR * 15 * HD
        for s in range(CH):
            for par in range(2):
                sp.dma_start(view(toep, par * P, [[2 * P, NPAIR], [1, P]], 16 * s, 16),
                             dview(kb_dram, par * 16 * RK + (CH - 1 - s) * HD, [[RK, 16], [15 * HD, NPAIR], [1, P]])).then_inc(sem("toep_in"), 16)
        sp.dma_start(wo[0][:, :, :], dview(A["w_out"], 0, [[D, P], [P * D, 4], [1, D]])).then_inc(sem("wo0_in"), 16)
        def u_again(j):
            for s in range(CH):
                sp.dma_start(u9[j % 2][16 * s:16 * s + 16, :, :],
                             dview(z_dram, j * P * CH * UC + s * UC, [[CH * UC, 16], [16 * CH * UC, 8], [1, UC]])).then_inc(sem(f"u{j}_in"), 16)

        sp.wait_ge(sem("pooled"), 2)
        u_again(0)
        u_again(1)
        for r in range(2):
            sp.wait_ge(sem("fin_evac"), r + 1)
            sp.dma_start(dview(O[2 + r], 0, [[P, Q], [1, P]]), fin[:, r, :]).then_inc(sem("outputs"), 16)
        for j in range(4):
            sp.wait_ge(sem("y_evac"), 4 * (j + 1))
            if j + 2 < 4:
                sp.wait_ge(sem("y_done"), 2 * (j + 1))
                u_again(j + 2)
            for t in range(CH):
                sp.dma_start(dview(y_dram, j * P * CH * UC + t * UC, [[CH * UC, 16], [16 * CH * UC, 8], [1, UC]]),
                             yb[j % 2][16 * t:16 * t + 16, :, :]).then_inc(sem("y_out"), 16)
            sp.wait_ge(sem("y_out"), 16 * 8 * (j + 1))
            sp.dma_start(view(yT, j * CH * UC, [[1, CH * UC]]), dview(y_dram, j * P * CH * UC, [[CH * UC, P], [1, CH * UC]])).then_inc(sem("yT_in"), 16)
        sp.wait_ge(sem("y_done"), 8)
        sp.dma_start(wglu[:, :, :], dview(A["ssm_w_glu"], 0, [[512, P], [P * 512, 4], [1, 512]])).then_inc(sem("wglu_in"), 16)
        sp.dma_start(wo[1][:, :, :], dview(A["w_out"], 512 * D, [[D, P], [P * D, 4], [1, D]])).then_inc(sem("wo1_in"), 16)
        sp.wait_ge(sem("conv_out"), 4)
        sp.dma_start(posc2[:, :], pos_cols2).then_inc(sem("posc2_in"), 16)

        def x2_out(i):
            sp.wait_ge(sem("x2_made"), 2 * (i + 1))
            sp.dma_start(dview(x2_dram, i * P * D, [[D, P], [1, D]]), xr[i % 3][:, :]).then_inc(sem(f"tile_out{i % 3}"), 16)

        for i in range(NT):
            if i >= 3:
                sp.wait_ge(sem(f"tile_out{i % 3}"), 16 * (i // 3))
                sp.wait_ge(sem("x2_normed"), i - 2)
            sp.dma_start(xr[i % 3][:, :], x_tile(i)).then_inc(sem(f"xr{i % 3}_in"), 16)
            if i < 8:
                if i >= 2:
                    sp.wait_ge(sem("pos_added"), 8 + i - 1)
                sp.dma_start(posr2[i % 2][:, :], pos_tile(i)).then_inc(sem(f"posr{i % 2}_in"), 16)
            if i >= 1:
                x2_out(i - 1)
        x2_out(NT - 1)
        sp.wait_ge(sem("g1_used"), 2 * NT)
        sp.wait_ge(sem("h2_split"), NT)

        def piece_in(n, c, w, tile, dynamic):
            if dynamic or n >= 3:
                sp.wait_ge(sem("piece_lo"), n - 2)
            dst = fst[c % 3][:, :]
            if w == "ffn_w2":
                src = A[w][0][bass.ds(tile * P, P), :]
            else:
                src = A[w][0].rearrange("(k p) n -> p k n", p=P)[:, :, bass.ds(tile * P, P)]
                dst = dst.rearrange("p (k n) -> p k n", n=P)
            sp.dma_start(dst, src).then_inc(sem(f"piece{c % 3}_in"), 16)

        def pieces_in(it, dynamic, last):
            n0 = 4 + 6 * it
            for f in range(FB):
                piece_in(n0 + f, 4 + f, "ffn_w2", FB * it + f, dynamic)
            if not last:
                for f in range(FB):
                    for e, w in enumerate(("ffn_w1", "ffn_w3")):
                        piece_in(n0 + 2 + 2 * f + e, 6 + 2 * f + e, w, FB * (it + 1) + f, dynamic)

        for f in range(FB):
            for e, w in enumerate(("ffn_w1", "ffn_w3")):
                piece_in(2 * f + e, 2 * f + e, w, f, False)
        pieces_in(0, False, False)
        with sp.Fori(1, NFB - 1) as it:
            pieces_in(it, True, False)
        pieces_in(NFB - 1, False, True)
        sp.wait_ge(sem("down_done"), 2 * NT * NFB)
        sp.dma_start(fgb[:, :], dview(A["final_g"], 0, [[0, P], [1, D]])).then_inc(sem("final_g_in"), 16)
        for i in range(NT):
            if i >= 3:
                sp.wait_ge(sem(f"tile_out{i % 3}"), 48 + 16 * (i // 3))
            else:
                sp.wait_ge(sem(f"tile_out{i % 3}"), 48)
            sp.dma_start(xe[i % 3][:, :], dview(x2_dram, i * P * D, [[D, P], [1, D]])).then_inc(sem(f"xr{i % 3}_in"), 16)
            if i >= 2:
                y_out(sp, i - 2)
        y_out(sp, NT - 2)
        y_out(sp, NT - 1)
        sp.wait_ge(sem("outputs"), 32)
        for s in range(3):
            sp.wait_ge(sem(f"tile_out{s}"), 96)

    @block.gpsimd
    def _(pool):
        nc.gpsimd.memset(ident[:, :], 0.0).then_inc(sem("ident0"), 1)
        nc.gpsimd.memset(onesm[:, :], 1.0 / 256).then_inc(sem("ones"), 1)
        pool.wait_ge(sem("ident0"), 1)
        nc.gpsimd.affine_select(out=ident[:, :], in_=ident[:, :], compare_op=ALU.not_equal, fill=1.0,
                                base=0, pattern=[[-1, P]], channel_multiplier=1).then_inc(sem("ident"), 1)
        def pos_add(i):
            if i == 0:
                pool.wait_ge(sem("posc_in"), 16)
            pool.wait_ge(sem(f"x{i % 4}_in"), 16 * (i // 4 + 1))
            pool.wait_ge(sem(f"posr{i % 2}_in"), 16 * (i // 2 + 1))
            nc.gpsimd.tensor_tensor(xt[i % 4][:, 0:512], xt[i % 4][:, 0:512], posr[i % 2][:, :], ALU.add).then_inc(sem("pos_half"), 1)
            nc.gpsimd.tensor_tensor(xt[i % 4][:, 512:1024], xt[i % 4][:, 512:1024], posc[:, :], ALU.add).then_inc(sem("pos_half"), 1)
            pool.wait_ge(sem("pos_half"), 2 * (i + 1))
            pool.sem_inc(sem("pos_added"), 1)

        def wc_piece(n):
            d, q0 = n // 4, 4 * n
            slot, tmp = wct[n % 2], wct_tmp
            step, base = (Q, 0) if d == 0 else (-Q, CH * Q)
            lr = view(powr, base + q0, [[1, 4], [step, NPOW], [0, HD]])
            li = view(powi, base + q0, [[1, 4], [step, NPOW], [0, HD]])
            cr = view(cc, q0 * HD, [[HD, 4], [0, NPOW], [1, HD]])
            ci = view(cc, (Q + q0) * HD, [[HD, 4], [0, NPOW], [1, HD]])

            def v3(t):
                return view(t, 0, [[NC, 4], [HD, NPOW], [1, HD]])
            if n >= 2:
                pool.wait_ge(sem(f"wc_out{n % 2}"), 32 * (n // 2))
            if n >= 1:
                pool.wait_ge(sem("wc_made"), 2 * n)
            nc.gpsimd.tensor_tensor(v3(slot[0]), lr, cr, ALU.mult).then_inc(sem("wc_terms"), 1)
            nc.gpsimd.tensor_tensor(v3(tmp[0]), li, ci, ALU.mult).then_inc(sem("wc_terms"), 1)
            nc.gpsimd.tensor_tensor(v3(slot[1]), lr, ci, ALU.mult).then_inc(sem("wc_terms"), 1)
            nc.gpsimd.tensor_tensor(v3(tmp[1]), li, cr, ALU.mult).then_inc(sem("wc_terms"), 1)
            pool.wait_ge(sem("wc_terms"), 4 * n + 2)
            nc.gpsimd.tensor_tensor(slot[0][:, :, :], slot[0][:, :, :], tmp[0][:, :, :], ALU.add).then_inc(sem("wc_made"), 1)
            pool.wait_ge(sem("wc_terms"), 4 * n + 4)
            nc.gpsimd.tensor_tensor(slot[1][:, :, :], slot[1][:, :, :], tmp[1][:, :, :], ALU.subtract).then_inc(sem("wc_made"), 1)
            pool.wait_ge(sem("wc_made"), 2 * n + 2)
            for r in range(2):
                pool.dma_start(dview(wc_dram, (r * Q + q0) * NC, [[2 * Q * NC, P], [1, 4 * NC]]),
                               view(slot[r], 0, [[1, 4 * NC]])).then_inc(sem(f"wc_out{n % 2}"), 16)

        for i in range(4):
            pos_add(i)
        pool.wait_ge(sem("powers"), 1)
        pool.wait_ge(sem("cc_evac"), 2)
        for n in range(3):
            wc_piece(n)
        for i in range(4, 8):
            pos_add(i)
            if i % 2:
                wc_piece(3 + i // 2 - 2)
        for n in range(5, 8):
            wc_piece(n)
        pool.wait_ge(sem("xT_bank"), 24)
        for s in range(2):
            nc.gpsimd.memset(zp[s][:, :, LC:LC + 1], 0.0).then_inc(sem("zero_column"), 1)
        for r in range(1):
            nc.gpsimd.memset(bblk[:, :, :, :], 0.0).then_inc(sem("bblk0"), 1)
        pool.wait_ge(sem("bblk0"), 1)
        for par in range(2):
            p0 = 64 * par
            nc.gpsimd.tensor_copy(view(bblk, 16 * par, [[32, 2 * Q], [1, HD]], p0, 64),
                                  view(bb, 0, [[HD, 2 * Q], [1, HD]], p0, 64)).then_inc(sem("bblk"), 1)
        pool.wait_ge(sem("bblk"), 2)
        pool.wait_ge(sem("v_done"), 32)
        for j in range(2):
            for o0 in (0, PZ + LAT, PL - PZ):
                nc.gpsimd.memset(pu[:, j, o0:o0 + PZ], 0.0).then_inc(sem("gaps"), 1)
            for o0 in (0, PAD + LAT, VL - PAD):
                nc.gpsimd.memset(vp[:, j, o0:o0 + PAD], 0.0).then_inc(sem("gaps"), 1)
        nc.gpsimd.memset(wpool[:, :, :], 0.0).then_inc(sem("wpool_zero"), 1)
        pool.wait_ge(sem("edges_in"), 16)
        pool.wait_ge(sem("gaps"), 12)
        steps = 0
        n_pool = [0]

        def pstep(ins):
            n_pool[0] += 1
            ins.then_inc(sem("pool_step"), 1)
            pool.wait_ge(sem("pool_step"), n_pool[0])

        for j in range(2):
            pool.wait_ge(sem("z_evac"), NB * (5 + j))
            W0, W1 = (lambda a, b, p0=0, n=P: psum_w[p0:p0 + n, 0, a:b]), (lambda a, b, p0=0, n=P: psum_w[p0:p0 + n, 1, a:b])
            pstep(nc.gpsimd.tensor_tensor(W0(1, PL), pu[:, j, 0:PL - 1], pu[:, j, 1:PL], ALU.add))
            if j == 0:
                pstep(nc.gpsimd.tensor_tensor(W1(2, PL - 1, 64, 64), W0(1, PL - 2, 64, 64), W0(3, PL, 64, 64), ALU.add))
            else:
                pstep(nc.gpsimd.tensor_tensor(W1(2, PL - 1), W0(1, PL - 2), W0(3, PL), ALU.add))
                pstep(nc.gpsimd.tensor_tensor(W0(4, PL - 3), W1(2, PL - 5), W1(6, PL - 1), ALU.add))
                pstep(nc.gpsimd.tensor_tensor(W1(8, PL - 7, 64, 64), W0(4, PL - 11, 64, 64), W0(12, PL - 3, 64, 64), ALU.add))
            for h, W in ((0, W0), (1, W1)):
                p0 = 64 * h
                pstep(nc.gpsimd.tensor_scalar(W(PZ, PL - PZ, p0, 64), W(PZ, PL - PZ, p0, 64), edge[p0:p0 + 64, j:j + 1], None, ALU.mult))
                for start, length in ((PZ, LAT), (PZ + LAT + PZ, CTX)):
                    for side in range(2):
                        a = start if side == 0 else start + length - 8
                        e0 = 2 + 16 * j + 8 * side
                        pstep(nc.gpsimd.tensor_tensor(W(a, a + 8, p0, 64), W(a, a + 8, p0, 64), edge[p0:p0 + 64, e0:e0 + 8], ALU.mult))
                pstep(nc.gpsimd.tensor_tensor(pu[p0:p0 + 64, j, PZ:PL - PZ], W(PZ, PL - PZ, p0, 64), pu[p0:p0 + 64, j, PZ:PL - PZ], ALU.subtract))
            pool.sem_inc(sem("pooled"), 1)
        for j in range(2):
            pool.wait_ge(sem("z_evac"), NB * (9 + j))
            for a0, b0, n in ((PAD, 0, LAT), (PAD + LAT + PAD, LAT, CTX)):
                nc.gpsimd.tensor_tensor(vp[:, j, a0:a0 + n], vp[:, j, a0:a0 + n], sig[:, j, b0:b0 + n], ALU.mult).then_inc(sem("gated"), 1)
        pool.wait_ge(sem("posc2_in"), 16)
        for i in range(8):
            pool.wait_ge(sem(f"xr{i % 3}_in"), 16 * (i // 3 + 1))
            pool.wait_ge(sem(f"posr{i % 2}_in"), 64 + 16 * (i // 2 + 1))
            nc.gpsimd.tensor_tensor(xr[i % 3][:, 0:512], xr[i % 3][:, 0:512], posr2[i % 2][:, :], ALU.add).then_inc(sem("pos_half"), 1)
            nc.gpsimd.tensor_tensor(xr[i % 3][:, 512:1024], xr[i % 3][:, 512:1024], posc2[:, :], ALU.add).then_inc(sem("pos_half"), 1)
            pool.wait_ge(sem("pos_half"), 16 + 2 * (i + 1))
            pool.sem_inc(sem("pos_added"), 1)
        def piece_lo(n, c):
            pool.wait_ge(sem("piece_hi"), n + 1)
            hi, lo, src = piece(c)
            nc.gpsimd.tensor_tensor(lo, src, hi.bitcast(F32), ALU.subtract).then_inc(sem("piece_lo"), 1)

        def f_low(it, f):
            for n in range(NB):
                b = NB * f + n
                pool.wait_ge(sem("f_hi"), 2 * NB * it + b + 1)
                nc.gpsimd.tensor_tensor(f_lo[:, f, n * BW:(n + 1) * BW], fv[b % 2][:, :],
                                        f_hi[:, f, n * BW:(n + 1) * BW].bitcast(F32), ALU.subtract).then_inc(sem("f_lo"), 1)

        def lows(it, last):
            n0 = 4 + 6 * it
            piece_lo(n0, 4)
            piece_lo(n0 + 1, 5)
            for f in range(FB):
                f_low(it, f)
                if not last:
                    for e in range(2):
                        piece_lo(n0 + 2 + 2 * f + e, 6 + 2 * f + e)

        for n in range(4):
            piece_lo(n, n)
        lows(0, False)
        with pool.Fori(1, NFB - 1) as it:
            lows(it, False)
        lows(NFB - 1, True)
        for i in range(NT):
            if i == 0:
                pool.wait_ge(sem("final_g_in"), 16)
            pool.wait_ge(sem("end_normed"), i + 1)
            nc.gpsimd.tensor_tensor(xe[i % 3][:, :], xe[i % 3][:, :], fgb[:, :], ALU.mult).then_inc(sem("y_made"), 1)

    B = PS

    def three(out, hi_w, lo_w, hi_x, lo_x, start, stop):
        nc.tensor.matmul(out, hi_w, hi_x, start=start, stop=False)
        nc.tensor.matmul(out, hi_w, lo_x, start=False, stop=False)
        return nc.tensor.matmul(out, lo_w, hi_x, start=False, stop=stop)

    @block.tensor
    def _(pe):
        mm, tr = nc.tensor.matmul, nc.tensor.transpose
        pe.wait_ge(sem("ident"), 1)
        pe.wait_ge(sem("vectors_in"), 240)
        pe.wait_ge(sem("dt_rows"), 1)
        tr(B[6][:, 0:VR], rows[:, :], ident[0:VR, 0:VR])
        tr(B[6][:, X_TAP:X_TAP + 2 * TAPS], rtap[:, :], ident[0:2 * TAPS, 0:2 * TAPS])
        for i in range(5):
            tr(B[6][:, X_LRE + Q * i:X_LRE + Q * (i + 1)], rlam[:, i, :], ident[0:Q, 0:Q])
        tr(B[7][0:32, 0:NPAIR], dn[:, :], ident[0:NPAIR, 0:NPAIR]).then_inc(sem("params_turned"), 1)
        pe.wait_ge(sem("raws_in"), 96)
        for i in range(4):
            for h in range(HD):
                src = view(raw[i], h, [[HD, P]], 0, Q) if i < 2 else view(raw[i], h * P, [[1, P]], 0, Q)
                last = tr(B[i][:, h * Q:(h + 1) * Q], src, ident[0:Q, 0:Q])
            last.then_inc(sem("raws_turned"), 1)

        def ada(a, slots, bank, tbank):
            for k in range(KT):
                n = KT * a + k
                pe.wait_ge(sem(f"ada{k % 2}_in"), 16 * (n // 2 + 1))
                for q in range(4):
                    last = mm(bank[32 * q:32 * q + 32, :], condT[:, k, :], slots[k % 2][:, 512 * q:512 * q + 512], start=(k == 0), stop=False)
                last.then_inc(sem("ada_tile"), 1)
            pe.wait_ge(sem(f"ada_bias{a}_in"), 64 if a == 0 else 64)
            for q in range(4):
                last = mm(bank[32 * q:32 * q + 32, :], ident[32 * q:32 * q + 32, 32 * q:32 * q + 32], abias[a][32 * q:32 * q + 32, :], start=False, stop=True)
            last.then_inc(sem("ada_bank"), 1)
            pe.wait_ge(sem("ada_row"), a + 1)
            for b in range(4):
                last = tr(tbank[:, P * b:P * b + P], arow[a][:, P * b:P * b + P], ident[:, :])
            last.then_inc(sem("mod_turned"), 1)

        pe.wait_ge(sem("cond"), 2)
        ada(0, ad0, B[4], B[5])
        n = 0
        for grp in XG:
            for k in range(KT):
                if n == 0:
                    pe.wait_ge(sem("bb_made"), 2)
                    pe.wait_ge(sem("cc_evac"), 2)
                if k == 0:
                    pe.wait_ge(sem("x_normed"), grp[-1] + 1)
                if n >= 4:
                    pe.wait_ge(sem("h_evac"), n - 3)
                for t, i in enumerate(grp):
                    last = tr(B[n % 4][:, P * t:P * t + P], xt[i % 4][:, P * k:P * k + P], ident[:, :])
                last.then_inc(sem("xT_bank"), 1)
                n += 1

        def z_tile(i):
            pe.wait_ge(sem("w_in_lo"), i + 1)
            for b in range(NB):
                n = NB * i + b
                if n < 3:
                    pe.wait_ge(sem("mod_evac"), 1)
                    pe.wait_ge(sem("squares"), 2 * NT)
                    pe.wait_ge(sem("h_split"), 24)
                else:
                    pe.wait_ge(sem("z_evac"), n - 2)
                for k in range(KT):
                    last = three(B[ZB[b]][:, 0:BW], w_hi[i % 2][:, k, :], w_lo[i % 2][:, k, :],
                                 nt_hi[:, k, b * BW:(b + 1) * BW], nt_lo[:, k, b * BW:(b + 1) * BW], k == 0, k == KT - 1)
                last.then_inc(sem("z_done"), 1)

        def wb_turn(j):
            for d in range(2):
                pe.wait_ge(sem("wbt_made"), 2 * (2 * j + d + 1))
                for r in range(2):
                    c = 4 * j + 2 * d + r
                    pe.wait_ge(sem("h_evac"), 24) if c < 2 else pe.wait_ge(sem("wb_evac"), c - 1)
                    for i in range(4):
                        last = tr(B[c % 2][:, P * i:P * i + P], wbt[d][r][:, i, :], ident[:, :])
                    last.then_inc(sem("wb_turned"), 1)

        def state_inputs(j):
            pe.wait_ge(sem(f"u{j}_in"), 128)
            pe.wait_ge(sem("wb_evac"), 4 * j + 4)
            for d in range(2):
                for pp in range(4):
                    c = 8 * j + 4 * d + pp
                    if c >= 3:
                        pe.wait_ge(sem("v_evac"), c - 2)
                    q = NPAIR * d + 4 * j + pp
                    for par in range(2):
                        rhs = u8[j % 2][:, 2 * pp + par, :] if d == 0 else u8[j % 2][:, 2 * pp + par, ::-1]
                        for r in range(2):
                            last = mm(B[VB[c % 3]][64 * par:64 * par + 64, UC * r:UC * r + UC],
                                      wb[:, r, q, 64 * par:64 * par + 64], rhs, start=True, stop=True)
                    last.then_inc(sem("v_done"), 1)

        for i in range(10):
            z_tile(i)
            if i < 4:
                wb_turn(i)
            elif i == 4:
                state_inputs(2)
                state_inputs(3)
            if i == 3:
                state_inputs(0)
                state_inputs(1)
        pe.wait_ge(sem("wb_evac"), 16)
        ada(1, ad1, B[0], B[1])
        pe.wait_ge(sem("mod_evac"), 2)
        ada(2, ad1, B[0], B[1])
        pe.wait_ge(sem("bblk"), 2)
        pe.wait_ge(sem("dsel"), 1)
        pe.wait_ge(sem("wc_in"), 16)
        pe.wait_ge(sem("v_evac"), 32)
        for c in range(8):
            bank = B[(7, 2)[c % 2]]
            if c >= 2:
                pe.wait_ge(sem("kb_evac"), c - 1)
            for i in range(4):
                gp = 4 * (c % 4) + i
                o = P * i
                if c < 4:
                    for r in range(2):
                        mm(bank[0:32, o:o + P], bblk[:, r, gp, :], wc[:, r, gp, 0:P], start=(r == 0), stop=False)
                    for r in range(2):
                        mm(bank[0:32, o:o + HD], bblk[:, r, NPAIR + gp, :], wc[:, r, NPAIR + gp, P:P + HD], start=False, stop=False)
                    last = mm(bank[0:32, o:o + HD], ident[0:32, 0:32], dsel[:, gp, :], start=False, stop=True)
                else:
                    for r in range(2):
                        last = mm(bank[0:32, o:o + P], bblk[:, r, NPAIR + gp, :], wc[:, r, NPAIR + gp, HD:HD + P], start=(r == 0), stop=(r == 1))
            last.then_inc(sem("kb_done"), 1)
        pe.wait_ge(sem("wpool_in"), 64)
        pe.wait_ge(sem("mod_evac"), 3)
        for j in range(2):
            pe.wait_ge(sem("pooled"), j + 1)
            for b in range(NB):
                n = NB * j + b
                if n >= 2:
                    pe.wait_ge(sem("pool_evac"), n - 1)
                bank = B[n % 2]
                if b < 2:
                    last = mm(bank[:, 0:BW], wpool[:, j, :], pu[:, j, PZ + b * BW:PZ + (b + 1) * BW], start=True, stop=True)
                else:
                    mm(bank[:, 0:256], wpool[:, j, :], pu[:, j, PZ + 768:PZ + LAT], start=True, stop=True)
                    last = mm(bank[:, 256:BW], wpool[:, j, :], pu[:, j, PZ + LAT + PZ:PZ + LAT + PZ + CTX], start=True, stop=True)
                last.then_inc(sem("pool_done"), 1)
        pe.wait_ge(sem("scan_done"), 1)
        pe.wait_ge(sem("z_evac"), 30)
        for r in range(2):
            last = tr(B[6][0:Q, P * r:P * r + P], scT[:, 0, r, :], ident[:, :])
        last.then_inc(sem("fin_turned"), 1)
        pe.wait_ge(sem("toep_in"), 256)
        pe.wait_ge(sem("kb_evac"), 8)
        for c in range(8):
            j = c // 2
            if c % 2 == 0:
                pe.wait_ge(sem(f"u{j}_in"), 256)
            if c >= 2:
                pe.wait_ge(sem("y_evac"), 2 * (c - 1))
            for i in range(2):
                gp = 2 * c + i
                for par in range(2):
                    out = B[(2, 4)[c % 2] + par][:, UC * i:UC * i + UC]
                    p0 = 64 * par
                    mm(out, toep[:, 2 * gp + par, :], u9[j % 2][:, (2 * gp + par) % 8, :], start=True, stop=False)
                    for r in range(2):
                        base = (r * Q + gp) * SLOTS
                        mm(out, wc[p0:p0 + 64, r, gp, HD:HD + P], view(st, base, [[1, UC]], p0, 64), start=False, stop=False)
                    for r in range(2):
                        base = (r * Q + NPAIR + gp) * SLOTS
                        last = mm(out, wc[p0:p0 + 64, r, NPAIR + gp, 0:P], view(st, base + UC - 1, [[-1, UC]], p0, 64), start=False, stop=(r == 1))
            last.then_inc(sem("y_done"), 1)
        pe.wait_ge(sem("yT_in"), 64)
        pe.wait_ge(sem("wglu_in"), 16)
        pe.wait_ge(sem("pool_evac"), 6)
        pe.wait_ge(sem("fin_evac"), 2)
        for m in range(4):
            for b, (c0, n) in enumerate(GB):
                c = NB * m + b
                if c >= 3:
                    pe.wait_ge(sem("glu_gate"), c - 2)
                for k in range(4):
                    last = mm(B[(6, 7, 0)[b]][:, 0:n], wglu[:, k, P * m:P * m + P], yT[:, k, c0:c0 + n], start=(k == 0), stop=(k == 3))
                last.then_inc(sem("glu_done"), 1)
        pe.wait_ge(sem("y_evac"), 16)
        for src, ready, done in ((cacc, "conv_made", "mean_done"), (lnw, "dev_squared", "var_done")):
            for b in range(NB):
                pe.wait_ge(sem(ready), 2 if src is cacc else 2 * (b + 1))
                for j in range(2):
                    last = mm(B[1 + b][:, 0:389], onesm[:, :], src[:, j, 389 * b:389 * b + 389], start=(j == 0), stop=(j == 1))
                last.then_inc(sem(done), 1)
        def gate_rows(a, q0, banks, used):
            for who in range(2):
                for h in range(2):
                    q = q0 + h
                    last = mm(banks[2 * who + h][:, :], ident[32 * q:32 * q + 32, 32 * q + 16 * who:32 * q + 16 * who + 1].broadcast_to([32, P]),
                              arow[a][32 * q:32 * q + 32, :], start=True, stop=True)
            last.then_inc(sem(used), 1)

        pe.wait_ge(sem("glu_gate"), 12)
        gate_rows(1, 0, B[4:8], "g1_rows")
        def h2_turn(i):
            pe.wait_ge(sem("x2_normed"), i + 1)
            for h in range(2):
                c = 2 * i + h
                if c >= 4:
                    pe.wait_ge(sem("h2_evac"), i - 1)
                for k in range(4):
                    last = tr(B[c % 4][:, P * k:P * k + P], xn2[:, P * (4 * h + k):P * (4 * h + k + 1)], ident[:, :])
            last.then_inc(sem("h2_turned"), 1)

        pe.wait_ge(sem("wo0_in"), 16)
        pe.wait_ge(sem("wo1_in"), 16)
        pe.wait_ge(sem("glu_made"), 4)
        pe.wait_ge(sem("conv_out"), 4)
        pe.wait_ge(sem("g1_evac"), 4)
        for i in range(NT):
            for h in range(2):
                c = 2 * i + h
                if c >= 4:
                    pe.wait_ge(sem("x2_made"), c - 3)
                for k in range(KT):
                    src = yms if k < 4 else ymp
                    last = mm(B[4 + c % 4][:, :], src[:, k % 4, P * i:P * i + P], wo[k // 4][:, k % 4, 512 * h:512 * h + 512],
                              start=(k == 0), stop=(k == KT - 1))
                last.then_inc(sem("o_done"), 1)
            if i >= 2:
                h2_turn(i - 2)
        h2_turn(NT - 2)
        h2_turn(NT - 1)
        def up(it, f, first):
            pe.wait_ge(sem("piece_lo"), 6 * it + 2 * (f + 1))
            for n in range(NB):
                b = NB * f + n
                if not first or b >= 2:
                    pe.wait_ge(sem("silu_made"), 2 * NB * it + b - 1)
                    pe.wait_ge(sem("f_made"), 2 * NB * it + b - 1)
                for e in range(2):
                    for k in range(KT):
                        last = three(B[2 * e + b % 2][:, 0:BW], f13h[f][:, e, k, :], f13l[f][:, e, k, :],
                                     nt_hi[:, k, n * BW:(n + 1) * BW], nt_lo[:, k, n * BW:(n + 1) * BW], k == 0, k == KT - 1)
                    last.then_inc(sem("gate_done" if e == 0 else "up_done"), 1)

        def down(it, first):
            pe.wait_ge(sem("piece_lo"), 6 * it + 6)
            for i in range(NT):
                if i % 3 == 0:
                    pe.wait_ge(sem("f_lo"), 2 * NB * it + NB + i // 3 + 1)
                for h in range(2):
                    c = 2 * i + h
                    if not first or c >= 4:
                        pe.wait_ge(sem("acc_done"), 2 * NT * it + c - 3)
                    for f in range(FB):
                        last = three(B[4 + c % 4][:, :], f_hi[:, f, P * i:P * i + P], f_lo[:, f, P * i:P * i + P],
                                     f2h[:, f, 512 * h:512 * h + 512], f2l[:, f, 512 * h:512 * h + 512], f == 0, f == FB - 1)
                    last.then_inc(sem("down_done"), 1)

        pe.wait_ge(sem("h2_split"), NT)
        for f in range(FB):
            up(0, f, True)
        down(0, True)
        with pe.Fori(1, NFB - 1) as it:
            for f in range(FB):
                up(it, f, False)
            down(it, False)
        for f in range(FB):
            up(NFB - 1, f, False)
        down(NFB - 1, False)
        pe.wait_ge(sem("f_made"), 2 * NB * NFB)
        gate_rows(2, 2, B[0:4], "g2_rows")

    @block.scalar
    def _(act):
        A_ = nc.scalar.activation

        act.wait_ge(sem("pv_evac"), 2)
        for who, v in enumerate((V_CX, V_CC)):
            A_(condT[:, :, 16 * who:16 * who + 16], view(pv, v, [[1, KT], [0, 16]]), ACT.Silu).then_inc(sem("cond"), 1)
        A_(prm[:, 0, :], pv[:, X_DT:X_DT + Q], ACT.Exp).then_inc(sem("dt"), 1)
        act.wait_ge(sem("lam_dt"), 2)
        A_(prm[:, 3, :], prm[:, 1, :], ACT.Exp).then_inc(sem("polar"), 1)
        act.wait_ge(sem("angles"), 2)
        A_(prm[:, 8, :], prm[:, 5, :], ACT.Sin).then_inc(sem("polar"), 1)
        A_(prm[:, 9, :], prm[:, 7, :], ACT.Sin).then_inc(sem("polar"), 1)
        act.wait_ge(sem("raws_turned"), 3)
        A_(view(cc, 0, [[1, HD], [HD, Q]]), B[2][:, :], ACT.Copy).then_inc(sem("cc_evac"), 1)
        act.wait_ge(sem("raws_turned"), 4)
        A_(view(cc, Q * HD, [[1, HD], [HD, Q]]), B[3][:, :], ACT.Copy, scale=-1.0).then_inc(sem("cc_evac"), 1)

        def mod_out(a, bank, tbank):
            act.wait_ge(sem("ada_bank"), a + 1)
            A_(arow[a][:, :], bank[:, :], ACT.Copy).then_inc(sem("ada_row"), 1)
            act.wait_ge(sem("mod_turned"), a + 1)
            A_(view(modc, 32 * a, [[2, 4], [8, 4], [1, 2]]), view(tbank, 0, [[P, 4], [32, 4], [16, 2]]), ACT.Copy).then_inc(sem("mod_evac"), 1)

        nsq = 0
        n = 0
        for g, grp in enumerate(XG):
            if g == 1:
                act.wait_ge(sem("xT_bank"), 8)
            for i in grp:
                if i < 8:
                    act.wait_ge(sem("pos_added"), i + 1)
                else:
                    act.wait_ge(sem("x0_in"), 48)
                for h in range(2):
                    if nsq >= 2:
                        act.wait_ge(sem("squares"), nsq - 1)
                    A_(B[6 + h][:, :], xt[i % 4][:, 512 * h:512 * h + 512], ACT.Square, accum_out=ss[:, 2 * i + h:2 * i + h + 1]).then_inc(sem("squares"), 1)
                    nsq += 1
            i0, i1 = grp[0], grp[-1] + 1
            act.wait_ge(sem("inverse_ms"), g + 1)
            A_(rstd[:, i0:i1], var[:, i0:i1], ACT.Sqrt).then_inc(sem("rstd"), 1)
            act.wait_ge(sem("rstd"), g + 1)
            for i in grp:
                A_(xt[i % 4][:, :], xt[i % 4][:, :], ACT.Copy, scale=rstd[:, i:i + 1]).then_inc(sem("x_normed"), 1)
            if g == 0:
                mod_out(0, B[4], B[5])
                act.wait_ge(sem("gsc1"), 1)
                act.wait_ge(sem("mod_evac"), 1)
            for k in range(KT):
                act.wait_ge(sem("xT_bank"), n + 1)
                if n >= 2:
                    act.wait_ge(sem("h_split"), n - 1)
                w = P * len(grp)
                who = 0 if g == 2 else 1
                A_(hf[n % 2][:, 0:w], B[n % 4][:, 0:w], ACT.Identity, scale=gsc[:, 0, k, who:who + 1],
                   bias=modc[:, k, who:who + 1]).then_inc(sem("h_evac"), 1)
                n += 1

        def w_high(i):
            act.wait_ge(sem(f"w_in{i % 2}_in"), 16 * (i // 2 + 1))
            if i < 2:
                act.wait_ge(sem("ada_tile"), 8)
            else:
                act.wait_ge(sem("z_done"), NB * (i - 1))
            nc.scalar.copy(w_hi[i % 2][:, :, :], wst[i % 2][:, :, :]).then_inc(sem("w_in_hi"), 1)

        def z_out(i):
            for b in range(NB):
                src = B[ZB[b]]
                act.wait_ge(sem("z_done"), NB * i + b + 1)
                if i < 4 and b == 0 and i >= 2:
                    act.wait_ge(sem("z_out"), 16 * (i - 1))
                if i == 4 and b == 0:
                    act.wait_ge(sem("v_done"), 32)
                if i < 4:
                    parts = ((48 * b, 0, 48),) if b < 2 else ((96, 0, 32), (LC + 1, 256, 16))
                    for c0, o, m in parts:
                        last = A_(view(zp[i % 2], c0, [[1, m], [UC, CH]]), src[:, o:o + CH * m], ACT.Copy)
                else:
                    dst, pad = ((pu, PZ), (vp, PAD), (sig, 0))[(i - 4) // 2]
                    fn = ACT.Sigmoid if dst is sig else ACT.Copy
                    parts = ((BW * b, 0, BW),) if b < 2 else ((768, 0, 256), (LAT + pad, 256, CTX))
                    for c0, o, m in parts:
                        last = A_(dst[:, i % 2, pad + c0:pad + c0 + m], src[:, o:o + m], fn)
                last.then_inc(sem("z_evac"), 1)

        def wb_out(j):
            for d in range(2):
                for r in range(2):
                    c = 4 * j + 2 * d + r
                    if c == 0:
                        act.wait_ge(sem("raws_turned"), 4)
                    act.wait_ge(sem("wb_turned"), c + 1)
                    q0 = NPAIR * d + 4 * j
                    A_(wb[:, r, q0:q0 + 4, :], B[c % 2][:, :].rearrange("p (q n) -> p q n", n=P), ACT.Copy).then_inc(sem("wb_evac"), 1)

        def v_out(j):
            for d in range(2):
                for pp in range(4):
                    c = 8 * j + 4 * d + pp
                    q = NPAIR * d + 4 * j + pp
                    act.wait_ge(sem("v_done"), c + 1)
                    if c == 0:
                        for s in range(2):
                            act.wait_ge(sem(f"wc_out{s}"), 128)
                    A_(view(st, q * SLOTS + 1, [[Q * SLOTS, 2], [1, UC]]), view(B[VB[c % 3]], 0, [[UC, 2], [1, UC]]), ACT.Copy).then_inc(sem("v_evac"), 1)

        w_high(0)
        w_high(1)
        for i in range(10):
            if i == 4:
                v_out(2)
                v_out(3)
                act.wait_ge(sem("gaps"), 12)
            z_out(i)
            if i < 4:
                wb_out(i)
            if i == 3:
                v_out(0)
                v_out(1)
            if i + 2 < 10:
                w_high(i + 2)
        mod_out(1, B[0], B[1])
        act.wait_ge(sem("a8_made"), 2)
        act.wait_ge(sem("wc_made"), 16)
        mod_out(2, B[0], B[1])
        for c in range(8):
            act.wait_ge(sem("kb_done"), c + 1)
            bank = B[(7, 2)[c % 2]]
            n, o = (P, 7 * HD) if c < 4 else (7 * HD, 0)
            A_(view(kb, 4 * (c % 4) * 15 * HD + o, [[15 * HD, 4], [1, n]], 0, 32), view(bank, 0, [[P, 4], [1, n]], 0, 32), ACT.Copy).then_inc(sem("kb_evac"), 1)
        for j in range(2):
            for b in range(NB):
                n = NB * j + b
                act.wait_ge(sem("pool_done"), n + 1)
                A_(ymp[:, j, b * BW:(b + 1) * BW], B[n % 2][:, 0:BW], ACT.Copy, scale=pv[:, V_PS + j:V_PS + j + 1]).then_inc(sem("pool_evac"), 1)
        act.wait_ge(sem("fin_turned"), 1)
        for r in range(2):
            A_(fin[:, r, :], B[6][0:Q, P * r:P * r + P], ACT.Copy).then_inc(sem("fin_evac"), 1)
        for c in range(8):
            j = c // 2
            act.wait_ge(sem("y_done"), c + 1)
            if c % 2 == 0 and j >= 2:
                act.wait_ge(sem("y_out"), 128 * (j - 1))
            for par in range(2):
                A_(view(yb[j % 2], (4 * (c % 2) + par) * UC, [[2 * UC, 2], [1, UC]]),
                   view(B[(2, 4)[c % 2] + par], 0, [[UC, 2], [1, UC]]), ACT.Gelu_apprx_tanh).then_inc(sem("y_evac"), 1)
        for m in range(4):
            for b, (c0, n) in enumerate(GB):
                act.wait_ge(sem("glu_done"), NB * m + b + 1)
                if b == 0 and m >= 1:
                    act.wait_ge(sem("glu_made"), m)
                A_(gsig[:, c0:c0 + n], B[(6, 7, 0)[b]][:, 0:n], ACT.Sigmoid, bias=pv[:, V_GB + m:V_GB + m + 1]).then_inc(sem("glu_gate"), 1)
        for b in range(NB):
            for j in range(2):
                act.wait_ge(sem("deviation"), 2 * b + j + 1)
                A_(lnw[:, j, 389 * b:389 * b + 389], cacc[:, j, 389 * b:389 * b + 389], ACT.Square).then_inc(sem("dev_squared"), 1)
        act.wait_ge(sem("inverse_var"), NB)
        A_(sig[:, 0, 0:1152], sig[:, 1, 0:1152], ACT.Sqrt) if False else None
        A_(view(sig, 0, [[1, VO]]), view(sig, 0, [[1, VO]]), ACT.Sqrt).then_inc(sem("ln_rstd"), 1)
        for j in range(2):
            act.wait_ge(sem("ln_scaled"), j + 1)
            for c0, o, m in ((0, 0, LAT), (VCTX, LAT, CTX)):
                A_(ymp[:, 2 + j, o:o + m], cacc[:, j, c0:c0 + m], ACT.Silu, scale=pv[:, V_LG + j:V_LG + j + 1],
                   bias=pv[:, V_LB + j:V_LB + j + 1]).then_inc(sem("conv_out"), 1)
        act.wait_ge(sem("g1_rows"), 1)
        act.wait_ge(sem("conv_out"), 4)
        for who in range(2):
            for h in range(2):
                A_(g1b[:, who, 512 * h:512 * h + 512], B[4 + 2 * who + h][:, :], ACT.Copy).then_inc(sem("g1_evac"), 1)
        for i in range(NT):
            who = 0 if i == 8 else 1
            if i >= 1:
                act.wait_ge(sem("h2_turned"), i)
            act.wait_ge(sem("x2_made"), 2 * i + 2)
            for h in range(2):
                A_(xn2[:, 512 * h:512 * h + 512], xr[i % 3][:, 512 * h:512 * h + 512], ACT.Square, accum_out=ss2[:, 2 * i + h:2 * i + h + 1]).then_inc(sem("squares"), 1)
            act.wait_ge(sem("inverse_ms"), 3 + i + 1)
            A_(rstd2[:, i:i + 1], var2[:, i:i + 1], ACT.Sqrt).then_inc(sem("rstd"), 1)
            act.wait_ge(sem("rstd"), 3 + i + 1)
            A_(xn2[:, :], xr[i % 3][:, :], ACT.Copy, scale=rstd2[:, i:i + 1]).then_inc(sem("x2_normed"), 1)
            act.wait_ge(sem("h2_turned"), i + 1)
            if i >= 1:
                act.wait_ge(sem("h2_split"), i)
            for k in range(KT):
                last = A_(h2f[:, k, :], B[(2 * i + k // 4) % 4][:, P * (k % 4):P * (k % 4) + P], ACT.Identity,
                          scale=gsc[:, 1, k, who:who + 1], bias=modc[:, 24 + k, who:who + 1])
            last.then_inc(sem("h2_evac"), 1)

        def piece_hi(n, c, after=None):
            s = n // 3 if False else None
            act.wait_ge(sem(f"piece{c % 3}_in"), piece_count(n, c))
            if after is not None:
                act.wait_ge(*after)
            hi, _, src = piece(c)
            nc.scalar.copy(hi, src).then_inc(sem("piece_hi"), 1)

        def hidden(it, f, first):
            for n in range(NB):
                b = NB * f + n
                g = 2 * NB * it + b
                act.wait_ge(sem("gate_done"), g + 1)
                if not first or b >= 2:
                    act.wait_ge(sem("f_made"), g - 1)
                A_(sa[b % 2][:, :], B[b % 2][:, 0:BW], ACT.Silu).then_inc(sem("silu_made"), 1)
                act.wait_ge(sem("f_made"), g + 1)
                if not first:
                    act.wait_ge(sem("down_done"), 2 * NT * (it - 1) + 6 * (n + 1))
                nc.scalar.copy(f_hi[:, f, n * BW:(n + 1) * BW], fv[b % 2][:, :]).then_inc(sem("f_hi"), 1)

        def iteration(it, first, last):
            n0 = 4 + 6 * it
            for f in range(FB):
                piece_hi(n0 + f, 4 + f, None if first else (sem("down_done"), 2 * NT * it))
            for f in range(FB):
                hidden(it, f, first)
                if not last:
                    for e in range(2):
                        piece_hi(n0 + 2 + 2 * f + e, 6 + 2 * f + e, (sem("up_done"), 2 * NB * it + NB * (f + 1)))

        for n in range(4):
            piece_hi(n, n)
        iteration(0, True, False)
        with act.Fori(1, NFB - 1) as it:
            iteration(it, False, False)
        iteration(NFB - 1, False, True)
        act.wait_ge(sem("g2_rows"), 1)
        for who in range(2):
            for h in range(2):
                A_(g2b[:, who, 512 * h:512 * h + 512], B[2 * who + h][:, :], ACT.Copy).then_inc(sem("g2_evac"), 1)
        for i in range(NT):
            act.wait_ge(sem("end_sum"), i + 1)
            for h in range(2):
                A_(te[i % 2][:, 512 * h:512 * h + 512], xe[i % 3][:, 512 * h:512 * h + 512], ACT.Square, accum_out=ss[:, 2 * i + h:2 * i + h + 1]).then_inc(sem("squares"), 1)
            act.wait_ge(sem("inverse_ms"), 3 + NT + i + 1)
            A_(rstd[:, i:i + 1], var[:, i:i + 1], ACT.Sqrt).then_inc(sem("rstd"), 1)
            act.wait_ge(sem("rstd"), 3 + NT + i + 1)
            A_(xe[i % 3][:, :], xe[i % 3][:, :], ACT.Copy, scale=rstd[:, i:i + 1]).then_inc(sem("end_normed"), 1)

    @block.vector
    def _(dve):
        TT, TS, STT = nc.vector.tensor_tensor, nc.vector.tensor_scalar, nc.vector.scalar_tensor_tensor
        steps = [0]

        def step(ins):
            steps[0] += 1
            ins.then_inc(sem("dve_step"), 1)
            dve.wait_ge(sem("dve_step"), steps[0])

        dve.wait_ge(sem("log_dt_in"), 16)
        nc.vector.tensor_copy(view(rlam, 4 * P, [[NS, 2], [1, NS]], 0, Q), view(ldt, 0, [[1, 2], [0, NS]], 0, Q)).then_inc(sem("dt_rows"), 1)
        dve.wait_ge(sem("params_turned"), 1)
        nc.vector.tensor_copy(pv[:, :], B[6][:, 0:NPV]).then_inc(sem("pv_evac"), 1)
        nc.vector.tensor_copy(dcol[:, :], B[7][0:32, 0:NPAIR]).then_inc(sem("pv_evac"), 1)
        dve.wait_ge(sem("pv_evac"), 2)
        lre, lim = pv[:, X_LRE:X_LRE + Q], pv[:, X_LIM:X_LIM + Q]
        p_ = lambda i: prm[:, i, :]
        dve.wait_ge(sem("dt"), 1)
        TT(p_(1), lre, p_(0), ALU.mult).then_inc(sem("lam_dt"), 1)
        TT(p_(2), lim, p_(0), ALU.mult).then_inc(sem("lam_dt"), 1)
        dve.wait_ge(sem("lam_dt"), 2)
        for a, b, turn in ((4, 5, 0.0), (6, 7, 0.25)):
            step(TS(p_(a), p_(2), 1.0 / TWO_PI, turn, ALU.mult, ALU.add))
            step(TS(p_(a), p_(a), ROUND, None, ALU.add))
            step(TS(p_(a), p_(a), ROUND, None, ALU.subtract))
            step(STT(p_(b), p_(a), -TP1, p_(2), ALU.mult, ALU.add))
            step(STT(p_(b), p_(a), -TP2, p_(b), ALU.mult, ALU.add))
            step(STT(p_(b), p_(a), -TP3, p_(b), ALU.mult, ALU.add))
            if turn:
                step(TS(p_(b), p_(b), TWO_PI / 4, None, ALU.add))
            TS(p_(b), p_(b), 3.1415925, -3.1415925, ALU.min, ALU.max).then_inc(sem("angles"), 1)
        nc.vector.memset(powr[:, 0, :], 1.0).then_inc(sem("unit"), 1)
        nc.vector.memset(powi[:, 0, :], 0.0).then_inc(sem("unit"), 1)
        dve.wait_ge(sem("polar"), 3)
        TT(powr[:, 1, :], p_(3), p_(9), ALU.mult)
        step(TT(powi[:, 1, :], p_(3), p_(8), ALU.mult))
        step(TT(p_(10), lre, lre, ALU.mult))
        step(TT(p_(11), lim, lim, ALU.mult))
        step(TT(p_(10), p_(10), p_(11), ALU.add))
        step(nc.vector.reciprocal(p_(10), p_(10)))
        step(TS(p_(11), powr[:, 1, :], -1.0, None, ALU.add))
        step(TT(p_(12), p_(11), lre, ALU.mult))
        step(TT(p_(14), powi[:, 1, :], lim, ALU.mult))
        step(TT(p_(12), p_(12), p_(14), ALU.add))
        step(TT(p_(12), p_(12), p_(10), ALU.mult))
        step(TT(p_(13), powi[:, 1, :], lre, ALU.mult))
        step(TT(p_(14), p_(11), lim, ALU.mult))
        step(TT(p_(13), p_(13), p_(14), ALU.subtract))
        step(TT(p_(13), p_(13), p_(10), ALU.mult))
        for lo, n in ((1, 1), (2, 2), (4, 4)):
            br, bi = view(powr, lo * Q, [[0, n], [1, Q]]), view(powi, lo * Q, [[0, n], [1, Q]])
            sr, si = powr[:, 1:1 + n, :], powi[:, 1:1 + n, :]
            t0, t1 = wbt_tmp[0][:, 0:n, 0:Q], wbt_tmp[1][:, 0:n, 0:Q]
            dr, di = powr[:, lo + 1:lo + 1 + n, :], powi[:, lo + 1:lo + 1 + n, :]
            step(TT(t0, br, sr, ALU.mult))
            step(TT(t1, bi, si, ALU.mult))
            step(TT(dr, t0, t1, ALU.subtract))
            step(TT(t0, br, si, ALU.mult))
            step(TT(t1, bi, sr, ALU.mult))
            step(TT(di, t0, t1, ALU.add))
        dve.wait_ge(sem("unit"), 2)
        dve.sem_inc(sem("powers"), 1)
        dve.wait_ge(sem("raws_turned"), 2)
        qre, qim = view(prm, 12 * Q, [[0, HD], [1, Q]]), view(prm, 13 * Q, [[0, HD], [1, Q]])
        bank = lambda b: B[b][:, :].rearrange("p (h q) -> p h q", q=Q)
        bout = lambda r: view(bb, r * Q * HD, [[1, HD], [HD, Q]])
        tv = [view(wbt_tmp[i], 0, [[1, HD], [HD, Q]]) for i in range(2)]
        step(TT(bout(0), bank(0), qre, ALU.mult))
        step(TT(tv[0], bank(1), qim, ALU.mult))
        step(TT(bout(1), bank(1), qre, ALU.mult))
        step(TT(tv[1], bank(0), qim, ALU.mult))
        TT(bout(0), bout(0), tv[0], ALU.subtract).then_inc(sem("bb_made"), 1)
        TT(bout(1), bout(1), tv[1], ALU.add).then_inc(sem("bb_made"), 1)
        dve.wait_ge(sem("ident"), 1)
        step(TT(dsel[:, 0, :], ident[0:32, 0:16], ident[0:32, 16:32], ALU.add))
        step(nc.vector.tensor_copy(view(dsel, HD, [[HD, NPAIR - 1], [1, HD]], 0, 32), view(dsel, 0, [[0, NPAIR - 1], [1, HD]], 0, 32)))
        TT(dsel[:, :, :], dsel[:, :, :], view(dcol, 0, [[1, NPAIR], [0, HD]], 0, 32), ALU.mult).then_inc(sem("dsel"), 1)

        def inverse_ms(s, v, i0, i1, name, ready, count):
            dve.wait_ge(sem(ready), count)
            n = i1 - i0
            step(TT(v[:, i0:i1], view(s, 2 * i0, [[2, n]]), view(s, 2 * i0 + 1, [[2, n]]), ALU.add))
            step(TS(v[:, i0:i1], v[:, i0:i1], 1.0 / D, EPS, ALU.mult, ALU.add))
            nc.vector.reciprocal(v[:, i0:i1], v[:, i0:i1]).then_inc(sem(name), 1)

        n = 0
        for g, grp in enumerate(XG):
            inverse_ms(ss, var, grp[0], grp[-1] + 1, "inverse_ms", "squares", 2 * (grp[-1] + 1))
            if g == 0:
                dve.wait_ge(sem("mod_evac"), 1)
                STT(gsc[:, 0, :, :], modc[:, 8:16, :], 1.0, view(pv, V_N1, [[1, KT], [0, 2]]), ALU.add, ALU.mult).then_inc(sem("gsc1"), 1)
            for k in range(KT):
                w = P * len(grp)
                c0 = P * grp[0]
                dve.wait_ge(sem("h_evac"), n + 1)
                hi, lo = nt_hi[:, k, c0:c0 + w], nt_lo[:, k, c0:c0 + w]
                nc.vector.tensor_copy(hi, hf[n % 2][:, 0:w]).then_inc(sem("h_hi"), 1)
                dve.wait_ge(sem("h_hi"), n + 1)
                TT(lo, hf[n % 2][:, 0:w], hi.bitcast(F32), ALU.subtract).then_inc(sem("h_split"), 1)
                n += 1

        def w_low(i):
            dve.wait_ge(sem("w_in_hi"), i + 1)
            TT(w_lo[i % 2][:, :, :], wst[i % 2][:, :, :], w_hi[i % 2][:, :, :].bitcast(F32), ALU.subtract).then_inc(sem("w_in_lo"), 1)

        def wbt_piece(j, d):
            n = 2 * j + d
            q0 = NPAIR * d + 4 * j
            step_, base = (-Q, (CH - 1) * Q) if d == 0 else (Q, 0)
            lr = view(powr, base + q0, [[1, 4], [step_, CH], [0, HD]])
            li = view(powi, base + q0, [[1, 4], [step_, CH], [0, HD]])
            br = view(bb, q0 * HD, [[HD, 4], [0, CH], [1, HD]])
            bi = view(bb, (Q + q0) * HD, [[HD, 4], [0, CH], [1, HD]])
            v3 = lambda t: view(t, 0, [[P, 4], [HD, CH], [1, HD]])
            out, tmp = wbt[d], wbt_tmp
            if n == 0:
                dve.wait_ge(sem("bb_made"), 2)
            if j >= 1:
                dve.wait_ge(sem("wb_turned"), 4 * (j - 1) + 2 * d + 2)
            if n >= 1:
                dve.wait_ge(sem("wbt_made"), 2 * n)
            TT(v3(out[0]), lr, br, ALU.mult).then_inc(sem("wbt_terms"), 1)
            TT(v3(tmp[0]), li, bi, ALU.mult).then_inc(sem("wbt_terms"), 1)
            TT(v3(out[1]), lr, bi, ALU.mult).then_inc(sem("wbt_terms"), 1)
            TT(v3(tmp[1]), li, br, ALU.mult).then_inc(sem("wbt_terms"), 1)
            dve.wait_ge(sem("wbt_terms"), 4 * n + 2)
            TT(out[0][:, :, :], out[0][:, :, :], tmp[0][:, :, :], ALU.subtract).then_inc(sem("wbt_made"), 1)
            dve.wait_ge(sem("wbt_terms"), 4 * n + 4)
            TT(out[1][:, :, :], out[1][:, :, :], tmp[1][:, :, :], ALU.add).then_inc(sem("wbt_made"), 1)

        w_low(0)
        w_low(1)
        for j in range(4):
            wbt_piece(j, 0)
            wbt_piece(j, 1)
            w_low(j + 2)
        dve.wait_ge(sem("wbt_made"), 16)
        nc.vector.tensor_copy(a8r[:, :], powr[:, CH, :]).then_inc(sem("a8_copied"), 1)
        TS(a8i[:, 0, :], powi[:, CH, :], -1.0, None, ALU.mult).then_inc(sem("a8_copied"), 1)
        nc.vector.tensor_copy(a8i[:, 1, :], powi[:, CH, :]).then_inc(sem("a8_copied"), 1)
        dve.wait_ge(sem("a8_copied"), 3)
        dve.sem_inc(sem("a8_made"), 2)
        for i in range(6, 10):
            w_low(i)
        dve.wait_ge(sem("v_evac"), 32)
        for r, x in enumerate((X_HRE, X_HIM)):
            nc.vector.tensor_copy(view(st, r * Q * SLOTS, [[SLOTS, NPAIR]]), pv[:, x:x + NPAIR]).then_inc(sem("h0"), 1)
            nc.vector.tensor_copy(view(st, (r * Q + NPAIR) * SLOTS + BSH, [[SLOTS, NPAIR]]), pv[:, x + NPAIR:x + Q]).then_inc(sem("h0"), 1)
            nc.vector.memset(view(st, (r * Q + NPAIR) * SLOTS, [[SLOTS, NPAIR]]), 0.0).then_inc(sem("h0"), 1)
        dve.wait_ge(sem("h0"), 6)
        DL = NPAIR * SLOTS + BSH
        DC = NPAIR * SLOTS - (LC + 1)
        count = [0]

        def state(base, dstep, k, flip=False):
            rs = -Q * SLOTS if flip else Q * SLOTS
            return view(st, base + k + (Q * SLOTS if flip else 0), [[rs, 2], [dstep, 2], [SLOTS, NPAIR]])

        ar = view(a8r, 0, [[0, 2], [NPAIR, 2], [1, NPAIR]])
        ai = view(a8i, 0, [[Q, 2], [NPAIR, 2], [1, NPAIR]])
        tt = lambda t, i: view(t, i * 2 * Q, [[Q, 2], [NPAIR, 2], [1, NPAIR]])

        def scan_step(chains):
            for name, t, base, dstep, k in chains:
                TT(tt(t, 0), ar, state(base, dstep, k), ALU.mult).then_inc(sem(name), 1)
                TT(tt(t, 1), ai, state(base, dstep, k, True), ALU.mult).then_inc(sem(name), 1)
            for name, t, base, dstep, k in chains:
                dve.wait_ge(sem(name), 4 * k + 1)
                TT(tt(t, 2), tt(t, 0), state(base, dstep, k + 1), ALU.add).then_inc(sem(name), 1)
            for name, t, base, dstep, k in chains:
                dve.wait_ge(sem(name), 4 * k + 3)
                TT(state(base, dstep, k + 1), tt(t, 2), tt(t, 1), ALU.add).then_inc(sem(name), 1)
            for name, t, base, dstep, k in chains:
                dve.wait_ge(sem(name), 4 * k + 4)

        for k in range(LC):
            chains = [("latent_step", scT, 0, DL, k)]
            if k < CC:
                chains.append(("context_step", scC, LC + 1, DC, k))
            scan_step(chains)
        nc.vector.tensor_copy(tt(scT, 0), state(UC, NPAIR * SLOTS - LC - 1, 0)).then_inc(sem("scan_done"), 1)
        dve.wait_ge(sem("mod_evac"), 3)
        STT(gsc[:, 1, :, :], modc[:, 32:40, :], 1.0, view(pv, V_N2, [[1, KT], [0, 2]]), ALU.add, ALU.mult).then_inc(sem("gsc2"), 1)
        dve.wait_ge(sem("gated"), 4)
        for tap in range(TAPS):
            for j in range(2):
                w = pv[:, X_TAP + 2 * tap + j:X_TAP + 2 * tap + j + 1]
                src = vp[:, j, tap:tap + VO]
                if tap == 0:
                    TS(cacc[:, j, :], src, w, pv[:, V_CB + j:V_CB + j + 1], ALU.mult, ALU.add).then_inc(sem("tap_done"), 1)
                else:
                    dve.wait_ge(sem("tap_done"), 2 * tap + j - 1)
                    STT(cacc[:, j, :], src, w, cacc[:, j, :], ALU.mult, ALU.add).then_inc(sem("tap_done" if tap < TAPS - 1 else "conv_made"), 1)
        for m in range(4):
            dve.wait_ge(sem("glu_gate"), NB * (m + 1))
            for c0, o, n in ((0, 0, LC), (LC + 1, LAT, CC)):
                last = TT(view(yms, m * T + o, [[1, CH], [CH, n]]), view(yT, m * CH * UC + c0, [[UC, CH], [1, n]]),
                          view(gsig, c0, [[UC, CH], [1, n]]), ALU.mult)
            last.then_inc(sem("glu_made"), 1)
        for b in range(NB):
            dve.wait_ge(sem("mean_done"), b + 1)
            dve.wait_ge(sem("conv_made"), 2)
            for j in range(2):
                TT(cacc[:, j, 389 * b:389 * b + 389], cacc[:, j, 389 * b:389 * b + 389], B[1 + b][:, 0:389], ALU.subtract).then_inc(sem("deviation"), 1)
        for b in range(NB):
            dve.wait_ge(sem("var_done"), b + 1)
            step(TS(view(sig, 389 * b, [[1, 389]]), B[1 + b][:, 0:389], EPS, None, ALU.add))
            nc.vector.reciprocal(view(sig, 389 * b, [[1, 389]]), view(sig, 389 * b, [[1, 389]])).then_inc(sem("inverse_var"), 1)
        dve.wait_ge(sem("ln_rstd"), 1)
        dve.wait_ge(sem("deviation"), 6)
        for j in range(2):
            TT(cacc[:, j, :], cacc[:, j, :], view(sig, 0, [[1, VO]]), ALU.mult).then_inc(sem("ln_scaled"), 1)
        dve.wait_ge(sem("g1_evac"), 4)
        dve.wait_ge(sem("ln_scaled"), 2)

        def h2_split(i):
            dve.wait_ge(sem("h2_evac"), i + 1)
            hi, lo = nt_hi[:, :, P * i:P * i + P], nt_lo[:, :, P * i:P * i + P]
            nc.vector.tensor_copy(hi, h2f[:, :, :]).then_inc(sem("h2_hi"), 1)
            dve.wait_ge(sem("h2_hi"), i + 1)
            TT(lo, h2f[:, :, :], hi.bitcast(F32), ALU.subtract).then_inc(sem("h2_split"), 1)

        for i in range(NT):
            who = 0 if i == 8 else 1
            if i < 8:
                dve.wait_ge(sem("pos_added"), 8 + i + 1)
            else:
                dve.wait_ge(sem("xr2_in"), 48)
            for h in range(2):
                c = 2 * i + h
                dve.wait_ge(sem("o_done"), c + 1)
                if c >= 1:
                    dve.wait_ge(sem("x2_made"), c)
                step(TT(tg[:, :], B[4 + c % 4][:, :], g1b[:, who, 512 * h:512 * h + 512], ALU.mult))
                TT(xr[i % 3][:, 512 * h:512 * h + 512], xr[i % 3][:, 512 * h:512 * h + 512], tg[:, :], ALU.add).then_inc(sem("x2_made"), 1)
            dve.wait_ge(sem("x2_made"), 2 * i + 2)
            inverse_ms(ss2, var2, i, i + 1, "inverse_ms", "squares", 2 * NT + 2 * i + 2)
            if i >= 1:
                h2_split(i - 1)
        h2_split(NT - 1)
        dve.sem_inc(sem("g1_used"), 2 * NT)

        def hidden(it, first):
            for f in range(FB):
                for n in range(NB):
                    b = NB * f + n
                    g = 2 * NB * it + b
                    dve.wait_ge(sem("silu_made"), g + 1)
                    dve.wait_ge(sem("up_done"), g + 1)
                    if not first or b >= 2:
                        dve.wait_ge(sem("f_lo"), g - 1)
                    TT(fv[b % 2][:, :], sa[b % 2][:, :], B[2 + b % 2][:, 0:BW], ALU.mult).then_inc(sem("f_made"), 1)

        def gather(it, first):
            if not first:
                dve.wait_ge(sem("acc_done"), 2 * NT * it)
            for c in range(2 * NT):
                a = acc[:, c // 2, 512 * (c % 2):512 * (c % 2) + 512]
                dve.wait_ge(sem("down_done"), 2 * NT * it + c + 1)
                if first:
                    nc.vector.tensor_copy(a, B[4 + c % 4][:, :]).then_inc(sem("acc_done"), 1)
                else:
                    TT(a, a, B[4 + c % 4][:, :], ALU.add).then_inc(sem("acc_done"), 1)

        hidden(0, True)
        gather(0, True)
        with dve.Fori(1, NFB - 1) as it:
            hidden(it, False)
            gather(it, False)
        hidden(NFB - 1, False)
        gather(NFB - 1, False)
        dve.wait_ge(sem("g2_evac"), 4)
        dve.wait_ge(sem("acc_done"), 2 * NT * NFB)
        for i in range(NT):
            who = 0 if i == 8 else 1
            dve.wait_ge(sem(f"xr{i % 3}_in"), 48 + 16 * (i // 3 + 1))
            if i >= 2:
                dve.wait_ge(sem("squares"), 4 * NT + 2 * (i - 1))
            step(TT(te[i % 2][:, :], acc[:, i, :], g2b[:, who, :], ALU.mult))
            TT(xe[i % 3][:, :], xe[i % 3][:, :], te[i % 2][:, :], ALU.add).then_inc(sem("end_sum"), 1)
            inverse_ms(ss, var, i, i + 1, "inverse_ms", "squares", 4 * NT + 2 * i + 2)

    ctx.close()


_INS = ['x_prompt', 'x_sample', 'state_ssm_re', 'state_ssm_im', 'c', 'c_ctx', 'ada_w', 'ada_b', 'norm1_g', 'w_in',
        'ssm_lam_re', 'ssm_lam_im', 'ssm_log_dt', 'ssm_b_re', 'ssm_b_im', 'ssm_c_re', 'ssm_c_im', 'ssm_d',
        'ssm_w_glu', 'ssm_b_glu', 'pool_w', 'pool_scale', 'conv_dw_w', 'conv_dw_b', 'conv_ln_g', 'conv_ln_b',
        'w_out', 'norm2_g', 'ffn_w1', 'ffn_w3', 'ffn_w2', 'final_g']
_OUTS = [(1, 128, 1024), (1, 1024, 1024), (1, 1, 2, 32, 64), (1, 1, 2, 32, 64)]


def shape_constants():
    quarter = D // 4
    omega = (1.0 / (10000.0 ** (np.arange(quarter, dtype=np.float32) / np.float32(quarter)))).astype(np.float32)

    def waves(n):
        a = np.arange(n, dtype=np.float32)[:, None] * omega[None]
        return np.concatenate([np.sin(a), np.cos(a)], axis=1).astype(np.float32)

    edges = np.ones((P, 34), np.float32)
    for g, w in enumerate((2, 4, 8, 16)):
        p0, j = 64 * (g % 2), g // 2
        edges[p0:p0 + 64, j] = 1.0 / w
        for i in range(8):
            edges[p0:p0 + 64, 2 + 16 * j + i] = w / (min(i + w // 2, LAT) - max(i - w // 2, 0))
            t = LAT - 8 + i
            edges[p0:p0 + 64, 2 + 16 * j + 8 + i] = w / (min(t + w // 2, LAT) - max(t - w // 2, 0))
    return {"pos_rows": waves(LAT // GRID_W), "pos_cols": waves(GRID_W), "pool_edges": edges}


def kernel(**inputs):
    import concourse.bacc as bacc
    from concourse.bass_utils import run_bass_kernel_spmd

    nc = bacc.Bacc("TRN2", target_bir_lowering=False, num_devices=1)
    arrays = {name: np.ascontiguousarray(inputs[name]) for name in _INS}
    arrays.update(shape_constants())
    ins = {name: nc.dram_tensor(f"in_{name}", a.shape, mybir.dt.from_np(a.dtype), kind="ExternalInput").ap() for name, a in arrays.items()}
    outs = [nc.dram_tensor(f"out_{i}", shape, F32, kind="ExternalOutput").ap() for i, shape in enumerate(_OUTS)]
    build(nc, ins, outs)
    r = run_bass_kernel_spmd(nc, [{f"in_{name}": a for name, a in arrays.items()}], core_ids=[0])
    return tuple(r.results[0][f"out_{i}"] for i in range(len(_OUTS)))
```

```python
from contextlib import ExitStack

import numpy as np
import concourse.bass as bass
from concourse import mybir

F32 = mybir.dt.float32
F32R = mybir.dt.float32r
ACT = mybir.ActivationFunctionType
ALU = mybir.AluOpType

P = 128
D = 1024
KT = D // P
LAT, CTX = 1024, 128
T = LAT + CTX
NB, BW = 3, 384
NT = T // P
GRID_W = 64
D_IN = 1280
DFF = 2816
EPS = 1e-6

CH = 8
G, NS, HD = 32, 64, 16
Q = G
NPAIR = G // 2
LC, CC = LAT // CH, CTX // CH
UC = LC + 1 + CC
SLOTS = UC + 1
BSH = CC + 1
NPOW = CH + 1

POOL_LOW = 6
FB = 2
NFB = DFF // P // FB
TWO_PI = 6.283185307179586
TP1 = 6.28125
TP2 = float(np.float32(TWO_PI - TP1))
TP3 = float(TWO_PI - TP1 - np.float32(TWO_PI - TP1))
ROUND = 12582912.0

V_N1, V_N2, V_GB, V_PS, V_CB, V_LG, V_LB, V_CX, V_CC = 0, 8, 16, 20, 22, 24, 26, 28, 36
VR = 44
TAPS = 31
PAD = TAPS // 2
VL = PAD + LAT + PAD + CTX + PAD
VO = LAT + PAD + CTX
VCTX = LAT + PAD
PZ = 8
PL = PZ + LAT + PZ + CTX + PZ


def view(t, off, dims, p0=0, n=P):
    full = t[:]
    ps = full.ap[0][0]
    return bass.AP(tensor=full.tensor, offset=full.offset + p0 * ps + off, ap=[[ps, n]] + [list(d) for d in dims])


def dview(ap, off, dims):
    return bass.AP(tensor=ap.tensor, offset=ap.offset + off, ap=[list(d) for d in dims])


def build(nc, A, O):
    ctx = ExitStack()

    def at(name, shape, off, dt=F32):
        n = int(np.prod(shape[1:])) * 4
        assert off % 32 == 0 and off + n <= LIMIT, (name, off + n)
        return nc.alloc_sbuf_tensor_at(name, shape, dt, offset=off)

    LIMIT = 229368
    O_NT = 16512
    O_WB = O_NT + 2 * KT * T * 4
    O_UZ = O_WB + 2 * Q * P * 4
    O_ST = O_UZ + 18560
    O_WS = O_ST + 2 * Q * SLOTS * 4
    O_BC = O_WS + 24576
    O_C = O_BC + 16384

    cur = [O_C]

    def const(name, shape, dt=F32):
        n = int(np.prod(shape[1:])) * 4
        t = at(name, shape, cur[0], dt)
        cur[0] += (n + 31) // 32 * 32
        return t

    ident = const("ident", [P, P])
    onesm = const("onesm", [P, P])
    X_TAP = VR
    X_LRE, X_LIM, X_HRE, X_HIM, X_DT = (VR + 2 * TAPS + Q * i for i in range(5))
    NPV = VR + 2 * TAPS + 5 * Q
    pv = const("pv", [P, NPV])
    dcol = const("dcol", [32, NPAIR])
    condT = const("condT", [P, KT, 32])
    modc = const("modc", [P, 48, 2])
    gsc = const("gsc", [P, 2, KT, 2])
    O_POW = cur[0]
    powr = const("powr", [P, NPOW, Q])
    powi = const("powi", [P, NPOW, Q])
    a8i = const("a8i", [P, 2, Q])
    ss = const("ss", [P, 2 * NT])
    rstd = const("rstd", [P, NT])
    ss2 = const("ss2", [P, 2 * NT])
    rstd2 = const("rstd2", [P, NT])
    var = const("var", [P, NT])
    var2 = const("var2", [P, NT])
    edge = const("edge", [P, 34])
    scT = const("scT", [P, 3, 2, Q])
    eps = const("eps", [P, 1])
    dsel = const("dsel", [32, NPAIR, HD])
    a8r = const("a8r", [P, Q])

    nt_hi = at("nt_hi", [P, KT, T], O_NT, F32R)
    nt_lo = at("nt_lo", [P, KT, T], O_NT + KT * T * 4, F32R)
    raw = [at(f"raw{i}", [32, 2 * HD * NS], O_NT + 40960 + i * 8192) for i in range(4)]
    xt = [at(f"xt{i}", [P, D], (O_UZ if i < 4 else O_WB - 16384) + i * 4096) for i in range(NT)]
    posc = at("posc", [P, 512], O_UZ + 16384)
    posr = [at(f"posr{i}", [P, 512], (O_WB + 20480 if i < 6 else O_BC + 8192 - 12288) + i * 2048) for i in range(8)]
    o = O_ST
    wbt_tmp = [at(f"wbt_tmp{i}", [P, 4, P], o + 2048 * i) for i in range(2)]
    o += 4096
    wbt = [[at(f"wbt{s}{r}", [P, 4, P], o + 2048 * (2 * s + r)) for r in range(2)] for s in range(2)]
    o += 8192
    NC = NPOW * HD
    wct_tmp = [at(f"wct_tmp{i}", [P, 4, NC], o + 2304 * i) for i in range(2)]
    o += 4608
    wct = [[at(f"wct{s}{r}", [P, 4, NC], o + 2304 * (2 * s + r)) for r in range(2)] for s in range(2)]
    o += 9216
    wcd = [[at(f"wcd{n}{r}", [P, 4, NC], O_NT + 40960 + 2304 * (2 * n + r)) for r in range(2)] for n in range(4)]
    wcd_tmp = [at(f"wcd_tmp{i}", [P, 4, NC], O_NT + 40960 + 2304 * (8 + i)) for i in range(2)]
    prm = at("prm", [P, 16, Q], o)
    o += 2048
    hf = [at(f"hf{i}", [P, 512], o + 2048 * i) for i in range(2)]
    o += 4096
    arow = [at("arow0", [P, 512], o), at("arow1", [P, 512], O_WS + 20480), at("arow2", [P, 512], O_POW)]
    abias = [at("abias0", [P, 512], o + 2048)] + [at("abias1", [P, 512], O_WS + 18432)] * 2
    o += 4096
    assert o <= O_WS
    o = O_BC + 12288
    rows = at("rows", [VR, P], o)
    rtap = at("rtap", [2 * TAPS, P], o + 512)
    rlam = at("rlam", [Q, 5, P], o + 1024)
    dn = at("dn", [NPAIR, 2 * HD], o + 3584)
    ldt = at("ldt", [Q, 2], o + 3712)
    assert o + 3744 <= O_C
    wb = at("wb", [P, 2, Q, P], O_WB)
    u8 = [at(f"u8{i}", [P, 8, UC], O_UZ + 4640 * i) for i in range(2)]
    zp = [at(f"zp{i}", [P, CH, UC], O_UZ + 9280 + 4640 * i) for i in range(2)]
    st = at("st", [P, 2 * Q * SLOTS], O_ST)
    wst = [at(f"wst{i}", [P, KT, P], O_WS + 4096 * i) for i in range(2)]
    w_hi = [at(f"w_hi{i}", [P, KT, P], O_WS + 8192 + 8192 * i, F32R) for i in range(2)]
    w_lo = [at(f"w_lo{i}", [P, KT, P], O_WS + 12288 + 8192 * i, F32R) for i in range(2)]
    ad0 = [at(f"ad0{i}", [P, 2048], O_WS + 8192 + 8192 * i) for i in range(2)]
    bb = at("bb", [P, 2, Q, HD], O_BC)
    cc = at("cc", [P, 2, Q, HD], O_BC + 4096)
    bblk = at("bblk", [P, 2, Q, 32], O_BC + 8192)
    pu = at("pu", [P, 2, PL], O_WB)
    psum_w = at("psum_w", [P, 2, PL], O_WB + 9408)
    vp = at("vp", [P, 2, VL], O_WB + 18816)
    cacc = at("cacc", [P, 2, VO], O_UZ)
    sig = at("sig", [P, 2, T], O_UZ + 9344)
    wpool = at("wpool", [P, 2, P], O_WB + 28416)
    fin = at("fin", [Q, 2, P], O_WB + 29440)
    scC = at("scC", [P, 3, 2, Q], O_WB + 30464)
    u9 = [at(f"u9{i}", [P, 8, UC], O_WB + 9408 + 4640 * i) for i in range(2)]
    wc = at("wc", [P, 2, Q, NC], O_NT)
    toep = at("toep", [P, G, P], O_NT + 36864)
    kb = at("kb", [32, NPAIR, 15 * HD], O_NT + 53248)
    ad1 = [at(f"ad1{i}", [P, 2048], (O_BC, O_WS + 9216, O_BC + 8192)[i]) for i in range(3)]
    yT = at("yT", [P, 4, CH * UC], O_NT + 53248)
    yb = [at(f"yb{i}", [P, 8, UC], O_WB + 4640 * i) for i in range(2)]
    ymp = at("ymp", [P, 4, T], O_WS)
    yms = at("yms", [P, 4, T], O_ST)
    wglu = at("wglu", [P, 4, 512], O_NT)
    gsig = at("gsig", [P, CH * UC], O_NT + 8192)
    wo = [at("wo1", [P, 4, D], O_BC), at("wo2", [P, 4, D], O_ST + 18432)]
    lnw = at("lnw", [P, 2, VO], O_WB + 18816)
    o = O_WB
    xr = [at(f"xr{i}", [P, D], o + 4096 * i) for i in range(3)]
    o += 12288
    g1b = at("g1b", [P, 2, D], o)
    o += 8192
    posr2 = [at(f"posr2{i}", [P, 512], o + 2048 * i) for i in range(2)]
    posc2 = at("posc2", [P, 512], o + 4096)
    o += 6144
    xn2 = at("xn2", [P, D], o)
    assert o + 4096 <= O_UZ
    tg = at("tg", [P, 512], O_UZ)
    h2f = at("h2f", [P, KT, P], O_UZ + 2048)
    acc = at("acc", [P, NT, D], O_WB)
    fst = [at(f"fst{i}", [P, D], O_UZ + 6144 + 4096 * i) for i in range(3)]
    assert O_UZ + 6144 + 12288 <= O_ST and O_WB + NT * D * 4 <= O_UZ + 6144
    o = O_ST
    f13h = [at(f"f13h{i}", [P, 2, KT, P], o + 16384 * i, F32R) for i in range(2)]
    f13l = [at(f"f13l{i}", [P, 2, KT, P], o + 8192 + 16384 * i, F32R) for i in range(2)]
    o += 32768
    f2h = at("f2h", [P, FB, D], o, F32R)
    f2l = at("f2l", [P, FB, D], o + 8192, F32R)
    o += 16384
    f_hi = at("f_hi", [P, FB, T], o, F32R)
    f_lo = at("f_lo", [P, FB, T], o + FB * T * 4, F32R)
    o += 2 * FB * T * 4
    sa = [at(f"sa{i}", [P, BW], o + 1536 * i) for i in range(2)]
    fv = [at(f"fv{i}", [P, BW], o + 3072 + 1536 * i) for i in range(2)]
    assert o + 6144 <= O_C
    xe = [at(f"xe{i}", [P, D], O_NT + 4096 * i) for i in range(NT)]
    o = O_NT + 4096 * NT
    g2b = at("g2b", [P, 2, D], o)
    fgb = at("fgb", [P, D], o + 8192)
    te = [at(f"te{i}", [P, D], o + 12288 + 4096 * i) for i in range(2)]
    sq = at("sq", [P, D], o + 20480)

    PS = [nc.alloc_psum_tensor(f"bank{i}", [P, 512], F32) for i in range(8)]
    z_dram = nc.dram_tensor("z_dram", [512, CH, UC], F32).ap()
    y_dram = nc.dram_tensor("y_dram", [512, CH, UC], F32).ap()
    wc_dram = nc.dram_tensor("wc_dram", [P, 2, Q, NC], F32).ap()
    kb_dram = nc.dram_tensor("kb_dram", [32, NPAIR, 15 * HD], F32).ap()
    x2_dram = nc.dram_tensor("x2_dram", [T, D], F32).ap()


    sems = {}

    def sem(name):
        if name not in sems:
            sems[name] = nc.alloc_semaphore(name)
        return sems[name]

    ZB = [4, 5, 6]
    VB = [2, 3, 7]
    GB = [(0, 3 * UC), (3 * UC, 3 * UC), (6 * UC, 2 * UC)]
    XG = [range(0, 4), range(4, 8), range(8, 9)]
    TB = [0, 2, 0, 2, 0, 2, 0, 6, 4]
    KC = (0, 1, 4, 5, 2, 3, 6, 7)
    UP = ("ffn_w1", "ffn_w3")

    def x_tile(i):
        return dview(A["x_sample"], i * P * D, [[D, P], [1, D]]) if i < 8 else dview(A["x_prompt"], 0, [[D, P], [1, D]])

    def pos_tile(i):
        return dview(A["pos_rows"], 2 * i * 512, [[512, 2], [0, GRID_W], [1, 512]])

    pos_cols2 = dview(A["pos_cols"], 0, [[0, 2], [512, GRID_W], [1, 512]])

    def wc_views(n):
        q0 = 4 * n
        step, base = (Q, 0) if n < 4 else (-Q, CH * Q)
        lr, li = (view(t, base + q0, [[1, 4], [step, NPOW], [0, HD]]) for t in (powr, powi))
        cr, ci = (view(cc, (r * Q + q0) * HD, [[HD, 4], [0, NPOW], [1, HD]]) for r in range(2))
        return lr, li, cr, ci, lambda t: view(t, 0, [[NC, 4], [HD, NPOW], [1, HD]])

    ADA_SLOTS = [n % 2 for n in range(KT + 4)] + [(n - KT - 2) % 3 for n in range(KT + 4, 3 * KT)]

    def ada_slot(n):
        e = ADA_SLOTS[n]
        return (ad0 if n < KT else ad1)[e], sem(f"ada{e}_in"), 16 * ADA_SLOTS[:n + 1].count(e)

    def ada_used(n):
        return max(m for m in range(n) if ADA_SLOTS[m] == ADA_SLOTS[n]) + 1

    def low_ready(i):
        return (sem("w_in_lo"), i + 1) if i < POOL_LOW else (sem("w_in_lo_pool"), i + 1 - POOL_LOW)

    def piece_count(n, c):
        return 16 * (c // 3 + 1) + (n - c) // 6 * 32 if isinstance(n, int) else (n - c) * 16 // 3 + 16 * (c // 3 + 1)

    def piece(c):
        c2 = c - 6 if c >= 6 else c
        if c2 < 4:
            return (f13h[c2 // 2][:, c2 % 2, :, :], f13l[c2 // 2][:, c2 % 2, :, :],
                    fst[c % 3][:, :].rearrange("p (k n) -> p k n", n=P))
        return f2h[:, c2 - 4, :], f2l[:, c2 - 4, :], fst[c % 3][:, :]

    block = ctx.enter_context(nc.Block())


    @block.sync
    def _(sp):
        def x_in(i):
            sp.dma_start(xt[i][:, :], x_tile(i)).then_inc(sem(f"x{i}_in"), 16)
            if i < 8:
                sp.dma_start(posr[i][:, :], pos_tile(i)).then_inc(sem(f"x{i}_in"), 16)

        def ada_bias(a):
            for q in range(4):
                sp.dma_start(abias[a][32 * q:32 * q + 32, :],
                             dview(A["ada_b"], a * 2048 + q * 512, [[0, 32], [1, 512]])).then_inc(sem(f"ada_bias{a}_in"), 16)

        def ada_in(n):
            slot, arrived, _ = ada_slot(n)
            sp.dma_start(slot[:, :], dview(A["ada_w"], n % KT * P * 6 * D + n // KT * 2048, [[6 * D, P], [1, 2048]])).then_inc(arrived, 16)

        def w_in_load(i):
            sp.dma_start(wst[i % 2][:, :, :], dview(A["w_in"], i * P, [[D_IN, P], [P * D_IN, KT], [1, P]])).then_inc(sem(f"w_in{i % 2}_in"), 16)

        ada_in(0)
        ada_in(1)
        for name, r0, n in (("norm1_g", V_N1, 8), ("norm2_g", V_N2, 8), ("ssm_b_glu", V_GB, 4), ("pool_scale", V_PS, 2),
                            ("conv_dw_b", V_CB, 2), ("conv_ln_g", V_LG, 2), ("conv_ln_b", V_LB, 2),
                            ("c_ctx", V_CX, 8), ("c", V_CC, 8)):
            sp.dma_start(rows[r0:r0 + n, :], dview(A[name], 0, [[P, n], [1, P]])).then_inc(sem("vectors_in"), 16)
        sp.dma_start(rtap[:, :], dview(A["conv_dw_w"], 0, [[P, 2 * TAPS], [1, P]])).then_inc(sem("vectors_in"), 16)
        for i, name in enumerate(("ssm_lam_re", "ssm_lam_im", "state_ssm_re", "state_ssm_im")):
            sp.dma_start(rlam[:, i, :], dview(A[name], 0, [[P, Q], [1, P]])).then_inc(sem("vectors_in"), 16)
        sp.dma_start(dn[:, :], dview(A["ssm_d"], 0, [[32, NPAIR], [1, 32]])).then_inc(sem("vectors_in"), 16)
        sp.dma_start(ldt[:, :], dview(A["ssm_log_dt"], 0, [[2, Q], [1, 2]])).then_inc(sem("log_dt_in"), 16)
        sp.dma_start(posc[:, :], pos_cols2).then_inc(sem("posc_in"), 16)
        x_in(0)
        x_in(1)
        for i, name in enumerate(("ssm_b_re", "ssm_b_im", "ssm_c_re", "ssm_c_im")):
            if i < 2:
                sp.dma_start(raw[i][:, :], dview(A[name], 0, [[2048, Q], [1, 2048]])).then_inc(sem("raws_in"), 16)
            else:
                for par in range(2):
                    sp.dma_start(view(raw[i], par * NS, [[P, HD], [1, NS]], 0, Q),
                                 dview(A[name], par * HD * NS, [[2048, Q], [NS, HD], [1, NS]])).then_inc(sem("raws_in"), 16)
        for n in range(2, KT):
            sp.wait_ge(sem("ada_tile"), n - 1)
            ada_in(n)
            x_in(n)
        x_in(8)
        ada_bias(0)
        w_in_load(0)
        w_in_load(1)
        sp.dma_start(edge[:, :], A["pool_edges"]).then_inc(sem("edges_in"), 16)
        for n in range(4):
            sp.wait_ge(sem("wc_made_dve"), 2 * (n + 1))
            for r in range(2):
                sp.dma_start(dview(wc_dram, (r * Q + 4 * n) * NC, [[2 * Q * NC, P], [1, 4 * NC]]),
                             view(wcd[n][r], 0, [[1, 4 * NC]])).then_inc(sem("wc_out2"), 16)
        for i in range(10):
            if i + 2 < 10:
                sp.wait_ge(*low_ready(i))
                w_in_load(i + 2)
            if i < 4:
                sp.wait_ge(sem("z_evac"), NB * (i + 1))
                sp.wait_ge(sem("zero_column"), 2)
                sp.dma_start(dview(z_dram, i * P * CH * UC, [[CH * UC, P], [1, CH * UC]]),
                             view(zp[i % 2], 0, [[1, CH * UC]])).then_inc(sem("z_out"), 16)
                sp.wait_ge(sem("z_out"), 16 * (i + 1))
                if i >= 2:
                    sp.wait_ge(sem("v_done"), 8 * (i - 1))
                for s in range(CH):
                    sp.dma_start(u8[i % 2][16 * s:16 * s + 16, :, :],
                                 dview(z_dram, i * P * CH * UC + s * UC, [[CH * UC, 16], [16 * CH * UC, 8], [1, UC]])).then_inc(sem(f"u{i}_in"), 16)
        sp.wait_ge(sem("gaps"), 13)
        for g in range(4):
            h = 64 * (g % 2)
            sp.dma_start(wpool[h:h + 64, g // 2, h:h + 64], dview(A["pool_w"], g * 4096, [[64, 64], [1, 64]])).then_inc(sem("wpool_in"), 16)
        sp.wait_ge(sem("bblk"), 2)
        sp.wait_ge(sem("wbt_made"), 16)
        ada_in(KT)
        sp.wait_ge(sem("z_done"), 30)
        ada_in(KT + 1)
        for s in range(2):
            sp.wait_ge(sem(f"wc_out{s}"), 64)
        sp.wait_ge(sem("wc_out2"), 128)
        for e in range(2):
            sp.dma_start(view(wc, 8 * e * NC, [[NPAIR * NC, 4], [1, 8 * NC]]),
                         dview(wc_dram, 8 * e * NC, [[2 * Q * NC, P], [NPAIR * NC, 4], [1, 8 * NC]])).then_inc(sem(f"wc{e}_in"), 16)
        def ada_more(n0, n1):
            for n in range(n0, n1):
                sp.wait_ge(sem("ada_tile"), ada_used(n))
                ada_in(n)

        ada_bias(1)
        ada_more(KT + 2, KT + 4)
        sp.wait_ge(sem("kb_evac"), 8)
        sp.dma_start(kb_dram, kb[:, :, :]).then_inc(sem("kb_out"), 16)
        ada_in(KT + 4)
        ada_more(KT + 5, KT + 7)
        sp.wait_ge(sem("kb_out"), 16)
        RK = NPAIR * 15 * HD
        for s in range(CH):
            for par in range(2):
                sp.dma_start(view(toep, par * P, [[2 * P, NPAIR], [1, P]], 16 * s, 16),
                             dview(kb_dram, par * 16 * RK + (CH - 1 - s) * HD, [[RK, 16], [15 * HD, NPAIR], [1, P]])).then_inc(sem("toep_in"), 16)
        def u_again(j):
            for s in range(CH):
                sp.dma_start(u9[j % 2][16 * s:16 * s + 16, :, :],
                             dview(z_dram, j * P * CH * UC + s * UC, [[CH * UC, 16], [16 * CH * UC, 8], [1, UC]])).then_inc(sem(f"u{j}_in"), 16)

        sp.wait_ge(sem("pooled"), 2)
        u_again(0)
        ada_more(KT + 7, 2 * KT)
        u_again(1)
        sp.wait_ge(sem("ada_bank"), 2)
        ada_bias(2)
        ada_more(2 * KT, 2 * KT + 3)
        for r in range(2):
            sp.wait_ge(sem("fin_evac"), r + 1)
            sp.dma_start(dview(O[2 + r], 0, [[P, Q], [1, P]]), fin[:, r, :]).then_inc(sem("outputs"), 16)
        for j in range(4):
            sp.wait_ge(sem("y_evac"), 4 * (j + 1))
            if j + 2 < 4:
                sp.wait_ge(sem("y_done"), 2 * (j + 1))
                u_again(j + 2)
            for t in range(CH):
                sp.dma_start(dview(y_dram, j * P * CH * UC + t * UC, [[CH * UC, 16], [16 * CH * UC, 8], [1, UC]]),
                             yb[j % 2][16 * t:16 * t + 16, :, :]).then_inc(sem("y_out"), 16)
            sp.wait_ge(sem("y_out"), 16 * 8 * (j + 1))
            sp.dma_start(view(yT, j * CH * UC, [[1, CH * UC]]), dview(y_dram, j * P * CH * UC, [[CH * UC, P], [1, CH * UC]])).then_inc(sem("yT_in"), 16)
            if j < 2:
                ada_more(2 * KT + 3 + 2 * j, 2 * KT + 5 + j)
            elif j == 2:
                ada_more(3 * KT - 2, 3 * KT - 1)
        ada_more(3 * KT - 1, 3 * KT)
        sp.wait_ge(sem("y_done"), 8)
        sp.dma_start(wglu[:, :, :], dview(A["ssm_w_glu"], 0, [[512, P], [P * 512, 4], [1, 512]])).then_inc(sem("wglu_in"), 16)
        sp.dma_start(wo[1][:, :, :], dview(A["w_out"], 512 * D, [[D, P], [P * D, 4], [1, D]])).then_inc(sem("wo1_in"), 16)
        sp.wait_ge(sem("ada_tile"), 3 * KT)
        sp.dma_start(wo[0][:, :, :], dview(A["w_out"], 0, [[D, P], [P * D, 4], [1, D]])).then_inc(sem("wo0_in"), 16)
        sp.wait_ge(sem("conv_out"), 4)
        sp.dma_start(posc2[:, :], pos_cols2).then_inc(sem("posc2_in"), 16)

        def piece_in(n, c, w, tile, dynamic):
            if dynamic or n >= 3:
                sp.wait_ge(sem("piece_lo"), n - 2)
            dst = fst[c % 3][:, :]
            if w == "ffn_w2":
                src = A[w][0][bass.ds(tile * P, P), :]
            else:
                src = A[w][0].rearrange("(k p) n -> p k n", p=P)[:, :, bass.ds(tile * P, P)]
                dst = dst.rearrange("p (k n) -> p k n", n=P)
            sp.dma_start(dst, src).then_inc(sem(f"piece{c % 3}_in"), 16)

        def x2_out(i):
            sp.wait_ge(sem("x2_made"), 2 * (i + 1))
            sp.dma_start(dview(x2_dram, i * P * D, [[D, P], [1, D]]), xr[i % 3][:, :]).then_inc(sem(f"tile_out{i % 3}"), 16)

        for i in range(NT):
            if i >= 3:
                sp.wait_ge(sem(f"tile_out{i % 3}"), 16 * (i // 3))
                sp.wait_ge(sem("x2_normed"), i - 2)
            sp.dma_start(xr[i % 3][:, :], x_tile(i)).then_inc(sem(f"xr{i % 3}_in"), 16)
            if i < 8:
                if i >= 2:
                    sp.wait_ge(sem("pos_half"), 2 * (8 + i - 1))
                sp.dma_start(posr2[i % 2][:, :], pos_tile(i)).then_inc(sem(f"posr{i % 2}_in"), 16)
            if i >= 1:
                x2_out(i - 1)
            if i >= 4 and i < 7:
                piece_in(i - 4, i - 4, UP[(i - 4) % 2], (i - 4) // 2, False)
        x2_out(NT - 1)

        def pieces_in(it, dynamic, last):
            n0 = 4 + 6 * it
            for f in range(FB):
                piece_in(n0 + f, 4 + f, "ffn_w2", FB * it + f, dynamic)
            if not last:
                for f in range(FB):
                    for e, w in enumerate(UP):
                        piece_in(n0 + 2 + 2 * f + e, 6 + 2 * f + e, w, FB * (it + 1) + f, dynamic)

        piece_in(3, 3, UP[1], 1, False)
        pieces_in(0, False, False)
        with sp.Fori(1, NFB - 1) as it:
            pieces_in(it, True, False)
        pieces_in(NFB - 1, False, True)
        sp.wait_ge(sem("up_done"), 2 * NB * NFB)
        for i in range(NT):
            if i < 3:
                sp.wait_ge(sem(f"tile_out{i}"), 48)
            sp.dma_start(xe[i][:, :], dview(x2_dram, i * P * D, [[D, P], [1, D]])).then_inc(sem(f"x{i}_in"), 16)
        sp.dma_start(fgb[:, :], dview(A["final_g"], 0, [[0, P], [1, D]])).then_inc(sem("final_g_in"), 16)
        for i in range(NT):
            sp.wait_ge(sem("y_made"), i + 1)
            dst = dview(O[1], i * P * D, [[D, P], [1, D]]) if i < 8 else dview(O[0], 0, [[D, P], [1, D]])
            sp.dma_start(dst, xe[i][:, :]).then_inc(sem("outputs"), 16)
        sp.wait_ge(sem("outputs"), 32 + 16 * NT)

    @block.gpsimd
    def _(pool):
        nc.gpsimd.memset(ident[:, :], 0.0).then_inc(sem("ident0"), 1)
        nc.gpsimd.memset(onesm[:, :], 1.0 / 256).then_inc(sem("ones"), 1)
        nc.gpsimd.memset(eps[:, :], EPS).then_inc(sem("ones"), 1)
        pool.wait_ge(sem("ident0"), 1)
        nc.gpsimd.affine_select(out=ident[:, :], in_=ident[:, :], compare_op=ALU.not_equal, fill=1.0,
                                base=0, pattern=[[-1, P]], channel_multiplier=1).then_inc(sem("ident"), 1)
        def pos_add(i):
            if i == 0:
                pool.wait_ge(sem("posc_in"), 16)
            pool.wait_ge(sem(f"x{i}_in"), 32)
            nc.gpsimd.tensor_tensor(xt[i][:, 0:512], xt[i][:, 0:512], posr[i][:, :], ALU.add).then_inc(sem("pos_half"), 1)
            nc.gpsimd.tensor_tensor(xt[i][:, 512:1024], xt[i][:, 512:1024], posc[:, :], ALU.add).then_inc(sem("pos_half"), 1)

        def wc_piece(n):
            lr, li, cr, ci, v3 = wc_views(4 + n)
            q0 = 4 * (4 + n)
            slot, tmp = wct[n % 2], wct_tmp
            if n >= 2:
                pool.wait_ge(sem(f"wc_out{n % 2}"), 32 * (n // 2))
            if n >= 1:
                pool.wait_ge(sem("wc_made"), 2 * n)
            nc.gpsimd.tensor_tensor(v3(slot[0]), lr, cr, ALU.mult).then_inc(sem("wc_terms"), 1)
            nc.gpsimd.tensor_tensor(v3(tmp[0]), li, ci, ALU.mult).then_inc(sem("wc_terms"), 1)
            nc.gpsimd.tensor_tensor(v3(slot[1]), lr, ci, ALU.mult).then_inc(sem("wc_terms"), 1)
            nc.gpsimd.tensor_tensor(v3(tmp[1]), li, cr, ALU.mult).then_inc(sem("wc_terms"), 1)
            pool.wait_ge(sem("wc_terms"), 4 * n + 2)
            nc.gpsimd.tensor_tensor(slot[0][:, :, :], slot[0][:, :, :], tmp[0][:, :, :], ALU.add).then_inc(sem("wc_made"), 1)
            pool.wait_ge(sem("wc_terms"), 4 * n + 4)
            nc.gpsimd.tensor_tensor(slot[1][:, :, :], slot[1][:, :, :], tmp[1][:, :, :], ALU.subtract).then_inc(sem("wc_made"), 1)
            pool.wait_ge(sem("wc_made"), 2 * n + 2)
            for r in range(2):
                pool.dma_start(dview(wc_dram, (r * Q + q0) * NC, [[2 * Q * NC, P], [1, 4 * NC]]),
                               view(slot[r], 0, [[1, 4 * NC]])).then_inc(sem(f"wc_out{n % 2}"), 16)

        for i in range(8):
            pos_add(i)
        pool.wait_ge(sem("powers"), 1)
        pool.wait_ge(sem("cc_evac"), 2)
        wc_piece(0)
        pool.wait_ge(sem("xT_bank"), 24)
        for s in range(2):
            nc.gpsimd.memset(zp[s][:, :, LC:LC + 1], 0.0).then_inc(sem("zero_column"), 1)
        for n in range(1, 4):
            wc_piece(n)
        pool.wait_ge(sem("v_done"), 32)
        for j in range(2):
            for o0 in (0, PZ + LAT, PL - PZ):
                nc.gpsimd.memset(pu[:, j, o0:o0 + PZ], 0.0).then_inc(sem("gaps"), 1)
            for o0 in (0, PAD + LAT, VL - PAD):
                nc.gpsimd.memset(vp[:, j, o0:o0 + PAD], 0.0).then_inc(sem("gaps"), 1)
        nc.gpsimd.memset(wpool[:, :, :], 0.0).then_inc(sem("gaps"), 1)
        for i in range(POOL_LOW, 10):
            if i == POOL_LOW + 1:
                nc.gpsimd.memset(bblk[:, :, :, :], 0.0).then_inc(sem("bblk0"), 1)
            pool.wait_ge(sem("w_in_hi"), i + 1)
            nc.gpsimd.tensor_tensor(w_lo[i % 2][:, :, :], wst[i % 2][:, :, :], w_hi[i % 2][:, :, :].bitcast(F32), ALU.subtract).then_inc(low_ready(i)[0], 1)
        pool.wait_ge(sem("bblk0"), 1)
        pool.wait_ge(*low_ready(9))
        for par in range(2):
            p0 = 64 * par
            nc.gpsimd.tensor_copy(view(bblk, 16 * par, [[32, 2 * Q], [1, HD]], p0, 64),
                                  view(bb, 0, [[HD, 2 * Q], [1, HD]], p0, 64)).then_inc(sem("bblk"), 1)
        pool.wait_ge(sem("edges_in"), 16)
        pool.wait_ge(sem("gaps"), 12)
        pool.wait_ge(sem("bblk"), 2)
        n_pool = [0]

        def pstep(ins):
            n_pool[0] += 1
            ins.then_inc(sem("pool_step"), 1)
            pool.wait_ge(sem("pool_step"), n_pool[0])

        for j in range(2):
            pool.wait_ge(sem("z_evac"), NB * (5 + j))
            W0, W1 = (lambda a, b, p0=0, n=P: psum_w[p0:p0 + n, 0, a:b]), (lambda a, b, p0=0, n=P: psum_w[p0:p0 + n, 1, a:b])
            pstep(nc.gpsimd.tensor_tensor(W0(1, PL), pu[:, j, 0:PL - 1], pu[:, j, 1:PL], ALU.add))
            if j == 0:
                pstep(nc.gpsimd.tensor_tensor(W1(2, PL - 1, 64, 64), W0(1, PL - 2, 64, 64), W0(3, PL, 64, 64), ALU.add))
            else:
                pstep(nc.gpsimd.tensor_tensor(W1(2, PL - 1), W0(1, PL - 2), W0(3, PL), ALU.add))
                pstep(nc.gpsimd.tensor_tensor(W0(4, PL - 3), W1(2, PL - 5), W1(6, PL - 1), ALU.add))
                pstep(nc.gpsimd.tensor_tensor(W1(8, PL - 7, 64, 64), W0(4, PL - 11, 64, 64), W0(12, PL - 3, 64, 64), ALU.add))
            for h, W in ((0, W0), (1, W1)):
                p0 = 64 * h
                pstep(nc.gpsimd.tensor_scalar(W(PZ, PL - PZ, p0, 64), W(PZ, PL - PZ, p0, 64), edge[p0:p0 + 64, j:j + 1], None, ALU.mult))
                for start, length in ((PZ, LAT), (PZ + LAT + PZ, CTX)):
                    for side in range(2):
                        a = start if side == 0 else start + length - 8
                        e0 = 2 + 16 * j + 8 * side
                        pstep(nc.gpsimd.tensor_tensor(W(a, a + 8, p0, 64), W(a, a + 8, p0, 64), edge[p0:p0 + 64, e0:e0 + 8], ALU.mult))
                pstep(nc.gpsimd.tensor_tensor(pu[p0:p0 + 64, j, PZ:PL - PZ], W(PZ, PL - PZ, p0, 64), pu[p0:p0 + 64, j, PZ:PL - PZ], ALU.subtract))
            pool.sem_inc(sem("pooled"), 1)
        for j in range(2):
            pool.wait_ge(sem("z_evac"), NB * (9 + j))
            for a0, b0, n in ((PAD, 0, LAT), (PAD + LAT + PAD, LAT, CTX)):
                nc.gpsimd.tensor_tensor(vp[:, j, a0:a0 + n], vp[:, j, a0:a0 + n], sig[:, j, b0:b0 + n], ALU.mult).then_inc(sem("gated"), 1)
        pool.wait_ge(sem("posc2_in"), 16)
        for i in range(8):
            pool.wait_ge(sem(f"xr{i % 3}_in"), 16 * (i // 3 + 1))
            pool.wait_ge(sem(f"posr{i % 2}_in"), 16 * (i // 2 + 1))
            nc.gpsimd.tensor_tensor(xr[i % 3][:, 0:512], xr[i % 3][:, 0:512], posr2[i % 2][:, :], ALU.add).then_inc(sem("pos_half"), 1)
            nc.gpsimd.tensor_tensor(xr[i % 3][:, 512:1024], xr[i % 3][:, 512:1024], posc2[:, :], ALU.add).then_inc(sem("pos_half"), 1)
        def piece_lo(n, c):
            pool.wait_ge(sem("piece_hi"), n + 1)
            hi, lo, src = piece(c)
            nc.gpsimd.tensor_tensor(lo, src, hi.bitcast(F32), ALU.subtract).then_inc(sem("piece_lo"), 1)

        def f_low(it, f):
            for n in range(NB):
                b = NB * f + n
                pool.wait_ge(sem("f_hi"), 2 * NB * it + b + 1)
                nc.gpsimd.tensor_tensor(f_lo[:, f, n * BW:(n + 1) * BW], fv[b % 2][:, :],
                                        f_hi[:, f, n * BW:(n + 1) * BW].bitcast(F32), ALU.subtract).then_inc(sem("f_lo"), 1)

        def lows(it, last):
            n0 = 4 + 6 * it
            piece_lo(n0, 4)
            piece_lo(n0 + 1, 5)
            for f in range(FB):
                f_low(it, f)
                if not last:
                    for e in range(2):
                        piece_lo(n0 + 2 + 2 * f + e, 6 + 2 * f + e)

        for n in range(4):
            piece_lo(n, n)
        lows(0, False)
        with pool.Fori(1, NFB - 1) as it:
            lows(it, False)
        lows(NFB - 1, True)
        for i in range(NT):
            if i == 0:
                pool.wait_ge(sem("final_g_in"), 16)
            pool.wait_ge(sem("end_normed"), i + 1)
            nc.gpsimd.tensor_tensor(xe[i][:, :], xe[i][:, :], fgb[:, :], ALU.mult).then_inc(sem("y_made"), 1)

    B = PS

    def three(out, hi_w, lo_w, hi_x, lo_x, start, stop):
        nc.tensor.matmul(out, hi_w, hi_x, start=start, stop=False)
        nc.tensor.matmul(out, hi_w, lo_x, start=False, stop=False)
        return nc.tensor.matmul(out, lo_w, hi_x, start=False, stop=stop)

    @block.tensor
    def _(pe):
        mm, tr = nc.tensor.matmul, nc.tensor.transpose
        pe.wait_ge(sem("ident"), 1)
        pe.wait_ge(sem("vectors_in"), 240)
        pe.wait_ge(sem("dt_rows"), 1)
        tr(B[6][:, 0:VR], rows[:, :], ident[0:VR, 0:VR])
        tr(B[6][:, X_TAP:X_TAP + 2 * TAPS], rtap[:, :], ident[0:2 * TAPS, 0:2 * TAPS])
        for i in range(5):
            tr(B[6][:, X_LRE + Q * i:X_LRE + Q * (i + 1)], rlam[:, i, :], ident[0:Q, 0:Q])
        tr(B[7][0:32, 0:NPAIR], dn[:, :], ident[0:NPAIR, 0:NPAIR]).then_inc(sem("params_turned"), 1)

        def raws_turn():
            pe.wait_ge(sem("raws_in"), 96)
            for i in range(4):
                for h in range(HD):
                    src = view(raw[i], h, [[HD, P]], 0, Q) if i < 2 else view(raw[i], h * P, [[1, P]], 0, Q)
                    last = tr(B[i][:, h * Q:(h + 1) * Q], src, ident[0:Q, 0:Q])
                last.then_inc(sem("raws_turned"), 1)

        def ada_tiles(a, k0, k1, bank):
            for k in range(k0, k1):
                slot, arrived, count = ada_slot(KT * a + k)
                pe.wait_ge(arrived, count)
                for q in range(4):
                    last = mm(bank[32 * q:32 * q + 32, :], condT[:, k, :], slot[:, 512 * q:512 * q + 512], start=(k == 0), stop=False)
                last.then_inc(sem("ada_tile"), 1)

        def ada_bias_add(a, bank):
            pe.wait_ge(sem(f"ada_bias{a}_in"), 64)
            for q in range(4):
                last = mm(bank[32 * q:32 * q + 32, :], ident[32 * q:32 * q + 32, 32 * q:32 * q + 32], abias[a][32 * q:32 * q + 32, :], start=False, stop=True)
            last.then_inc(sem("ada_bank"), 1)

        def mod_turn(a, bank):
            pe.wait_ge(sem("ada_row"), a + 1)
            for b in range(4):
                last = tr(bank[:, P * b:P * b + P], arow[a][:, P * b:P * b + P], ident[:, :])
            last.then_inc(sem("mod_turned"), 1)

        def x_turns(n0, n1):
            for n in range(n0, n1):
                grp, k = XG[n // KT], n % KT
                if n == 0:
                    pe.wait_ge(sem("bb_made"), 2)
                    pe.wait_ge(sem("cc_evac"), 2)
                if k == 0:
                    pe.wait_ge(sem("x_normed"), grp[-1] + 1)
                if n >= 4:
                    pe.wait_ge(sem("h_evac"), n - 3)
                for t, i in enumerate(grp):
                    last = tr(B[n % 4][:, P * t:P * t + P], xt[i][:, P * k:P * k + P], ident[:, :])
                last.then_inc(sem("xT_bank"), 1)

        pe.wait_ge(sem("cond"), 2)
        ada_tiles(0, 0, 4, B[4])
        raws_turn()
        ada_tiles(0, 4, KT, B[4])
        ada_bias_add(0, B[4])
        x_turns(0, 4)
        mod_turn(0, B[5])
        x_turns(4, 2 * KT)

        def z_tile(i):
            pe.wait_ge(*low_ready(i))
            for b in range(NB):
                n = NB * i + b
                if n < 3:
                    pe.wait_ge(sem("mod_evac"), 1)
                    pe.wait_ge(sem("squares"), 2 * NT)
                    pe.wait_ge(sem("h_split"), KT * (n + 1))
                    if n == 1:
                        x_turns(2 * KT, 3 * KT)
                else:
                    pe.wait_ge(sem("z_evac"), n - 2)
                for k in range(KT):
                    last = three(B[ZB[b]][:, 0:BW], w_hi[i % 2][:, k, :], w_lo[i % 2][:, k, :],
                                 nt_hi[:, k, b * BW:(b + 1) * BW], nt_lo[:, k, b * BW:(b + 1) * BW], k == 0, k == KT - 1)
                last.then_inc(sem("z_done"), 1)

        def wb_turn(j):
            for d in range(2):
                pe.wait_ge(sem("wbt_made"), 2 * (2 * j + d + 1))
                for r in range(2):
                    c = 4 * j + 2 * d + r
                    pe.wait_ge(sem("h_evac"), 24) if c < 2 else pe.wait_ge(sem("wb_evac"), c - 1)
                    for i in range(4):
                        last = tr(B[c % 2][:, P * i:P * i + P], wbt[d][r][:, i, :], ident[:, :])
                    last.then_inc(sem("wb_turned"), 1)

        def state_inputs(j):
            pe.wait_ge(sem(f"u{j}_in"), 128)
            pe.wait_ge(sem("wb_evac"), 4 * j + 4)
            for d in range(2):
                for pp in range(4):
                    c = 8 * j + 4 * d + pp
                    if c >= 3:
                        pe.wait_ge(sem("v_evac"), c - 2)
                    q = NPAIR * d + 4 * j + pp
                    for par in range(2):
                        rhs = u8[j % 2][:, 2 * pp + par, :] if d == 0 else u8[j % 2][:, 2 * pp + par, ::-1]
                        for r in range(2):
                            last = mm(B[VB[c % 3]][64 * par:64 * par + 64, UC * r:UC * r + UC],
                                      wb[:, r, q, 64 * par:64 * par + 64], rhs, start=True, stop=True)
                    last.then_inc(sem("v_done"), 1)

        for i in range(10):
            z_tile(i)
            if i < 4:
                wb_turn(i)
            elif i == 4:
                state_inputs(2)
                state_inputs(3)
            if i == 3:
                state_inputs(0)
                state_inputs(1)
        pe.wait_ge(sem("bblk"), 2)
        pe.wait_ge(sem("dsel"), 1)
        pe.wait_ge(sem("v_evac"), 32)
        pe.wait_ge(sem("wb_evac"), 16)
        ada_tiles(1, 0, 2, B[0])
        for n, c in enumerate(KC):
            bank = B[(7, 2)[n % 2]]
            if n % 4 == 0:
                pe.wait_ge(sem(f"wc{n // 4}_in"), 16)
            if n >= 2:
                pe.wait_ge(sem("kb_evac"), n - 1)
            for i in range(4):
                gp = 4 * (c % 4) + i
                o = P * i
                if c < 4:
                    for r in range(2):
                        mm(bank[0:32, o:o + P], bblk[:, r, gp, :], wc[:, r, gp, 0:P], start=(r == 0), stop=False)
                    for r in range(2):
                        mm(bank[0:32, o:o + HD], bblk[:, r, NPAIR + gp, :], wc[:, r, NPAIR + gp, P:P + HD], start=False, stop=False)
                    last = mm(bank[0:32, o:o + HD], ident[0:32, 0:32], dsel[:, gp, :], start=False, stop=True)
                else:
                    for r in range(2):
                        last = mm(bank[0:32, o:o + P], bblk[:, r, NPAIR + gp, :], wc[:, r, NPAIR + gp, HD:HD + P], start=(r == 0), stop=(r == 1))
            last.then_inc(sem("kb_done"), 1)
        ada_tiles(1, 2, KT, B[0])
        ada_bias_add(1, B[0])
        pe.wait_ge(sem("wpool_in"), 64)
        pe.wait_ge(sem("z_evac"), 30)
        pe.wait_ge(sem("kb_evac"), 8)
        for j in range(2):
            pe.wait_ge(sem("pooled"), j + 1)
            for b in range(NB):
                n = NB * j + b
                if n >= 2:
                    pe.wait_ge(sem("pool_evac"), n - 1)
                bank = B[6 + n % 2]
                if b < 2:
                    last = mm(bank[:, 0:BW], wpool[:, j, :], pu[:, j, PZ + b * BW:PZ + (b + 1) * BW], start=True, stop=True)
                else:
                    mm(bank[:, 0:256], wpool[:, j, :], pu[:, j, PZ + 768:PZ + LAT], start=True, stop=True)
                    last = mm(bank[:, 256:BW], wpool[:, j, :], pu[:, j, PZ + LAT + PZ:PZ + LAT + PZ + CTX], start=True, stop=True)
                last.then_inc(sem("pool_done"), 1)
        mod_turn(1, B[1])
        pe.wait_ge(sem("scan_done"), 1)
        pe.wait_ge(sem("pool_evac"), 6)
        for r in range(2):
            last = tr(B[6][0:Q, P * r:P * r + P], scT[:, 0, r, :], ident[:, :])
        last.then_inc(sem("fin_turned"), 1)
        pe.wait_ge(sem("toep_in"), 256)
        pe.wait_ge(sem("kb_evac"), 8)
        for c in range(8):
            j = c // 2
            if c % 2 == 0:
                pe.wait_ge(sem(f"u{j}_in"), 256)
            if c >= 2:
                pe.wait_ge(sem("y_evac"), 2 * (c - 1))
            for i in range(2):
                gp = 2 * c + i
                for par in range(2):
                    out = B[(2, 4)[c % 2] + par][:, UC * i:UC * i + UC]
                    p0 = 64 * par
                    mm(out, toep[:, 2 * gp + par, :], u9[j % 2][:, (2 * gp + par) % 8, :], start=True, stop=False)
                    for r in range(2):
                        base = (r * Q + gp) * SLOTS
                        mm(out, wc[p0:p0 + 64, r, gp, HD:HD + P], view(st, base, [[1, UC]], p0, 64), start=False, stop=False)
                    for r in range(2):
                        base = (r * Q + NPAIR + gp) * SLOTS
                        last = mm(out, wc[p0:p0 + 64, r, NPAIR + gp, 0:P], view(st, base + UC - 1, [[-1, UC]], p0, 64), start=False, stop=(r == 1))
            last.then_inc(sem("y_done"), 1)
            if c % 2 and c < 7:
                pe.wait_ge(sem("mod_evac"), 2)
                ada_tiles(2, (0, 2, 3)[c // 2], (2, 3, 4)[c // 2], B[0])
        ada_tiles(2, 4, KT, B[0])
        ada_bias_add(2, B[0])
        pe.wait_ge(sem("yT_in"), 64)
        pe.wait_ge(sem("wglu_in"), 16)
        pe.wait_ge(sem("ada_row"), 3)
        pe.wait_ge(sem("fin_evac"), 2)

        def glu_tile(m):
            for b, (c0, n) in enumerate(GB):
                c = NB * m + b
                if c >= 3:
                    pe.wait_ge(sem("glu_gate"), c - 2)
                for k in range(4):
                    last = mm(B[(6, 7, 0)[b]][:, 0:n], wglu[:, k, P * m:P * m + P], yT[:, k, c0:c0 + n], start=(k == 0), stop=(k == 3))
                last.then_inc(sem("glu_done"), 1)

        def channel_mean(src, done, b):
            for j in range(2):
                last = mm(B[1 + b][:, 0:389], onesm[:, :], src[:, j, 389 * b:389 * b + 389], start=(j == 0), stop=(j == 1))
            last.then_inc(sem(done), 1)

        glu_tile(0)
        mod_turn(2, B[1])
        pe.wait_ge(sem("mod_evac"), 3)
        pe.wait_ge(sem("y_evac"), 16)
        pe.wait_ge(sem("conv_made"), 2)
        for b in range(NB):
            channel_mean(cacc, "mean_done", b)
        glu_tile(1)
        glu_tile(2)
        for b in range(NB):
            pe.wait_ge(sem("dev_squared"), 2 * (b + 1))
            channel_mean(lnw, "var_done", b)
        glu_tile(3)
        def gate_rows(a, q0, banks):
            for who in range(2):
                for h in range(2):
                    q = q0 + h
                    last = mm(banks[2 * who + h][:, :], ident[32 * q:32 * q + 32, 32 * q + 16 * who:32 * q + 16 * who + 1].broadcast_to([32, P]),
                              arow[a][32 * q:32 * q + 32, :], start=True, stop=True)
            last.then_inc(sem("gate_rows"), 1)

        pe.wait_ge(sem("glu_gate"), 12)
        gate_rows(1, 0, B[4:8])
        def h2_turn(i):
            pe.wait_ge(sem("x2_normed"), i + 1)
            if i >= 2:
                pe.wait_ge(sem("h2_evac"), i - 1)
            for k in range(KT):
                last = tr(B[TB[i] + k // 4][:, P * (k % 4):P * (k % 4) + P], xn2[:, P * k:P * k + P], ident[:, :])
            last.then_inc(sem("h2_turned"), 1)

        pe.wait_ge(sem("wo0_in"), 16)
        pe.wait_ge(sem("wo1_in"), 16)
        pe.wait_ge(sem("glu_made"), 4)
        pe.wait_ge(sem("conv_out"), 4)
        pe.wait_ge(sem("gate_evac"), 4)
        for i in range(NT):
            for h in range(2):
                c = 2 * i + h
                if c >= 4:
                    pe.wait_ge(sem("x2_made"), c - 3)
                for k in range(KT):
                    src = yms if k < 4 else ymp
                    last = mm(B[4 + c % 4][:, :], src[:, k % 4, P * i:P * i + P], wo[k // 4][:, k % 4, 512 * h:512 * h + 512],
                              start=(k == 0), stop=(k == KT - 1))
                last.then_inc(sem("o_done"), 1)
            if i >= 1:
                h2_turn(i - 1)
        def up(it, f, first):
            pe.wait_ge(sem("piece_lo"), 6 * it + 2 * (f + 1))
            for n in range(NB):
                b = NB * f + n
                if first and f == 0:
                    if n == 1:
                        h2_turn(NT - 1)
                    pe.wait_ge(sem("h2_split"), 3 * (n + 1))
                    pe.wait_ge(sem("h2_evac"), 7)
                if not first or b >= 2:
                    pe.wait_ge(sem("silu_made"), 2 * NB * it + b - 1)
                    pe.wait_ge(sem("f_made"), 2 * NB * it + b - 1)
                for e in range(2):
                    for k in range(KT):
                        last = three(B[2 * e + b % 2][:, 0:BW], f13h[f][:, e, k, :], f13l[f][:, e, k, :],
                                     nt_hi[:, k, n * BW:(n + 1) * BW], nt_lo[:, k, n * BW:(n + 1) * BW], k == 0, k == KT - 1)
                    last.then_inc(sem("gate_done" if e == 0 else "up_done"), 1)

        def down(it, first, last_one=False):
            pe.wait_ge(sem("piece_lo"), 6 * it + 6)
            for i in range(NT):
                if last_one and i == 1:
                    pe.wait_ge(sem("f_made"), 2 * NB * NFB)
                    gate_rows(2, 2, B[0:4])
                if i % 3 == 0:
                    pe.wait_ge(sem("f_lo"), 2 * NB * it + NB + i // 3 + 1)
                for h in range(2):
                    c = 2 * i + h
                    if not first or c >= 4:
                        pe.wait_ge(sem("acc_done"), 2 * NT * it + c - 3)
                    for f in range(FB):
                        last = three(B[4 + c % 4][:, :], f_hi[:, f, P * i:P * i + P], f_lo[:, f, P * i:P * i + P],
                                     f2h[:, f, 512 * h:512 * h + 512], f2l[:, f, 512 * h:512 * h + 512], f == 0, f == FB - 1)
                    last.then_inc(sem("down_done"), 1)

        for f in range(FB):
            up(0, f, True)
        down(0, True)
        with pe.Fori(1, NFB - 1) as it:
            for f in range(FB):
                up(it, f, False)
            down(it, False)
        for f in range(FB):
            up(NFB - 1, f, False)
        down(NFB - 1, False, True)

    @block.scalar
    def _(act):
        A_ = nc.scalar.activation

        act.wait_ge(sem("pv_evac"), 2)
        for who, v in enumerate((V_CX, V_CC)):
            A_(condT[:, :, 16 * who:16 * who + 16], view(pv, v, [[1, KT], [0, 16]]), ACT.Silu).then_inc(sem("cond"), 1)
        A_(prm[:, 0, :], pv[:, X_DT:X_DT + Q], ACT.Exp).then_inc(sem("dt"), 1)
        act.wait_ge(sem("lam_dt"), 2)
        A_(prm[:, 3, :], prm[:, 1, :], ACT.Exp).then_inc(sem("polar"), 1)
        act.wait_ge(sem("angles"), 2)
        A_(prm[:, 8, :], prm[:, 5, :], ACT.Sin).then_inc(sem("polar"), 1)
        A_(prm[:, 9, :], prm[:, 7, :], ACT.Sin).then_inc(sem("polar"), 1)

        def mod_row_out(a, bank):
            act.wait_ge(sem("ada_bank"), a + 1)
            A_(arow[a][:, :], bank[:, :], ACT.Copy).then_inc(sem("ada_row"), 1)

        def mod_turn_out(a, bank):
            act.wait_ge(sem("mod_turned"), a + 1)
            A_(view(modc, 32 * a, [[2, 4], [8, 4], [1, 2]]), view(bank, 0, [[P, 4], [32, 4], [16, 2]]), ACT.Copy).then_inc(sem("mod_evac"), 1)

        def square_sums(g):
            for i in XG[g]:
                if i < 8:
                    act.wait_ge(sem("pos_half"), 2 * (i + 1))
                else:
                    act.wait_ge(sem("x8_in"), 16)
                for h in range(2):
                    if 2 * i + h >= 2:
                        act.wait_ge(sem("squares"), 2 * i + h - 1)
                    A_(B[6 + h][:, :], xt[i][:, 512 * h:512 * h + 512], ACT.Square, accum_out=ss[:, 2 * i + h:2 * i + h + 1]).then_inc(sem("squares"), 1)

        def normalise(g):
            i0, i1 = XG[g][0], XG[g][-1] + 1
            act.wait_ge(sem("inverse_ms"), g + 1)
            A_(rstd[:, i0:i1], var[:, i0:i1], ACT.Sqrt).then_inc(sem("rstd"), 1)
            act.wait_ge(sem("rstd"), g + 1)
            for i in XG[g]:
                A_(xt[i][:, :], xt[i][:, :], ACT.Copy, scale=rstd[:, i:i + 1]).then_inc(sem("x_normed"), 1)

        square_sums(0)
        normalise(0)
        act.wait_ge(sem("raws_turned"), 3)
        A_(view(cc, 0, [[1, HD], [HD, Q]]), B[2][:, :], ACT.Copy).then_inc(sem("cc_evac"), 1)
        act.wait_ge(sem("raws_turned"), 4)
        A_(view(cc, Q * HD, [[1, HD], [HD, Q]]), B[3][:, :], ACT.Copy, scale=-1.0).then_inc(sem("cc_evac"), 1)
        square_sums(1)
        mod_row_out(0, B[4])
        normalise(1)
        mod_turn_out(0, B[5])
        act.wait_ge(sem("gsc1"), 1)
        act.wait_ge(sem("mod_evac"), 1)

        def w_high(i):
            act.wait_ge(sem(f"w_in{i % 2}_in"), 16 * (i // 2 + 1))
            if i < 2:
                act.wait_ge(sem("ada_tile"), 8)
            else:
                act.wait_ge(sem("z_done"), NB * (i - 1))
            nc.scalar.copy(w_hi[i % 2][:, :, :], wst[i % 2][:, :, :]).then_inc(sem("w_in_hi"), 1)

        n = 0
        for g, grp in enumerate(XG):
            if g >= 1:
                w_high(g - 1)
            if g == 1:
                square_sums(2)
                normalise(2)
            for k in range(KT):
                act.wait_ge(sem("xT_bank"), n + 1)
                if n >= 2:
                    act.wait_ge(sem("h_split"), n - 1)
                w = P * len(grp)
                who = 0 if g == 2 else 1
                A_(hf[n % 2][:, 0:w], B[n % 4][:, 0:w], ACT.Identity, scale=gsc[:, 0, k, who:who + 1],
                   bias=modc[:, k, who:who + 1]).then_inc(sem("h_evac"), 1)
                n += 1

        def z_out(i):
            for b in range(NB):
                src = B[ZB[b]]
                act.wait_ge(sem("z_done"), NB * i + b + 1)
                if i < 4 and b == 0 and i >= 2:
                    act.wait_ge(sem("z_out"), 16 * (i - 1))
                if i == 4 and b == 0:
                    act.wait_ge(sem("v_done"), 32)
                if i < 4:
                    parts = ((48 * b, 0, 48),) if b < 2 else ((96, 0, 32), (LC + 1, 256, 16))
                    for c0, o, m in parts:
                        last = A_(view(zp[i % 2], c0, [[1, m], [UC, CH]]), src[:, o:o + CH * m], ACT.Copy)
                else:
                    dst, pad = ((pu, PZ), (vp, PAD), (sig, 0))[(i - 4) // 2]
                    fn = ACT.Sigmoid if dst is sig else ACT.Copy
                    parts = ((BW * b, 0, BW),) if b < 2 else ((768, 0, 256), (LAT + pad, 256, CTX))
                    for c0, o, m in parts:
                        last = A_(dst[:, i % 2, pad + c0:pad + c0 + m], src[:, o:o + m], fn)
                last.then_inc(sem("z_evac"), 1)

        def wb_out(j):
            for d in range(2):
                for r in range(2):
                    c = 4 * j + 2 * d + r
                    if c == 0:
                        act.wait_ge(sem("raws_turned"), 4)
                    act.wait_ge(sem("wb_turned"), c + 1)
                    q0 = NPAIR * d + 4 * j
                    A_(wb[:, r, q0:q0 + 4, :], B[c % 2][:, :].rearrange("p (q n) -> p q n", n=P), ACT.Copy).then_inc(sem("wb_evac"), 1)

        def v_out(j):
            for d in range(2):
                for pp in range(4):
                    c = 8 * j + 4 * d + pp
                    q = NPAIR * d + 4 * j + pp
                    act.wait_ge(sem("v_done"), c + 1)
                    if c == 0:
                        for s in range(2):
                            act.wait_ge(sem(f"wc_out{s}"), 64)
                    A_(view(st, q * SLOTS + 1, [[Q * SLOTS, 2], [1, UC]]), view(B[VB[c % 3]], 0, [[UC, 2], [1, UC]]), ACT.Copy).then_inc(sem("v_evac"), 1)

        for i in range(10):
            if i == 4:
                v_out(2)
                v_out(3)
                act.wait_ge(sem("gaps"), 12)
            z_out(i)
            if i < 4:
                wb_out(i)
            if i == 3:
                v_out(0)
                v_out(1)
            if i + 2 < 10:
                w_high(i + 2)
        for n, c in enumerate(KC):
            act.wait_ge(sem("kb_done"), n + 1)
            bank = B[(7, 2)[n % 2]]
            w, o = (P, 7 * HD) if c < 4 else (7 * HD, 0)
            A_(view(kb, 4 * (c % 4) * 15 * HD + o, [[15 * HD, 4], [1, w]], 0, 32), view(bank, 0, [[P, 4], [1, w]], 0, 32), ACT.Copy).then_inc(sem("kb_evac"), 1)
        mod_row_out(1, B[0])
        for j in range(2):
            for b in range(NB):
                n = NB * j + b
                act.wait_ge(sem("pool_done"), n + 1)
                A_(ymp[:, j, b * BW:(b + 1) * BW], B[6 + n % 2][:, 0:BW], ACT.Copy, scale=pv[:, V_PS + j:V_PS + j + 1]).then_inc(sem("pool_evac"), 1)
        mod_turn_out(1, B[1])
        act.wait_ge(sem("fin_turned"), 1)
        for r in range(2):
            A_(fin[:, r, :], B[6][0:Q, P * r:P * r + P], ACT.Copy).then_inc(sem("fin_evac"), 1)
        for c in range(8):
            j = c // 2
            act.wait_ge(sem("y_done"), c + 1)
            if c % 2 == 0 and j >= 2:
                act.wait_ge(sem("y_out"), 128 * (j - 1))
            for par in range(2):
                A_(view(yb[j % 2], (4 * (c % 2) + par) * UC, [[2 * UC, 2], [1, UC]]),
                   view(B[(2, 4)[c % 2] + par], 0, [[UC, 2], [1, UC]]), ACT.Gelu_apprx_tanh).then_inc(sem("y_evac"), 1)
        act.wait_ge(sem("a8_copied"), 3)
        act.wait_ge(sem("wc_made"), 8)
        act.wait_ge(sem("wc_made_dve"), 8)
        mod_row_out(2, B[0])

        def glu_gate(m):
            for b, (c0, n) in enumerate(GB):
                act.wait_ge(sem("glu_done"), NB * m + b + 1)
                if b == 0 and m >= 1:
                    act.wait_ge(sem("glu_made"), m)
                A_(gsig[:, c0:c0 + n], B[(6, 7, 0)[b]][:, 0:n], ACT.Sigmoid, bias=pv[:, V_GB + m:V_GB + m + 1]).then_inc(sem("glu_gate"), 1)

        glu_gate(0)
        mod_turn_out(2, B[1])
        for b in range(NB):
            for j in range(2):
                act.wait_ge(sem("deviation"), 2 * b + j + 1)
                A_(lnw[:, j, 389 * b:389 * b + 389], cacc[:, j, 389 * b:389 * b + 389], ACT.Square).then_inc(sem("dev_squared"), 1)
        glu_gate(1)
        glu_gate(2)
        act.wait_ge(sem("ones"), 2)
        for b in range(NB):
            act.wait_ge(sem("var_done"), b + 1)
            A_(view(sig, 389 * b, [[1, 389]]), B[1 + b][:, 0:389], ACT.Sqrt, bias=eps[:, 0:1]).then_inc(sem("ln_root"), 1)
        glu_gate(3)
        for j in range(2):
            act.wait_ge(sem("ln_scaled"), j + 1)
            for c0, o, m in ((0, 0, LAT), (VCTX, LAT, CTX)):
                A_(ymp[:, 2 + j, o:o + m], cacc[:, j, c0:c0 + m], ACT.Silu, scale=pv[:, V_LG + j:V_LG + j + 1],
                   bias=pv[:, V_LB + j:V_LB + j + 1]).then_inc(sem("conv_out"), 1)
        act.wait_ge(sem("gate_rows"), 1)
        act.wait_ge(sem("conv_out"), 4)
        for who in range(2):
            for h in range(2):
                A_(g1b[:, who, 512 * h:512 * h + 512], B[4 + 2 * who + h][:, :], ACT.Copy).then_inc(sem("gate_evac"), 1)
        def piece_hi(n, c, after=None):
            act.wait_ge(sem(f"piece{c % 3}_in"), piece_count(n, c))
            if after is not None:
                act.wait_ge(*after)
            hi, _, src = piece(c)
            nc.scalar.copy(hi, src).then_inc(sem("piece_hi"), 1)

        def root_ms(scratch, x, s, v, i, n_squares, n_roots):
            A_(scratch[:, :], x[:, :], ACT.Square, accum_out=s[:, i:i + 1]).then_inc(sem("squares"), 1)
            act.wait_ge(sem("squares"), n_squares + i + 1)
            A_(v[:, i:i + 1], s[:, i:i + 1], ACT.Sqrt, scale=1.0 / D, bias=eps[:, 0:1]).then_inc(sem("rstd"), 1)

        act.wait_ge(sem("ones"), 2)
        for i in range(NT):
            who = 0 if i == 8 else 1
            if i >= 1:
                act.wait_ge(sem("h2_turned"), i)
            if i == NT - 1:
                act.wait_ge(sem("o_done"), 2 * NT)
                piece_hi(0, 0)
                piece_hi(1, 1)
            act.wait_ge(sem("x2_made"), 2 * i + 2)
            root_ms(xn2, xr[i % 3], ss2, var2, i, 2 * NT, 3)
            act.wait_ge(sem("inverse_ms"), 3 + i + 1)
            A_(xn2[:, :], xr[i % 3][:, :], ACT.Copy, scale=rstd2[:, i:i + 1]).then_inc(sem("x2_normed"), 1)
            act.wait_ge(sem("h2_turned"), i + 1)
            if i >= 1:
                act.wait_ge(sem("h2_split"), i)
            for k in range(KT):
                last = A_(h2f[:, k, :], B[TB[i] + k // 4][:, P * (k % 4):P * (k % 4) + P], ACT.Identity,
                          scale=gsc[:, 1, k, who:who + 1], bias=modc[:, 24 + k, who:who + 1])
            last.then_inc(sem("h2_evac"), 1)


        def hidden(it, f, first):
            for n in range(NB):
                b = NB * f + n
                g = 2 * NB * it + b
                act.wait_ge(sem("gate_done"), g + 1)
                if not first or b >= 2:
                    act.wait_ge(sem("f_made"), g - 1)
                A_(sa[b % 2][:, :], B[b % 2][:, 0:BW], ACT.Silu).then_inc(sem("silu_made"), 1)
                act.wait_ge(sem("f_made"), g + 1)
                if not first:
                    act.wait_ge(sem("down_done"), 2 * NT * (it - 1) + 6 * (n + 1))
                nc.scalar.copy(f_hi[:, f, n * BW:(n + 1) * BW], fv[b % 2][:, :]).then_inc(sem("f_hi"), 1)

        def iteration(it, first, last):
            n0 = 4 + 6 * it
            for f in range(FB):
                piece_hi(n0 + f, 4 + f, None if first else (sem("down_done"), 2 * NT * it))
            for f in range(FB):
                hidden(it, f, first)
                if not last:
                    for e in range(2):
                        piece_hi(n0 + 2 + 2 * f + e, 6 + 2 * f + e, (sem("up_done"), 2 * NB * it + NB * (f + 1)))

        for n in range(2, 4):
            piece_hi(n, n)
        iteration(0, True, False)
        with act.Fori(1, NFB - 1) as it:
            iteration(it, False, False)
        iteration(NFB - 1, False, True)
        act.wait_ge(sem("gate_rows"), 2)
        for who in range(2):
            for h in range(2):
                A_(g2b[:, who, 512 * h:512 * h + 512], B[2 * who + h][:, :], ACT.Copy).then_inc(sem("gate_evac"), 1)
        for i in range(NT):
            act.wait_ge(sem("end_sum"), i + 1)
            root_ms(sq, xe[i], ss, var, i, 3 * NT, 3 + NT)
            act.wait_ge(sem("inverse_ms"), 3 + NT + i + 1)
            A_(xe[i][:, :], xe[i][:, :], ACT.Copy, scale=rstd[:, i:i + 1]).then_inc(sem("end_normed"), 1)

    @block.vector
    def _(dve):
        TT, TS, STT = nc.vector.tensor_tensor, nc.vector.tensor_scalar, nc.vector.scalar_tensor_tensor
        steps = [0]

        def step(ins):
            steps[0] += 1
            ins.then_inc(sem("dve_step"), 1)
            dve.wait_ge(sem("dve_step"), steps[0])

        dve.wait_ge(sem("log_dt_in"), 16)
        nc.vector.tensor_copy(view(rlam, 4 * P, [[NS, 2], [1, NS]], 0, Q), view(ldt, 0, [[1, 2], [0, NS]], 0, Q)).then_inc(sem("dt_rows"), 1)
        dve.wait_ge(sem("params_turned"), 1)
        nc.vector.tensor_copy(pv[:, :], B[6][:, 0:NPV]).then_inc(sem("pv_evac"), 1)
        nc.vector.tensor_copy(dcol[:, :], B[7][0:32, 0:NPAIR]).then_inc(sem("pv_evac"), 1)
        dve.wait_ge(sem("pv_evac"), 2)
        lre, lim = pv[:, X_LRE:X_LRE + Q], pv[:, X_LIM:X_LIM + Q]
        p_ = lambda i: prm[:, i, :]
        dve.wait_ge(sem("dt"), 1)
        TT(p_(1), lre, p_(0), ALU.mult).then_inc(sem("lam_dt"), 1)
        TT(p_(2), lim, p_(0), ALU.mult).then_inc(sem("lam_dt"), 1)
        dve.wait_ge(sem("lam_dt"), 2)
        for a, b, turn in ((4, 5, 0.0), (6, 7, 0.25)):
            step(TS(p_(a), p_(2), 1.0 / TWO_PI, turn, ALU.mult, ALU.add))
            step(TS(p_(a), p_(a), ROUND, None, ALU.add))
            step(TS(p_(a), p_(a), ROUND, None, ALU.subtract))
            step(STT(p_(b), p_(a), -TP1, p_(2), ALU.mult, ALU.add))
            step(STT(p_(b), p_(a), -TP2, p_(b), ALU.mult, ALU.add))
            step(STT(p_(b), p_(a), -TP3, p_(b), ALU.mult, ALU.add))
            if turn:
                step(TS(p_(b), p_(b), TWO_PI / 4, None, ALU.add))
            TS(p_(b), p_(b), 3.1415925, -3.1415925, ALU.min, ALU.max).then_inc(sem("angles"), 1)
        step(nc.vector.memset(powr[:, 0, :], 1.0))
        step(nc.vector.memset(powi[:, 0, :], 0.0))
        dve.wait_ge(sem("polar"), 3)
        TT(powr[:, 1, :], p_(3), p_(9), ALU.mult)
        step(TT(powi[:, 1, :], p_(3), p_(8), ALU.mult))
        step(TT(p_(10), lre, lre, ALU.mult))
        step(TT(p_(11), lim, lim, ALU.mult))
        step(TT(p_(10), p_(10), p_(11), ALU.add))
        step(nc.vector.reciprocal(p_(10), p_(10)))
        step(TS(p_(11), powr[:, 1, :], -1.0, None, ALU.add))
        step(TT(p_(12), p_(11), lre, ALU.mult))
        step(TT(p_(14), powi[:, 1, :], lim, ALU.mult))
        step(TT(p_(12), p_(12), p_(14), ALU.add))
        step(TT(p_(12), p_(12), p_(10), ALU.mult))
        step(TT(p_(13), powi[:, 1, :], lre, ALU.mult))
        step(TT(p_(14), p_(11), lim, ALU.mult))
        step(TT(p_(13), p_(13), p_(14), ALU.subtract))
        step(TT(p_(13), p_(13), p_(10), ALU.mult))
        for lo, n in ((1, 1), (2, 2), (4, 4)):
            br, bi = view(powr, lo * Q, [[0, n], [1, Q]]), view(powi, lo * Q, [[0, n], [1, Q]])
            sr, si = powr[:, 1:1 + n, :], powi[:, 1:1 + n, :]
            t0, t1 = wbt_tmp[0][:, 0:n, 0:Q], wbt_tmp[1][:, 0:n, 0:Q]
            dr, di = powr[:, lo + 1:lo + 1 + n, :], powi[:, lo + 1:lo + 1 + n, :]
            step(TT(t0, br, sr, ALU.mult))
            step(TT(t1, bi, si, ALU.mult))
            step(TT(dr, t0, t1, ALU.subtract))
            step(TT(t0, br, si, ALU.mult))
            step(TT(t1, bi, sr, ALU.mult))
            step(TT(di, t0, t1, ALU.add))
        dve.sem_inc(sem("powers"), 1)
        def inverse_ms(s, v, i0, i1, name, ready, count):
            dve.wait_ge(sem(ready), count)
            n = i1 - i0
            step(TT(v[:, i0:i1], view(s, 2 * i0, [[2, n]]), view(s, 2 * i0 + 1, [[2, n]]), ALU.add))
            step(TS(v[:, i0:i1], v[:, i0:i1], 1.0 / D, EPS, ALU.mult, ALU.add))
            nc.vector.reciprocal(v[:, i0:i1], v[:, i0:i1]).then_inc(sem(name), 1)

        inverse_ms(ss, var, XG[0][0], XG[0][-1] + 1, "inverse_ms", "squares", 2 * (XG[0][-1] + 1))
        dve.wait_ge(sem("raws_turned"), 2)
        qre, qim = view(prm, 12 * Q, [[0, HD], [1, Q]]), view(prm, 13 * Q, [[0, HD], [1, Q]])
        bank = lambda b: B[b][:, :].rearrange("p (h q) -> p h q", q=Q)
        bout = lambda r: view(bb, r * Q * HD, [[1, HD], [HD, Q]])
        tv = [view(wbt_tmp[i], 0, [[1, HD], [HD, Q]]) for i in range(2)]
        step(TT(bout(0), bank(0), qre, ALU.mult))
        step(TT(tv[0], bank(1), qim, ALU.mult))
        step(TT(bout(1), bank(1), qre, ALU.mult))
        step(TT(tv[1], bank(0), qim, ALU.mult))
        TT(bout(0), bout(0), tv[0], ALU.subtract).then_inc(sem("bb_made"), 1)
        TT(bout(1), bout(1), tv[1], ALU.add).then_inc(sem("bb_made"), 1)
        dve.wait_ge(sem("ident"), 1)
        step(TT(dsel[:, 0, :], ident[0:32, 0:16], ident[0:32, 16:32], ALU.add))
        step(nc.vector.tensor_copy(view(dsel, HD, [[HD, NPAIR - 1], [1, HD]], 0, 32), view(dsel, 0, [[0, NPAIR - 1], [1, HD]], 0, 32)))
        TT(dsel[:, :, :], dsel[:, :, :], view(dcol, 0, [[1, NPAIR], [0, HD]], 0, 32), ALU.mult).then_inc(sem("dsel"), 1)


        dve.wait_ge(sem("cc_evac"), 2)
        dve.wait_ge(sem("raws_turned"), 4)
        for n in range(4):
            lr, li, cr, ci, v3 = wc_views(n)
            slot, tmp = wcd[n], wcd_tmp
            TT(v3(slot[0]), lr, cr, ALU.mult)
            step(TT(v3(tmp[0]), li, ci, ALU.mult))
            TT(v3(slot[1]), lr, ci, ALU.mult)
            step(TT(v3(tmp[1]), li, cr, ALU.mult))
            TT(slot[0][:, :, :], slot[0][:, :, :], tmp[0][:, :, :], ALU.add).then_inc(sem("wc_made_dve"), 1)
            TT(slot[1][:, :, :], slot[1][:, :, :], tmp[1][:, :, :], ALU.subtract).then_inc(sem("wc_made_dve"), 1)
            dve.wait_ge(sem("wc_made_dve"), 2 * (n + 1))

        def w_low(i):
            dve.wait_ge(sem("w_in_hi"), i + 1)
            TT(w_lo[i % 2][:, :, :], wst[i % 2][:, :, :], w_hi[i % 2][:, :, :].bitcast(F32), ALU.subtract).then_inc(low_ready(i)[0], 1)

        inverse_ms(ss, var, XG[1][0], XG[1][-1] + 1, "inverse_ms", "squares", 2 * (XG[1][-1] + 1))
        dve.wait_ge(sem("mod_evac"), 1)
        STT(gsc[:, 0, :, :], modc[:, 8:16, :], 1.0, view(pv, V_N1, [[1, KT], [0, 2]]), ALU.add, ALU.mult).then_inc(sem("gsc1"), 1)
        dve.wait_ge(sem("wc_out2"), 128)
        n = 0
        for g, grp in enumerate(XG):
            if g >= 1:
                w_low(g - 1)
            if g == 1:
                inverse_ms(ss, var, XG[2][0], XG[2][-1] + 1, "inverse_ms", "squares", 2 * (XG[2][-1] + 1))
            for k in range(KT):
                w = P * len(grp)
                c0 = P * grp[0]
                dve.wait_ge(sem("h_evac"), n + 1)
                hi, lo = nt_hi[:, k, c0:c0 + w], nt_lo[:, k, c0:c0 + w]
                nc.vector.tensor_copy(hi, hf[n % 2][:, 0:w]).then_inc(sem("h_hi"), 1)
                dve.wait_ge(sem("h_hi"), n + 1)
                TT(lo, hf[n % 2][:, 0:w], hi.bitcast(F32), ALU.subtract).then_inc(sem("h_split"), 1)
                n += 1

        def wbt_piece(j, d):
            n = 2 * j + d
            q0 = NPAIR * d + 4 * j
            step_, base = (-Q, (CH - 1) * Q) if d == 0 else (Q, 0)
            lr = view(powr, base + q0, [[1, 4], [step_, CH], [0, HD]])
            li = view(powi, base + q0, [[1, 4], [step_, CH], [0, HD]])
            br = view(bb, q0 * HD, [[HD, 4], [0, CH], [1, HD]])
            bi = view(bb, (Q + q0) * HD, [[HD, 4], [0, CH], [1, HD]])
            v3 = lambda t: view(t, 0, [[P, 4], [HD, CH], [1, HD]])
            out, tmp = wbt[d], wbt_tmp
            if n == 0:
                dve.wait_ge(sem("bb_made"), 2)
            if j >= 1:
                dve.wait_ge(sem("wb_turned"), 4 * (j - 1) + 2 * d + 2)
            if n >= 1:
                dve.wait_ge(sem("wbt_made"), 2 * n)
            TT(v3(out[0]), lr, br, ALU.mult).then_inc(sem("wbt_terms"), 1)
            TT(v3(tmp[0]), li, bi, ALU.mult).then_inc(sem("wbt_terms"), 1)
            TT(v3(out[1]), lr, bi, ALU.mult).then_inc(sem("wbt_terms"), 1)
            TT(v3(tmp[1]), li, br, ALU.mult).then_inc(sem("wbt_terms"), 1)
            dve.wait_ge(sem("wbt_terms"), 4 * n + 2)
            TT(out[0][:, :, :], out[0][:, :, :], tmp[0][:, :, :], ALU.subtract).then_inc(sem("wbt_made"), 1)
            dve.wait_ge(sem("wbt_terms"), 4 * n + 4)
            TT(out[1][:, :, :], out[1][:, :, :], tmp[1][:, :, :], ALU.add).then_inc(sem("wbt_made"), 1)

        for j in range(4):
            wbt_piece(j, 0)
            wbt_piece(j, 1)
            w_low(j + 2)
        dve.wait_ge(sem("wbt_made"), 16)
        nc.vector.tensor_copy(a8r[:, :], powr[:, CH, :]).then_inc(sem("a8_copied"), 1)
        TS(a8i[:, 0, :], powi[:, CH, :], -1.0, None, ALU.mult).then_inc(sem("a8_copied"), 1)
        nc.vector.tensor_copy(a8i[:, 1, :], powi[:, CH, :]).then_inc(sem("a8_copied"), 1)
        dve.wait_ge(sem("a8_copied"), 3)
        dve.wait_ge(sem("v_evac"), 32)
        for r, x in enumerate((X_HRE, X_HIM)):
            nc.vector.tensor_copy(view(st, r * Q * SLOTS, [[SLOTS, NPAIR]]), pv[:, x:x + NPAIR]).then_inc(sem("h0"), 1)
            nc.vector.tensor_copy(view(st, (r * Q + NPAIR) * SLOTS + BSH, [[SLOTS, NPAIR]]), pv[:, x + NPAIR:x + Q]).then_inc(sem("h0"), 1)
            nc.vector.memset(view(st, (r * Q + NPAIR) * SLOTS, [[SLOTS, NPAIR]]), 0.0).then_inc(sem("h0"), 1)
        dve.wait_ge(sem("h0"), 6)
        DL = NPAIR * SLOTS + BSH
        DC = NPAIR * SLOTS - (LC + 1)
        count = [0]

        def state(base, dstep, k, flip=False):
            rs = -Q * SLOTS if flip else Q * SLOTS
            return view(st, base + k + (Q * SLOTS if flip else 0), [[rs, 2], [dstep, 2], [SLOTS, NPAIR]])

        ar = view(a8r, 0, [[0, 2], [NPAIR, 2], [1, NPAIR]])
        ai = view(a8i, 0, [[Q, 2], [NPAIR, 2], [1, NPAIR]])
        tt = lambda t, i: view(t, i * 2 * Q, [[Q, 2], [NPAIR, 2], [1, NPAIR]])

        def scan_step(chains):
            for name, t, base, dstep, k in chains:
                TT(tt(t, 0), ar, state(base, dstep, k), ALU.mult).then_inc(sem(name), 1)
                TT(tt(t, 1), ai, state(base, dstep, k, True), ALU.mult).then_inc(sem(name), 1)
            for name, t, base, dstep, k in chains:
                dve.wait_ge(sem(name), 4 * k + 1)
                TT(tt(t, 2), tt(t, 0), state(base, dstep, k + 1), ALU.add).then_inc(sem(name), 1)
            for name, t, base, dstep, k in chains:
                dve.wait_ge(sem(name), 4 * k + 3)
                TT(state(base, dstep, k + 1), tt(t, 2), tt(t, 1), ALU.add).then_inc(sem(name), 1)
            for name, t, base, dstep, k in chains:
                dve.wait_ge(sem(name), 4 * k + 4)

        for k in range(LC):
            chains = [("latent_step", scT, 0, DL, k)]
            if k < CC:
                chains.append(("context_step", scC, LC + 1, DC, k))
            scan_step(chains)
        nc.vector.tensor_copy(tt(scT, 0), state(UC, NPAIR * SLOTS - LC - 1, 0)).then_inc(sem("scan_done"), 1)

        dve.wait_ge(sem("gated"), 4)
        for tap in range(TAPS):
            for j in range(2):
                w = pv[:, X_TAP + 2 * tap + j:X_TAP + 2 * tap + j + 1]
                src = vp[:, j, tap:tap + VO]
                if tap == 0:
                    TS(cacc[:, j, :], src, w, pv[:, V_CB + j:V_CB + j + 1], ALU.mult, ALU.add).then_inc(sem("tap_done"), 1)
                else:
                    dve.wait_ge(sem("tap_done"), 2 * tap + j - 1)
                    STT(cacc[:, j, :], src, w, cacc[:, j, :], ALU.mult, ALU.add).then_inc(sem("tap_done" if tap < TAPS - 1 else "conv_made"), 1)
        def glu_out(m):
            dve.wait_ge(sem("glu_gate"), NB * (m + 1))
            for c0, o, n in ((0, 0, LC), (LC + 1, LAT, CC)):
                last = TT(view(yms, m * T + o, [[1, CH], [CH, n]]), view(yT, m * CH * UC + c0, [[UC, CH], [1, n]]),
                          view(gsig, c0, [[UC, CH], [1, n]]), ALU.mult)
            last.then_inc(sem("glu_made"), 1)

        glu_out(0)
        dve.wait_ge(sem("conv_made"), 2)
        for b in range(NB):
            dve.wait_ge(sem("mean_done"), b + 1)
            for j in range(2):
                TT(cacc[:, j, 389 * b:389 * b + 389], cacc[:, j, 389 * b:389 * b + 389], B[1 + b][:, 0:389], ALU.subtract).then_inc(sem("deviation"), 1)
        glu_out(1)
        glu_out(2)
        dve.wait_ge(sem("deviation"), 6)
        for b in range(NB):
            dve.wait_ge(sem("ln_root"), b + 1)
            step(nc.vector.reciprocal(view(sig, 389 * b, [[1, 389]]), view(sig, 389 * b, [[1, 389]])))
        for j in range(2):
            TT(cacc[:, j, :], cacc[:, j, :], view(sig, 0, [[1, VO]]), ALU.mult).then_inc(sem("ln_scaled"), 1)
        glu_out(3)
        dve.wait_ge(sem("mod_evac"), 3)
        STT(gsc[:, 1, :, :], modc[:, 32:40, :], 1.0, view(pv, V_N2, [[1, KT], [0, 2]]), ALU.add, ALU.mult).then_inc(sem("gsc2"), 1)
        dve.wait_ge(sem("gate_evac"), 4)
        dve.wait_ge(sem("ln_scaled"), 2)

        def inverse_root(r, v, i, n_roots):
            dve.wait_ge(sem("rstd"), n_roots + i + 1)
            nc.vector.reciprocal(r[:, i:i + 1], v[:, i:i + 1]).then_inc(sem("inverse_ms"), 1)

        def h2_split(i):
            dve.wait_ge(sem("h2_evac"), i + 1)
            hi, lo = nt_hi[:, :, P * i:P * i + P], nt_lo[:, :, P * i:P * i + P]
            nc.vector.tensor_copy(hi, h2f[:, :, :]).then_inc(sem("h2_hi"), 1)
            dve.wait_ge(sem("h2_hi"), i + 1)
            TT(lo, h2f[:, :, :], hi.bitcast(F32), ALU.subtract).then_inc(sem("h2_split"), 1)

        for i in range(NT):
            who = 0 if i == 8 else 1
            if i < 8:
                dve.wait_ge(sem("pos_half"), 2 * (8 + i + 1))
            else:
                dve.wait_ge(sem("xr2_in"), 48)
            for h in range(2):
                c = 2 * i + h
                dve.wait_ge(sem("o_done"), c + 1)
                if c >= 1:
                    dve.wait_ge(sem("x2_made"), c)
                step(TT(tg[:, :], B[4 + c % 4][:, :], g1b[:, who, 512 * h:512 * h + 512], ALU.mult))
                TT(xr[i % 3][:, 512 * h:512 * h + 512], xr[i % 3][:, 512 * h:512 * h + 512], tg[:, :], ALU.add).then_inc(sem("x2_made"), 1)
            inverse_root(rstd2, var2, i, 3)
            if i >= 1:
                h2_split(i - 1)
        h2_split(NT - 1)

        def hidden(it, first):
            for f in range(FB):
                for n in range(NB):
                    b = NB * f + n
                    g = 2 * NB * it + b
                    dve.wait_ge(sem("silu_made"), g + 1)
                    dve.wait_ge(sem("up_done"), g + 1)
                    if not first or b >= 2:
                        dve.wait_ge(sem("f_lo"), g - 1)
                    TT(fv[b % 2][:, :], sa[b % 2][:, :], B[2 + b % 2][:, 0:BW], ALU.mult).then_inc(sem("f_made"), 1)

        def gather(it, first):
            if first:
                for s in range(3):
                    dve.wait_ge(sem(f"tile_out{s}"), 48)
            if not first:
                dve.wait_ge(sem("acc_done"), 2 * NT * it)
            for c in range(2 * NT):
                a = acc[:, c // 2, 512 * (c % 2):512 * (c % 2) + 512]
                dve.wait_ge(sem("down_done"), 2 * NT * it + c + 1)
                if first:
                    nc.vector.tensor_copy(a, B[4 + c % 4][:, :]).then_inc(sem("acc_done"), 1)
                else:
                    TT(a, a, B[4 + c % 4][:, :], ALU.add).then_inc(sem("acc_done"), 1)

        hidden(0, True)
        gather(0, True)
        with dve.Fori(1, NFB - 1) as it:
            hidden(it, False)
            gather(it, False)
        hidden(NFB - 1, False)
        dve.wait_ge(sem("acc_done"), 2 * NT * (NFB - 1))
        for i in range(NT):
            who = 0 if i == 8 else 1
            for h in range(2):
                c = 2 * i + h
                dve.wait_ge(sem("down_done"), 2 * NT * (NFB - 1) + c + 1)
                a = acc[:, i, 512 * h:512 * h + 512]
                TT(a, a, B[4 + c % 4][:, :], ALU.add).then_inc(sem("acc_done"), 1)
            if i == 0:
                dve.wait_ge(sem("gate_evac"), 8)
            dve.wait_ge(sem("acc_done"), 2 * NT * (NFB - 1) + 2 * i + 2)
            if i >= 2:
                dve.wait_ge(sem("end_sum"), i - 1)
            step(TT(te[i % 2][:, :], acc[:, i, :], g2b[:, who, :], ALU.mult))
            dve.wait_ge(sem(f"x{i}_in"), 48 if i < 8 else 32)
            TT(xe[i][:, :], xe[i][:, :], te[i % 2][:, :], ALU.add).then_inc(sem("end_sum"), 1)
            if i >= 1:
                inverse_root(rstd, var, i - 1, 3 + NT)
        inverse_root(rstd, var, NT - 1, 3 + NT)

    ctx.close()


_INS = ['x_prompt', 'x_sample', 'state_ssm_re', 'state_ssm_im', 'c', 'c_ctx', 'ada_w', 'ada_b', 'norm1_g', 'w_in',
        'ssm_lam_re', 'ssm_lam_im', 'ssm_log_dt', 'ssm_b_re', 'ssm_b_im', 'ssm_c_re', 'ssm_c_im', 'ssm_d',
        'ssm_w_glu', 'ssm_b_glu', 'pool_w', 'pool_scale', 'conv_dw_w', 'conv_dw_b', 'conv_ln_g', 'conv_ln_b',
        'w_out', 'norm2_g', 'ffn_w1', 'ffn_w3', 'ffn_w2', 'final_g']
_OUTS = [(1, 128, 1024), (1, 1024, 1024), (1, 1, 2, 32, 64), (1, 1, 2, 32, 64)]


def shape_constants():
    quarter = D // 4
    omega = (1.0 / (10000.0 ** (np.arange(quarter, dtype=np.float32) / np.float32(quarter)))).astype(np.float32)

    def waves(n):
        a = np.arange(n, dtype=np.float32)[:, None] * omega[None]
        return np.concatenate([np.sin(a), np.cos(a)], axis=1).astype(np.float32)

    edges = np.ones((P, 34), np.float32)
    for g, w in enumerate((2, 4, 8, 16)):
        p0, j = 64 * (g % 2), g // 2
        edges[p0:p0 + 64, j] = 1.0 / w
        for i in range(8):
            edges[p0:p0 + 64, 2 + 16 * j + i] = w / (min(i + w // 2, LAT) - max(i - w // 2, 0))
            t = LAT - 8 + i
            edges[p0:p0 + 64, 2 + 16 * j + 8 + i] = w / (min(t + w // 2, LAT) - max(t - w // 2, 0))
    return {"pos_rows": waves(LAT // GRID_W), "pos_cols": waves(GRID_W), "pool_edges": edges}


def kernel(**inputs):
    import concourse.bacc as bacc
    from concourse.bass_utils import run_bass_kernel_spmd

    nc = bacc.Bacc("TRN2", target_bir_lowering=False, num_devices=1)
    arrays = {name: np.ascontiguousarray(inputs[name]) for name in _INS}
    arrays.update(shape_constants())
    ins = {name: nc.dram_tensor(f"in_{name}", a.shape, mybir.dt.from_np(a.dtype), kind="ExternalInput").ap() for name, a in arrays.items()}
    outs = [nc.dram_tensor(f"out_{i}", shape, F32, kind="ExternalOutput").ap() for i, shape in enumerate(_OUTS)]
    build(nc, ins, outs)
    r = run_bass_kernel_spmd(nc, [{f"in_{name}": a for name, a in arrays.items()}], core_ids=[0])
    return tuple(r.results[0][f"out_{i}"] for i in range(len(_OUTS)))
```

```python
from contextlib import ExitStack

import numpy as np
import concourse.bass as bass
from concourse import mybir

F32 = mybir.dt.float32
F32R = mybir.dt.float32r
ACT = mybir.ActivationFunctionType
ALU = mybir.AluOpType

P = 128
D = 1024
KT = D // P
LAT, CTX = 1024, 128
T = LAT + CTX
NB, BW = 3, 384
NT = T // P
GRID_W = 64
D_IN = 1280
DFF = 2816
EPS = 1e-6

CH = 8
G, NS, HD = 32, 64, 16
Q = G
NPAIR = G // 2
LC, CC = LAT // CH, CTX // CH
UC = LC + 1 + CC
SLOTS = UC + 1
BSH = CC + 1
NPOW = CH + 1

POOL_LOW = 6
FB = 2
NFB = DFF // P // FB
TWO_PI = 6.283185307179586
TP1 = 6.28125
TP2 = float(np.float32(TWO_PI - TP1))
TP3 = float(TWO_PI - TP1 - np.float32(TWO_PI - TP1))
ROUND = 12582912.0

V_N1, V_N2, V_GB, V_PS, V_CB, V_LG, V_LB, V_CX, V_CC = 0, 8, 16, 20, 22, 24, 26, 28, 36
VR = 44
TAPS = 31
PAD = TAPS // 2
VL = PAD + LAT + PAD + CTX + PAD
VO = LAT + PAD + CTX
VCTX = LAT + PAD
PZ = 8
PL = PZ + LAT + PZ + CTX + PZ


def view(t, off, dims, p0=0, n=P):
    full = t[:]
    ps = full.ap[0][0]
    return bass.AP(tensor=full.tensor, offset=full.offset + p0 * ps + off, ap=[[ps, n]] + [list(d) for d in dims])


def dview(ap, off, dims):
    return bass.AP(tensor=ap.tensor, offset=ap.offset + off, ap=[list(d) for d in dims])


def build(nc, A, O):
    ctx = ExitStack()

    def at(name, shape, off, dt=F32):
        n = int(np.prod(shape[1:])) * 4
        assert off % 32 == 0 and off + n <= LIMIT, (name, off + n)
        return nc.alloc_sbuf_tensor_at(name, shape, dt, offset=off)

    LIMIT = 229368
    O_NT = 16512
    O_WB = O_NT + 2 * KT * T * 4
    O_UZ = O_WB + 2 * Q * P * 4
    O_ST = O_UZ + 18560
    O_WS = O_ST + 2 * Q * SLOTS * 4
    O_BC = O_WS + 24576
    O_C = O_BC + 16384

    cur = [O_C]

    def const(name, shape, dt=F32):
        n = int(np.prod(shape[1:])) * 4
        t = at(name, shape, cur[0], dt)
        cur[0] += (n + 31) // 32 * 32
        return t

    ident = const("ident", [P, P])
    onesm = const("onesm", [P, P])
    X_TAP = VR
    X_LRE, X_LIM, X_HRE, X_HIM, X_DT = (VR + 2 * TAPS + Q * i for i in range(5))
    NPV = VR + 2 * TAPS + 5 * Q
    pv = const("pv", [P, NPV])
    dcol = const("dcol", [32, NPAIR])
    condT = const("condT", [P, KT, 32])
    modc = const("modc", [P, 48, 2])
    gsc = const("gsc", [P, 2, KT, 2])
    O_POW = cur[0]
    powr = const("powr", [P, NPOW, Q])
    powi = const("powi", [P, NPOW, Q])
    a8i = const("a8i", [P, 2, Q])
    ss = const("ss", [P, 2 * NT])
    rstd = const("rstd", [P, NT])
    ss2 = const("ss2", [P, 2 * NT])
    rstd2 = const("rstd2", [P, NT])
    var = const("var", [P, NT])
    var2 = const("var2", [P, NT])
    edge = const("edge", [P, 34])
    scT = const("scT", [P, 3, 2, Q])
    eps = const("eps", [P, 1])
    dsel = const("dsel", [32, NPAIR, HD])
    a8r = const("a8r", [P, Q])

    nt_hi = at("nt_hi", [P, KT, T], O_NT, F32R)
    nt_lo = at("nt_lo", [P, KT, T], O_NT + KT * T * 4, F32R)
    raw = [at(f"raw{i}", [32, 2 * HD * NS], O_NT + 40960 + i * 8192) for i in range(4)]
    xt = [at(f"xt{i}", [P, D], (O_UZ if i < 4 else O_WB - 16384) + i * 4096) for i in range(NT)]
    posc = at("posc", [P, 512], O_UZ + 16384)
    posr = [at(f"posr{i}", [P, 512], (O_WB + 20480 if i < 6 else O_BC + 8192 - 12288) + i * 2048) for i in range(8)]
    o = O_ST
    wbt_tmp = [at(f"wbt_tmp{i}", [P, 4, P], o + 2048 * i) for i in range(2)]
    o += 4096
    wbt = [[at(f"wbt{s}{r}", [P, 4, P], o + 2048 * (2 * s + r)) for r in range(2)] for s in range(2)]
    o += 8192
    NC = NPOW * HD
    wct_tmp = [at(f"wct_tmp{i}", [P, 4, NC], o + 2304 * i) for i in range(2)]
    o += 4608
    wct = [[at(f"wct{s}{r}", [P, 4, NC], o + 2304 * (2 * s + r)) for r in range(2)] for s in range(2)]
    o += 9216
    wcd = [[at(f"wcd{n}{r}", [P, 4, NC], O_NT + 40960 + 2304 * (2 * n + r)) for r in range(2)] for n in range(4)]
    wcd_tmp = [at(f"wcd_tmp{i}", [P, 4, NC], O_NT + 40960 + 2304 * (8 + i)) for i in range(2)]
    prm = at("prm", [P, 16, Q], o)
    o += 2048
    hf = [at(f"hf{i}", [P, 512], (o, o + 2048, O_UZ + 16384)[i]) for i in range(3)]
    o += 4096
    arow = [at("arow0", [P, 512], o), at("arow1", [P, 512], O_WS + 20480), at("arow2", [P, 512], O_POW)]
    abias = [at("abias0", [P, 512], o + 2048)] + [at("abias1", [P, 512], O_WS + 18432)] * 2
    o += 4096
    assert o <= O_WS
    o = O_BC + 12288
    rows = at("rows", [VR, P], o)
    rtap = at("rtap", [2 * TAPS, P], o + 512)
    rlam = at("rlam", [Q, 5, P], o + 1024)
    dn = at("dn", [NPAIR, 2 * HD], o + 3584)
    ldt = at("ldt", [Q, 2], o + 3712)
    assert o + 3744 <= O_C
    wb = at("wb", [P, 2, Q, P], O_WB)
    u8 = [at(f"u8{i}", [P, 8, UC], O_UZ + 4640 * i) for i in range(2)]
    zp = [at(f"zp{i}", [P, CH, UC], O_UZ + 9280 + 4640 * i) for i in range(2)]
    st = at("st", [P, 2 * Q * SLOTS], O_ST)
    wst = [at(f"wst{i}", [P, KT, P], O_WS + 4096 * i) for i in range(2)]
    w_hi = [at(f"w_hi{i}", [P, KT, P], O_WS + 8192 + 8192 * i, F32R) for i in range(2)]
    w_lo = [at(f"w_lo{i}", [P, KT, P], O_WS + 12288 + 8192 * i, F32R) for i in range(2)]
    ad0 = [at(f"ad0{i}", [P, 2048], O_WS + 8192 + 8192 * i) for i in range(2)]
    bb = at("bb", [P, 2, Q, HD], O_BC)
    cc = at("cc", [P, 2, Q, HD], O_BC + 4096)
    bblk = at("bblk", [P, 2, Q, 32], O_BC + 8192)
    pu = at("pu", [P, 2, PL], O_WB)
    psum_w = at("psum_w", [P, 2, PL], O_WB + 9408)
    vp = at("vp", [P, 2, VL], O_WB + 18816)
    cacc = at("cacc", [P, 2, VO], O_UZ)
    sig = at("sig", [P, 2, T], O_UZ + 9344)
    wpool = at("wpool", [P, 2, P], O_WB + 28416)
    fin = at("fin", [Q, 2, P], O_WB + 29440)
    scC = at("scC", [P, 3, 2, Q], O_WB + 30464)
    u9 = [at(f"u9{i}", [P, 8, UC], O_WB + 9408 + 4640 * i) for i in range(2)]
    wc = at("wc", [P, 2, Q, NC], O_NT)
    toep = at("toep", [P, G, P], O_NT + 36864)
    kb = at("kb", [32, NPAIR, 15 * HD], O_NT + 53248)
    ad1 = [at(f"ad1{i}", [P, 2048], (O_BC, O_WS + 9216, O_BC + 8192)[i]) for i in range(3)]
    yT = at("yT", [P, 4, CH * UC], O_NT + 53248)
    yb = [at(f"yb{i}", [P, 8, UC], O_WB + 4640 * i) for i in range(2)]
    ymp = at("ymp", [P, 2, T], O_WS)
    wglu = at("wglu", [P, 4, 512], O_WB)
    gsig = at("gsig", [P, CH * UC], O_WB + 8192)
    ym = [at("ym0", [P, T], O_WB + 12832), at("ym1", [P, T], O_ST + 32768)]
    Y_SLOT = ((4, 5), (6, 7), (12, 13), (14, 15), (0, 1), (2, 3), (8, 9), (10, 11))
    y_hi, y_lo = ([at(f"y{e}_{k}", [P, T], O_NT + 4 * T * Y_SLOT[k][e], F32R) for k in range(KT)] for e in range(2))
    O_OUT = [O_ST + 8192 * k for k in range(4)] + [O_WS, O_WS + 8192, O_BC, O_BC + 8192]
    wo_hi, wo_lo = ([at(f"wo{e}_{k}", [P, D], O_OUT[k] + 4096 * e, F32R) for k in range(KT)] for e in range(2))
    wos = [at("wos0", [P, D], O_UZ + 14016), at("wos1", [P, D], O_WB + 28672)]
    lnw = at("lnw", [P, 2, VO], O_WB + 18816)
    o = O_WB
    xr = [at(f"xr{i}", [P, D], o + 4096 * i) for i in range(3)]
    o += 12288
    g1b = at("g1b", [P, 2, D], O_WS + 16384)
    o += 8192
    posr2 = [at(f"posr2{i}", [P, 512], o + 2048 * i) for i in range(2)]
    posc2 = at("posc2", [P, 512], o + 4096)
    o += 6144
    xn2 = at("xn2", [P, D], o)
    assert o + 4096 <= O_UZ
    tg = at("tg", [P, 512], O_UZ)
    h2f = at("h2f", [P, KT, P], O_UZ + 2048)
    acc = at("acc", [P, NT, D], O_WB)
    fst = [at(f"fst{i}", [P, D], O_UZ + 6144 + 4096 * i) for i in range(3)]
    assert O_UZ + 6144 + 12288 <= O_ST and O_WB + NT * D * 4 <= O_UZ + 6144
    o = O_ST
    f13h = [at(f"f13h{i}", [P, 2, KT, P], o + 16384 * i, F32R) for i in range(2)]
    f13l = [at(f"f13l{i}", [P, 2, KT, P], o + 8192 + 16384 * i, F32R) for i in range(2)]
    o += 32768
    f2h = at("f2h", [P, FB, D], o, F32R)
    f2l = at("f2l", [P, FB, D], o + 8192, F32R)
    o += 16384
    f_hi = at("f_hi", [P, FB, T], o, F32R)
    f_lo = at("f_lo", [P, FB, T], o + FB * T * 4, F32R)
    o += 2 * FB * T * 4
    sa = [at(f"sa{i}", [P, BW], o + 1536 * i) for i in range(2)]
    fv = [at(f"fv{i}", [P, BW], o + 3072 + 1536 * i) for i in range(2)]
    assert o + 6144 <= O_C
    g2b = [at("g2b0", [P, D], O_UZ + 6144), at("g2b1", [P, D], o + 6144)]
    assert o + 6144 + 4096 <= O_C
    xe = [at(f"xe{i}", [P, D], O_ST + 4096 * i) for i in range(4)]
    fgb = at("fgb", [P, D], O_NT)
    te = [at(f"te{i}", [P, D], O_NT + 4096 * (i + 1)) for i in range(2)]
    sq = at("sq", [P, D], O_NT + 12288)

    PS = [nc.alloc_psum_tensor(f"bank{i}", [P, 512], F32) for i in range(8)]
    z_dram = nc.dram_tensor("z_dram", [512, CH, UC], F32).ap()
    y_dram = nc.dram_tensor("y_dram", [512, CH, UC], F32).ap()
    wc_dram = nc.dram_tensor("wc_dram", [P, 2, Q, NC], F32).ap()
    kb_dram = nc.dram_tensor("kb_dram", [32, NPAIR, 15 * HD], F32).ap()
    x2_dram = nc.dram_tensor("x2_dram", [T, D], F32).ap()


    sems = {}

    def sem(name):
        if name not in sems:
            sems[name] = nc.alloc_semaphore(name)
        return sems[name]

    ZB = [4, 5, 6]
    VB = [2, 3, 7]
    GB = [(0, 3 * UC), (3 * UC, 3 * UC), (6 * UC, 2 * UC)]
    XG = [range(0, 4), range(4, 8), range(8, 9)]
    TB = [0, 2, 0, 2, 0, 2, 0, 6, 4]
    KC = (0, 1, 4, 5, 2, 3, 6, 7)
    OUT = (0, 1, 2, 3, 6, 7, 4, 5)
    UP = ("ffn_w1", "ffn_w3")

    def x_tile(i):
        return dview(A["x_sample"], i * P * D, [[D, P], [1, D]]) if i < 8 else dview(A["x_prompt"], 0, [[D, P], [1, D]])

    def pos_tile(i):
        return dview(A["pos_rows"], 2 * i * 512, [[512, 2], [0, GRID_W], [1, 512]])

    pos_cols2 = dview(A["pos_cols"], 0, [[0, 2], [512, GRID_W], [1, 512]])

    def wc_views(n):
        q0 = 4 * n
        step, base = (Q, 0) if n < 4 else (-Q, CH * Q)
        lr, li = (view(t, base + q0, [[1, 4], [step, NPOW], [0, HD]]) for t in (powr, powi))
        cr, ci = (view(cc, (r * Q + q0) * HD, [[HD, 4], [0, NPOW], [1, HD]]) for r in range(2))
        return lr, li, cr, ci, lambda t: view(t, 0, [[NC, 4], [HD, NPOW], [1, HD]])

    ADA_SLOTS = [n % 2 for n in range(KT + 4)] + [(n - KT - 2) % 3 for n in range(KT + 4, 3 * KT)]

    def ada_slot(n):
        e = ADA_SLOTS[n]
        return (ad0 if n < KT else ad1)[e], sem(f"ada{e}_in"), 16 * ADA_SLOTS[:n + 1].count(e)

    def ada_used(n):
        return max(m for m in range(n) if ADA_SLOTS[m] == ADA_SLOTS[n]) + 1

    def low_ready(i):
        return (sem("w_in_lo"), i + 1) if i < POOL_LOW else (sem("w_in_lo_pool"), i + 1 - POOL_LOW)

    def piece_count(n, c):
        return 16 * (c // 3 + 1) + (n - c) // 6 * 32 if isinstance(n, int) else (n - c) * 16 // 3 + 16 * (c // 3 + 1)

    def piece(c):
        c2 = c - 6 if c >= 6 else c
        if c2 < 4:
            return (f13h[c2 // 2][:, c2 % 2, :, :], f13l[c2 // 2][:, c2 % 2, :, :],
                    fst[c % 3][:, :].rearrange("p (k n) -> p k n", n=P))
        return f2h[:, c2 - 4, :], f2l[:, c2 - 4, :], fst[c % 3][:, :]

    block = ctx.enter_context(nc.Block())


    @block.sync
    def _(sp):
        def x_in(i):
            sp.dma_start(xt[i][:, :], x_tile(i)).then_inc(sem(f"x{i}_in"), 16)
            if i < 8:
                sp.dma_start(posr[i][:, :], pos_tile(i)).then_inc(sem(f"x{i}_in"), 16)

        def ada_bias(a):
            for q in range(4):
                sp.dma_start(abias[a][32 * q:32 * q + 32, :],
                             dview(A["ada_b"], a * 2048 + q * 512, [[0, 32], [1, 512]])).then_inc(sem(f"ada_bias{a}_in"), 16)

        def ada_in(n):
            slot, arrived, _ = ada_slot(n)
            sp.dma_start(slot[:, :], dview(A["ada_w"], n % KT * P * 6 * D + n // KT * 2048, [[6 * D, P], [1, 2048]])).then_inc(arrived, 16)

        def w_in_load(i):
            sp.dma_start(wst[i % 2][:, :, :], dview(A["w_in"], i * P, [[D_IN, P], [P * D_IN, KT], [1, P]])).then_inc(sem(f"w_in{i % 2}_in"), 16)

        ada_in(0)
        ada_in(1)
        for name, r0, n in (("norm1_g", V_N1, 8), ("norm2_g", V_N2, 8), ("ssm_b_glu", V_GB, 4), ("pool_scale", V_PS, 2),
                            ("conv_dw_b", V_CB, 2), ("conv_ln_g", V_LG, 2), ("conv_ln_b", V_LB, 2),
                            ("c_ctx", V_CX, 8), ("c", V_CC, 8)):
            sp.dma_start(rows[r0:r0 + n, :], dview(A[name], 0, [[P, n], [1, P]])).then_inc(sem("vectors_in"), 16)
        sp.dma_start(rtap[:, :], dview(A["conv_dw_w"], 0, [[P, 2 * TAPS], [1, P]])).then_inc(sem("vectors_in"), 16)
        for i, name in enumerate(("ssm_lam_re", "ssm_lam_im", "state_ssm_re", "state_ssm_im")):
            sp.dma_start(rlam[:, i, :], dview(A[name], 0, [[P, Q], [1, P]])).then_inc(sem("vectors_in"), 16)
        sp.dma_start(dn[:, :], dview(A["ssm_d"], 0, [[32, NPAIR], [1, 32]])).then_inc(sem("vectors_in"), 16)
        sp.dma_start(ldt[:, :], dview(A["ssm_log_dt"], 0, [[2, Q], [1, 2]])).then_inc(sem("log_dt_in"), 16)
        sp.dma_start(posc[:, :], pos_cols2).then_inc(sem("posc_in"), 16)
        x_in(0)
        x_in(1)
        for i, name in enumerate(("ssm_b_re", "ssm_b_im", "ssm_c_re", "ssm_c_im")):
            if i < 2:
                sp.dma_start(raw[i][:, :], dview(A[name], 0, [[2048, Q], [1, 2048]])).then_inc(sem("raws_in"), 16)
            else:
                for par in range(2):
                    sp.dma_start(view(raw[i], par * NS, [[P, HD], [1, NS]], 0, Q),
                                 dview(A[name], par * HD * NS, [[2048, Q], [NS, HD], [1, NS]])).then_inc(sem("raws_in"), 16)
        for n in range(2, KT):
            sp.wait_ge(sem("ada_tile"), n - 1)
            ada_in(n)
            x_in(n)
        x_in(8)
        ada_bias(0)
        w_in_load(0)
        w_in_load(1)
        sp.dma_start(edge[:, :], A["pool_edges"]).then_inc(sem("edges_in"), 16)
        for n in range(4):
            sp.wait_ge(sem("wc_made_dve"), 2 * (n + 1))
            for r in range(2):
                sp.dma_start(dview(wc_dram, (r * Q + 4 * n) * NC, [[2 * Q * NC, P], [1, 4 * NC]]),
                             view(wcd[n][r], 0, [[1, 4 * NC]])).then_inc(sem("wc_out2"), 16)
        for i in range(10):
            if i + 2 < 10:
                sp.wait_ge(*low_ready(i))
                w_in_load(i + 2)
            if i < 4:
                sp.wait_ge(sem("z_evac"), NB * (i + 1))
                sp.wait_ge(sem("zero_column"), 2)
                sp.dma_start(dview(z_dram, i * P * CH * UC, [[CH * UC, P], [1, CH * UC]]),
                             view(zp[i % 2], 0, [[1, CH * UC]])).then_inc(sem("z_out"), 16)
                sp.wait_ge(sem("z_out"), 16 * (i + 1))
                if i >= 2:
                    sp.wait_ge(sem("v_done"), 8 * (i - 1))
                for s in range(CH):
                    sp.dma_start(u8[i % 2][16 * s:16 * s + 16, :, :],
                                 dview(z_dram, i * P * CH * UC + s * UC, [[CH * UC, 16], [16 * CH * UC, 8], [1, UC]])).then_inc(sem(f"u{i}_in"), 16)
        sp.wait_ge(sem("gaps"), 13)
        for g in range(4):
            h = 64 * (g % 2)
            sp.dma_start(wpool[h:h + 64, g // 2, h:h + 64], dview(A["pool_w"], g * 4096, [[64, 64], [1, 64]])).then_inc(sem("wpool_in"), 16)
        sp.wait_ge(sem("bblk"), 2)
        sp.wait_ge(sem("wbt_made"), 16)
        ada_in(KT)
        sp.wait_ge(sem("z_done"), 30)
        ada_in(KT + 1)
        for s in range(2):
            sp.wait_ge(sem(f"wc_out{s}"), 64)
        sp.wait_ge(sem("wc_out2"), 128)
        for e in range(2):
            sp.dma_start(view(wc, 8 * e * NC, [[NPAIR * NC, 4], [1, 8 * NC]]),
                         dview(wc_dram, 8 * e * NC, [[2 * Q * NC, P], [NPAIR * NC, 4], [1, 8 * NC]])).then_inc(sem(f"wc{e}_in"), 16)
        def ada_more(n0, n1):
            for n in range(n0, n1):
                sp.wait_ge(sem("ada_tile"), ada_used(n))
                ada_in(n)

        ada_bias(1)
        ada_more(KT + 2, KT + 4)
        sp.wait_ge(sem("kb_evac"), 8)
        sp.dma_start(kb_dram, kb[:, :, :]).then_inc(sem("kb_out"), 16)
        ada_in(KT + 4)
        ada_more(KT + 5, 2 * KT)
        sp.wait_ge(sem("kb_out"), 16)
        RK = NPAIR * 15 * HD
        for s in range(CH):
            for par in range(2):
                sp.dma_start(view(toep, par * P, [[2 * P, NPAIR], [1, P]], 16 * s, 16),
                             dview(kb_dram, par * 16 * RK + (CH - 1 - s) * HD, [[RK, 16], [15 * HD, NPAIR], [1, P]])).then_inc(sem("toep_in"), 16)
        def u_again(j):
            for s in range(CH):
                sp.dma_start(u9[j % 2][16 * s:16 * s + 16, :, :],
                             dview(z_dram, j * P * CH * UC + s * UC, [[CH * UC, 16], [16 * CH * UC, 8], [1, UC]])).then_inc(sem(f"u{j}_in"), 16)

        sp.wait_ge(sem("pooled"), 2)
        u_again(0)
        u_again(1)
        sp.wait_ge(sem("ada_bank"), 2)
        ada_bias(2)
        ada_more(2 * KT, 2 * KT + 3)
        for r in range(2):
            sp.wait_ge(sem("fin_evac"), r + 1)
            sp.dma_start(dview(O[2 + r], 0, [[P, Q], [1, P]]), fin[:, r, :]).then_inc(sem("outputs"), 16)

        def out_weights(n):
            sp.dma_start(wos[n % 2][:, :], dview(A["w_out"], OUT[n] * P * D, [[D, P], [1, D]])).then_inc(sem(f"wo{n % 2}_in"), 16)

        sp.wait_ge(sem("gated"), 4)
        sp.wait_ge(sem("pool_done"), 6)
        sp.wait_ge(sem("outputs"), 32)
        for n in range(2):
            out_weights(n)
        for j in range(4):
            sp.wait_ge(sem("y_evac"), 4 * (j + 1))
            if j + 2 < 4:
                sp.wait_ge(sem("y_done"), 2 * (j + 1))
                u_again(j + 2)
            for t in range(CH):
                sp.dma_start(dview(y_dram, j * P * CH * UC + t * UC, [[CH * UC, 16], [16 * CH * UC, 8], [1, UC]]),
                             yb[j % 2][16 * t:16 * t + 16, :, :]).then_inc(sem("y_out"), 16)
            if j == 3:
                ada_more(3 * KT - 1, 3 * KT)
            sp.wait_ge(sem("y_out"), 16 * 8 * (j + 1))
            sp.dma_start(view(yT, j * CH * UC, [[1, CH * UC]]), dview(y_dram, j * P * CH * UC, [[CH * UC, P], [1, CH * UC]])).then_inc(sem("yT_in"), 16)
            if j < 2:
                ada_more(2 * KT + 3 + 2 * j, 2 * KT + 5 + j)
            elif j == 2:
                ada_more(3 * KT - 2, 3 * KT - 1)
        sp.wait_ge(sem("y_done"), 8)
        sp.dma_start(wglu[:, :, :], dview(A["ssm_w_glu"], 0, [[512, P], [P * 512, 4], [1, 512]])).then_inc(sem("wglu_in"), 16)
        for n in range(2, KT):
            sp.wait_ge(sem("wo_lo"), n - 1)
            out_weights(n)
        sp.wait_ge(sem("conv_out"), 4)
        sp.wait_ge(sem("glu_done"), 12)
        sp.wait_ge(sem("glu_made"), 4)
        sp.wait_ge(sem("y_part_pool"), 4)
        sp.dma_start(posc2[:, :], pos_cols2).then_inc(sem("posc_in"), 16)

        def piece_in(n, c, w, tile, dynamic):
            if dynamic or n >= 3:
                sp.wait_ge(sem("piece_lo"), n - 2)
            dst = fst[c % 3][:, :]
            if w == "ffn_w2":
                src = A[w][0][bass.ds(tile * P, P), :]
            else:
                src = A[w][0].rearrange("(k p) n -> p k n", p=P)[:, :, bass.ds(tile * P, P)]
                dst = dst.rearrange("p (k n) -> p k n", n=P)
            sp.dma_start(dst, src).then_inc(sem(f"piece{c % 3}_in"), 16)

        def x2_out(i):
            sp.wait_ge(sem("x2_made"), 2 * (i + 1))
            sp.dma_start(dview(x2_dram, i * P * D, [[D, P], [1, D]]), xr[i % 3][:, :]).then_inc(sem(f"tile_out{i % 3}"), 16)

        for i in range(NT):
            if i >= 3:
                sp.wait_ge(sem(f"tile_out{i % 3}"), 16 * (i // 3))
                sp.wait_ge(sem("x2_normed"), i - 2)
            sp.dma_start(xr[i % 3][:, :], x_tile(i)).then_inc(sem(f"xr{i % 3}_in"), 16)
            if i < 8:
                if i >= 2:
                    sp.wait_ge(sem("pos_half"), 2 * (8 + i - 1))
                sp.dma_start(posr2[i % 2][:, :], pos_tile(i)).then_inc(sem(f"posr{i % 2}_in"), 16)
            if i >= 1:
                x2_out(i - 1)
            if i >= 4 and i < 7:
                piece_in(i - 4, i - 4, UP[(i - 4) % 2], (i - 4) // 2, False)
        x2_out(NT - 1)

        def pieces_in(it, dynamic, last):
            n0 = 4 + 6 * it
            for f in range(FB):
                piece_in(n0 + f, 4 + f, "ffn_w2", FB * it + f, dynamic)
            if not last:
                for f in range(FB):
                    for e, w in enumerate(UP):
                        piece_in(n0 + 2 + 2 * f + e, 6 + 2 * f + e, w, FB * (it + 1) + f, dynamic)

        piece_in(3, 3, UP[1], 1, False)
        pieces_in(0, False, False)
        with sp.Fori(1, NFB - 1) as it:
            pieces_in(it, True, False)
        pieces_in(NFB - 1, False, True)
        sp.wait_ge(sem("up_done"), 2 * NB * (NFB - 1) + NB)
        for i in range(NT):
            if i < 3:
                sp.wait_ge(sem(f"tile_out{i}"), 48)
            if i >= 4:
                sp.wait_ge(sem("x2_added"), i - 3)
            sp.dma_start(xe[i % 4][:, :], dview(x2_dram, i * P * D, [[D, P], [1, D]])).then_inc(sem(f"x{i}_in"), 16)
        sp.wait_ge(sem("up_done"), 2 * NB * NFB)
        sp.dma_start(fgb[:, :], dview(A["final_g"], 0, [[0, P], [1, D]])).then_inc(sem("final_g_in"), 16)
        for i in range(NT):
            if i < NT - 1:
                sp.wait_ge(sem("y_made"), i + 1)
            else:
                sp.wait_ge(sem("last_y_made"), 1)
            dst = dview(O[1], i * P * D, [[D, P], [1, D]]) if i < 8 else dview(O[0], 0, [[D, P], [1, D]])
            sp.dma_start(dst, acc[:, i, :]).then_inc(sem("outputs"), 16)
        sp.wait_ge(sem("outputs"), 32 + 16 * NT)

    @block.gpsimd
    def _(pool):
        nc.gpsimd.memset(ident[:, :], 0.0).then_inc(sem("ident0"), 1)
        nc.gpsimd.memset(onesm[:, :], 1.0 / 256).then_inc(sem("ones"), 1)
        nc.gpsimd.memset(eps[:, :], EPS).then_inc(sem("ones"), 1)
        pool.wait_ge(sem("ident0"), 1)
        nc.gpsimd.affine_select(out=ident[:, :], in_=ident[:, :], compare_op=ALU.not_equal, fill=1.0,
                                base=0, pattern=[[-1, P]], channel_multiplier=1).then_inc(sem("ident"), 1)
        def pos_add(i):
            if i == 0:
                pool.wait_ge(sem("posc_in"), 16)
            pool.wait_ge(sem(f"x{i}_in"), 32)
            nc.gpsimd.tensor_tensor(xt[i][:, 0:512], xt[i][:, 0:512], posr[i][:, :], ALU.add).then_inc(sem("pos_half"), 1)
            nc.gpsimd.tensor_tensor(xt[i][:, 512:1024], xt[i][:, 512:1024], posc[:, :], ALU.add).then_inc(sem("pos_half"), 1)

        def wc_piece(n):
            lr, li, cr, ci, v3 = wc_views(4 + n)
            q0 = 4 * (4 + n)
            slot, tmp = wct[n % 2], wct_tmp
            if n >= 2:
                pool.wait_ge(sem(f"wc_out{n % 2}"), 32 * (n // 2))
            if n >= 1:
                pool.wait_ge(sem("wc_made"), 2 * n)
            nc.gpsimd.tensor_tensor(v3(slot[0]), lr, cr, ALU.mult).then_inc(sem("wc_terms"), 1)
            nc.gpsimd.tensor_tensor(v3(tmp[0]), li, ci, ALU.mult).then_inc(sem("wc_terms"), 1)
            nc.gpsimd.tensor_tensor(v3(slot[1]), lr, ci, ALU.mult).then_inc(sem("wc_terms"), 1)
            nc.gpsimd.tensor_tensor(v3(tmp[1]), li, cr, ALU.mult).then_inc(sem("wc_terms"), 1)
            pool.wait_ge(sem("wc_terms"), 4 * n + 2)
            nc.gpsimd.tensor_tensor(slot[0][:, :, :], slot[0][:, :, :], tmp[0][:, :, :], ALU.add).then_inc(sem("wc_made"), 1)
            pool.wait_ge(sem("wc_terms"), 4 * n + 4)
            nc.gpsimd.tensor_tensor(slot[1][:, :, :], slot[1][:, :, :], tmp[1][:, :, :], ALU.subtract).then_inc(sem("wc_made"), 1)
            pool.wait_ge(sem("wc_made"), 2 * n + 2)
            for r in range(2):
                pool.dma_start(dview(wc_dram, (r * Q + q0) * NC, [[2 * Q * NC, P], [1, 4 * NC]]),
                               view(slot[r], 0, [[1, 4 * NC]])).then_inc(sem(f"wc_out{n % 2}"), 16)

        for i in range(8):
            pos_add(i)
        pool.wait_ge(sem("powers"), 1)
        pool.wait_ge(sem("cc_evac"), 2)
        wc_piece(0)
        pool.wait_ge(sem("xT_bank"), 24)
        pool.wait_ge(sem("h_split"), 24)
        for s in range(2):
            nc.gpsimd.memset(zp[s][:, :, LC:LC + 1], 0.0).then_inc(sem("zero_column"), 1)
        for n in range(1, 4):
            wc_piece(n)
        pool.wait_ge(sem("v_done"), 32)
        for j in range(2):
            for o0 in (0, PZ + LAT, PL - PZ):
                nc.gpsimd.memset(pu[:, j, o0:o0 + PZ], 0.0).then_inc(sem("gaps"), 1)
            for o0 in (0, PAD + LAT, VL - PAD):
                nc.gpsimd.memset(vp[:, j, o0:o0 + PAD], 0.0).then_inc(sem("gaps"), 1)
        nc.gpsimd.memset(wpool[:, :, :], 0.0).then_inc(sem("gaps"), 1)
        for i in range(POOL_LOW, 10):
            if i == POOL_LOW + 1:
                nc.gpsimd.memset(bblk[:, :, :, :], 0.0).then_inc(sem("gaps"), 1)
            pool.wait_ge(sem("w_in_hi"), i + 1)
            nc.gpsimd.tensor_tensor(w_lo[i % 2][:, :, :], wst[i % 2][:, :, :], w_hi[i % 2][:, :, :].bitcast(F32), ALU.subtract).then_inc(low_ready(i)[0], 1)
        pool.wait_ge(sem("gaps"), 14)
        pool.wait_ge(*low_ready(9))
        for par in range(2):
            p0 = 64 * par
            nc.gpsimd.tensor_copy(view(bblk, 16 * par, [[32, 2 * Q], [1, HD]], p0, 64),
                                  view(bb, 0, [[HD, 2 * Q], [1, HD]], p0, 64)).then_inc(sem("bblk"), 1)
        pool.wait_ge(sem("edges_in"), 16)
        pool.wait_ge(sem("gaps"), 12)
        pool.wait_ge(sem("bblk"), 2)
        n_pool = [0]

        def pstep(ins):
            n_pool[0] += 1
            ins.then_inc(sem("pool_step"), 1)
            pool.wait_ge(sem("pool_step"), n_pool[0])

        for j in range(2):
            pool.wait_ge(sem("z_evac"), NB * (5 + j))
            W0, W1 = (lambda a, b, p0=0, n=P: psum_w[p0:p0 + n, 0, a:b]), (lambda a, b, p0=0, n=P: psum_w[p0:p0 + n, 1, a:b])
            pstep(nc.gpsimd.tensor_tensor(W0(1, PL), pu[:, j, 0:PL - 1], pu[:, j, 1:PL], ALU.add))
            if j == 0:
                pstep(nc.gpsimd.tensor_tensor(W1(2, PL - 1, 64, 64), W0(1, PL - 2, 64, 64), W0(3, PL, 64, 64), ALU.add))
            else:
                pstep(nc.gpsimd.tensor_tensor(W1(2, PL - 1), W0(1, PL - 2), W0(3, PL), ALU.add))
                pstep(nc.gpsimd.tensor_tensor(W0(4, PL - 3), W1(2, PL - 5), W1(6, PL - 1), ALU.add))
                pstep(nc.gpsimd.tensor_tensor(W1(8, PL - 7, 64, 64), W0(4, PL - 11, 64, 64), W0(12, PL - 3, 64, 64), ALU.add))
            for h, W in ((0, W0), (1, W1)):
                p0 = 64 * h
                pstep(nc.gpsimd.tensor_scalar(W(PZ, PL - PZ, p0, 64), W(PZ, PL - PZ, p0, 64), edge[p0:p0 + 64, j:j + 1], None, ALU.mult))
                for start, length in ((PZ, LAT), (PZ + LAT + PZ, CTX)):
                    for side in range(2):
                        a = start if side == 0 else start + length - 8
                        e0 = 2 + 16 * j + 8 * side
                        pstep(nc.gpsimd.tensor_tensor(W(a, a + 8, p0, 64), W(a, a + 8, p0, 64), edge[p0:p0 + 64, e0:e0 + 8], ALU.mult))
                pstep(nc.gpsimd.tensor_tensor(pu[p0:p0 + 64, j, PZ:PL - PZ], W(PZ, PL - PZ, p0, 64), pu[p0:p0 + 64, j, PZ:PL - PZ], ALU.subtract))
            pool.sem_inc(sem("pooled"), 1)
        for j in range(2):
            pool.wait_ge(sem("z_evac"), NB * (9 + j))
            for a0, b0, n in ((PAD, 0, LAT), (PAD + LAT + PAD, LAT, CTX)):
                nc.gpsimd.tensor_tensor(vp[:, j, a0:a0 + n], vp[:, j, a0:a0 + n], sig[:, j, b0:b0 + n], ALU.mult).then_inc(sem("gated"), 1)
        def wo_low(n):
            k = OUT[n]
            pool.wait_ge(sem("wo_hi"), n + 1)
            nc.gpsimd.tensor_tensor(wo_lo[k][:, :], wos[n % 2][:, :], wo_hi[k][:, :].bitcast(F32), ALU.subtract).then_inc(sem("wo_lo"), 1)

        for j in range(2):
            pool.wait_ge(sem("y_part_act"), j + 1)
            nc.gpsimd.tensor_tensor(y_lo[4 + j][:, :], ymp[:, j, :], y_hi[4 + j][:, :].bitcast(F32), ALU.subtract).then_inc(sem("y_part_pool"), 1)
        for n in range(KT):
            wo_low(n)
        for m in (2, 3):
            pool.wait_ge(sem("y_part_dve"), m + 1)
            nc.gpsimd.tensor_tensor(y_lo[m][:, :], ym[m % 2][:, :], y_hi[m][:, :].bitcast(F32), ALU.subtract).then_inc(sem("y_part_pool"), 1)
        pool.wait_ge(sem("posc_in"), 32)
        for i in range(8):
            pool.wait_ge(sem(f"xr{i % 3}_in"), 16 * (i // 3 + 1))
            pool.wait_ge(sem(f"posr{i % 2}_in"), 16 * (i // 2 + 1))
            nc.gpsimd.tensor_tensor(xr[i % 3][:, 0:512], xr[i % 3][:, 0:512], posr2[i % 2][:, :], ALU.add).then_inc(sem("pos_half"), 1)
            nc.gpsimd.tensor_tensor(xr[i % 3][:, 512:1024], xr[i % 3][:, 512:1024], posc2[:, :], ALU.add).then_inc(sem("pos_half"), 1)
        def piece_lo(n, c):
            pool.wait_ge(sem("piece_hi"), n + 1)
            hi, lo, src = piece(c)
            nc.gpsimd.tensor_tensor(lo, src, hi.bitcast(F32), ALU.subtract).then_inc(sem("piece_lo"), 1)

        def f_low(it, f, n0=0, n1=NB):
            for n in range(n0, n1):
                b = NB * f + n
                pool.wait_ge(sem("f_hi"), 2 * NB * it + b + 1)
                nc.gpsimd.tensor_tensor(f_lo[:, f, n * BW:(n + 1) * BW], fv[b % 2][:, :],
                                        f_hi[:, f, n * BW:(n + 1) * BW].bitcast(F32), ALU.subtract).then_inc(sem("f_lo"), 1)

        def lows(it, first, last):
            n0 = 4 + 6 * it
            if first:
                f_low(0, 0, 0, 1)
                piece_lo(2, 2)
                piece_lo(3, 3)
                f_low(0, 0, 1, NB)
            piece_lo(n0, 4)
            piece_lo(n0 + 1, 5)
            for f in range(FB):
                if not (first and f == 0):
                    f_low(it, f)
                if not last:
                    for e in range(2):
                        piece_lo(n0 + 2 + 2 * f + e, 6 + 2 * f + e)

        for n in range(2):
            piece_lo(n, n)
        lows(0, True, False)
        with pool.Fori(1, NFB - 1) as it:
            lows(it, False, False)
        lows(NFB - 1, False, True)
        for i in range(NT - 1):
            if i == 0:
                pool.wait_ge(sem("final_g_in"), 16)
            pool.wait_ge(sem("end_normed"), i + 1)
            nc.gpsimd.tensor_tensor(acc[:, i, :], acc[:, i, :], fgb[:, :], ALU.mult).then_inc(sem("y_made"), 1)

    B = PS

    def three(out, hi_w, lo_w, hi_x, lo_x, start, stop):
        nc.tensor.matmul(out, hi_w, hi_x, start=start, stop=False)
        nc.tensor.matmul(out, hi_w, lo_x, start=False, stop=False)
        return nc.tensor.matmul(out, lo_w, hi_x, start=False, stop=stop)

    @block.tensor
    def _(pe):
        mm, tr = nc.tensor.matmul, nc.tensor.transpose
        pe.wait_ge(sem("ident"), 1)
        pe.wait_ge(sem("vectors_in"), 240)
        pe.wait_ge(sem("dt_rows"), 1)
        tr(B[6][:, 0:VR], rows[:, :], ident[0:VR, 0:VR])
        tr(B[6][:, X_TAP:X_TAP + 2 * TAPS], rtap[:, :], ident[0:2 * TAPS, 0:2 * TAPS])
        for i in range(5):
            tr(B[6][:, X_LRE + Q * i:X_LRE + Q * (i + 1)], rlam[:, i, :], ident[0:Q, 0:Q])
        tr(B[7][0:32, 0:NPAIR], dn[:, :], ident[0:NPAIR, 0:NPAIR]).then_inc(sem("params_turned"), 1)

        def raws_turn():
            pe.wait_ge(sem("raws_in"), 96)
            for i in range(4):
                for h in range(HD):
                    src = view(raw[i], h, [[HD, P]], 0, Q) if i < 2 else view(raw[i], h * P, [[1, P]], 0, Q)
                    last = tr(B[i][:, h * Q:(h + 1) * Q], src, ident[0:Q, 0:Q])
                last.then_inc(sem("raws_turned"), 1)

        def ada_tiles(a, k0, k1, bank):
            for k in range(k0, k1):
                slot, arrived, count = ada_slot(KT * a + k)
                pe.wait_ge(arrived, count)
                for q in range(4):
                    last = mm(bank[32 * q:32 * q + 32, :], condT[:, k, :], slot[:, 512 * q:512 * q + 512], start=(k == 0), stop=False)
                last.then_inc(sem("ada_tile"), 1)

        def ada_bias_add(a, bank):
            pe.wait_ge(sem(f"ada_bias{a}_in"), 64)
            for q in range(4):
                last = mm(bank[32 * q:32 * q + 32, :], ident[32 * q:32 * q + 32, 32 * q:32 * q + 32], abias[a][32 * q:32 * q + 32, :], start=False, stop=True)
            last.then_inc(sem("ada_bank"), 1)

        def mod_turn(a, bank):
            pe.wait_ge(sem("ada_row"), a + 1)
            for b in range(4):
                last = tr(bank[:, P * b:P * b + P], arow[a][:, P * b:P * b + P], ident[:, :])
            last.then_inc(sem("mod_turned"), 1)

        def x_turns(n0, n1):
            for n in range(n0, n1):
                grp, k = XG[n // KT], n % KT
                if n == 0:
                    pe.wait_ge(sem("bb_made"), 2)
                    pe.wait_ge(sem("cc_evac"), 2)
                if k == 0:
                    pe.wait_ge(sem("x_normed"), grp[-1] + 1)
                if n >= 4:
                    pe.wait_ge(sem("h_evac"), n - 3)
                for t, i in enumerate(grp):
                    last = tr(B[n % 4][:, P * t:P * t + P], xt[i][:, P * k:P * k + P], ident[:, :])
                last.then_inc(sem("xT_bank"), 1)

        pe.wait_ge(sem("cond"), 2)
        ada_tiles(0, 0, 4, B[4])
        raws_turn()
        ada_tiles(0, 4, KT, B[4])
        ada_bias_add(0, B[4])
        x_turns(0, 4)
        mod_turn(0, B[5])
        x_turns(4, 2 * KT)

        def z_tile(i):
            pe.wait_ge(*low_ready(i))
            for b in range(NB):
                n = NB * i + b
                if n < 3:
                    pe.wait_ge(sem("mod_evac"), 1)
                    pe.wait_ge(sem("squares"), 2 * NT)
                    pe.wait_ge(sem("h_split"), KT * (n + 1))
                    if n == 1:
                        x_turns(2 * KT, 3 * KT)
                else:
                    pe.wait_ge(sem("z_evac"), n - 2)
                for k in range(KT):
                    last = three(B[ZB[b]][:, 0:BW], w_hi[i % 2][:, k, :], w_lo[i % 2][:, k, :],
                                 nt_hi[:, k, b * BW:(b + 1) * BW], nt_lo[:, k, b * BW:(b + 1) * BW], k == 0, k == KT - 1)
                last.then_inc(sem("z_done"), 1)

        def wb_turn(j):
            for d in range(2):
                pe.wait_ge(sem("wbt_made"), 2 * (2 * j + d + 1))
                for r in range(2):
                    c = 4 * j + 2 * d + r
                    pe.wait_ge(sem("h_evac"), 24) if c < 2 else pe.wait_ge(sem("wb_evac"), c - 1)
                    for i in range(4):
                        last = tr(B[c % 2][:, P * i:P * i + P], wbt[d][r][:, i, :], ident[:, :])
                    last.then_inc(sem("wb_turned"), 1)

        def state_inputs(j):
            pe.wait_ge(sem(f"u{j}_in"), 128)
            pe.wait_ge(sem("wb_evac"), 4 * j + 4)
            for d in range(2):
                for pp in range(4):
                    c = 8 * j + 4 * d + pp
                    if c >= 3:
                        pe.wait_ge(sem("v_evac"), c - 2)
                    q = NPAIR * d + 4 * j + pp
                    for par in range(2):
                        rhs = u8[j % 2][:, 2 * pp + par, :] if d == 0 else u8[j % 2][:, 2 * pp + par, ::-1]
                        for r in range(2):
                            last = mm(B[VB[c % 3]][64 * par:64 * par + 64, UC * r:UC * r + UC],
                                      wb[:, r, q, 64 * par:64 * par + 64], rhs, start=True, stop=True)
                    last.then_inc(sem("v_done"), 1)

        for i in range(10):
            z_tile(i)
            if i < 4:
                wb_turn(i)
            elif i == 4:
                state_inputs(2)
                state_inputs(3)
            if i == 3:
                state_inputs(0)
                state_inputs(1)
        pe.wait_ge(sem("bblk"), 2)
        pe.wait_ge(sem("dsel"), 1)
        pe.wait_ge(sem("v_evac"), 32)
        pe.wait_ge(sem("wb_evac"), 16)
        ada_tiles(1, 0, 2, B[0])
        for n, c in enumerate(KC):
            bank = B[(7, 2)[n % 2]]
            if n % 4 == 0:
                pe.wait_ge(sem(f"wc{n // 4}_in"), 16)
            if n >= 2:
                pe.wait_ge(sem("kb_evac"), n - 1)
            for i in range(4):
                gp = 4 * (c % 4) + i
                o = P * i
                if c < 4:
                    for r in range(2):
                        mm(bank[0:32, o:o + P], bblk[:, r, gp, :], wc[:, r, gp, 0:P], start=(r == 0), stop=False)
                    for r in range(2):
                        mm(bank[0:32, o:o + HD], bblk[:, r, NPAIR + gp, :], wc[:, r, NPAIR + gp, P:P + HD], start=False, stop=False)
                    last = mm(bank[0:32, o:o + HD], ident[0:32, 0:32], dsel[:, gp, :], start=False, stop=True)
                else:
                    for r in range(2):
                        last = mm(bank[0:32, o:o + P], bblk[:, r, NPAIR + gp, :], wc[:, r, NPAIR + gp, HD:HD + P], start=(r == 0), stop=(r == 1))
            last.then_inc(sem("kb_done"), 1)
        ada_tiles(1, 2, KT, B[0])
        ada_bias_add(1, B[0])
        pe.wait_ge(sem("wpool_in"), 64)
        pe.wait_ge(sem("z_evac"), 30)
        pe.wait_ge(sem("kb_evac"), 8)
        for j in range(2):
            pe.wait_ge(sem("pooled"), j + 1)
            for b in range(NB):
                n = NB * j + b
                if n >= 2:
                    pe.wait_ge(sem("pool_evac"), n - 1)
                bank = B[6 + n % 2]
                if b < 2:
                    last = mm(bank[:, 0:BW], wpool[:, j, :], pu[:, j, PZ + b * BW:PZ + (b + 1) * BW], start=True, stop=True)
                else:
                    mm(bank[:, 0:256], wpool[:, j, :], pu[:, j, PZ + 768:PZ + LAT], start=True, stop=True)
                    last = mm(bank[:, 256:BW], wpool[:, j, :], pu[:, j, PZ + LAT + PZ:PZ + LAT + PZ + CTX], start=True, stop=True)
                last.then_inc(sem("pool_done"), 1)
        mod_turn(1, B[1])
        pe.wait_ge(sem("scan_done"), 1)
        pe.wait_ge(sem("pool_evac"), 6)
        for r in range(2):
            last = tr(B[6][0:Q, P * r:P * r + P], scT[:, 0, r, :], ident[:, :])
        last.then_inc(sem("fin_turned"), 1)
        def gate_rows(a, q0, banks):
            for who in range(2):
                for h in range(2):
                    q = q0 + h
                    last = mm(banks[2 * who + h][:, :], ident[32 * q:32 * q + 32, 32 * q + 16 * who:32 * q + 16 * who + 1].broadcast_to([32, P]),
                              arow[a][32 * q:32 * q + 32, :], start=True, stop=True)
            last.then_inc(sem("gate_rows"), 1)

        pe.wait_ge(sem("toep_in"), 256)
        pe.wait_ge(sem("kb_evac"), 8)
        for c in range(8):
            j = c // 2
            if c % 2 == 0:
                pe.wait_ge(sem(f"u{j}_in"), 256)
            if c >= 2:
                pe.wait_ge(sem("y_evac"), 2 * (c - 1))
            for i in range(2):
                gp = 2 * c + i
                for par in range(2):
                    out = B[(2, 4)[c % 2] + par][:, UC * i:UC * i + UC]
                    p0 = 64 * par
                    mm(out, toep[:, 2 * gp + par, :], u9[j % 2][:, (2 * gp + par) % 8, :], start=True, stop=False)
                    for r in range(2):
                        base = (r * Q + gp) * SLOTS
                        mm(out, wc[p0:p0 + 64, r, gp, HD:HD + P], view(st, base, [[1, UC]], p0, 64), start=False, stop=False)
                    for r in range(2):
                        base = (r * Q + NPAIR + gp) * SLOTS
                        last = mm(out, wc[p0:p0 + 64, r, NPAIR + gp, 0:P], view(st, base + UC - 1, [[-1, UC]], p0, 64), start=False, stop=(r == 1))
            last.then_inc(sem("y_done"), 1)
            if c % 2 and c < 7:
                pe.wait_ge(sem("mod_evac"), 2)
                ada_tiles(2, (0, 2, 3)[c // 2], (2, 3, 4)[c // 2], B[0])
        ada_tiles(2, 4, 6, B[0])
        pe.wait_ge(sem("y_evac"), 16)
        gate_rows(1, 0, B[2:6])
        ada_tiles(2, 6, KT, B[0])
        ada_bias_add(2, B[0])
        pe.wait_ge(sem("yT_in"), 64)
        pe.wait_ge(sem("wglu_in"), 16)
        pe.wait_ge(sem("ada_row"), 3)
        pe.wait_ge(sem("fin_evac"), 2)

        def glu_tile(m):
            for b, (c0, n) in enumerate(GB):
                c = NB * m + b
                if c >= 3:
                    pe.wait_ge(sem("glu_gate"), c - 2)
                for k in range(4):
                    last = mm(B[(6, 7, 0)[b]][:, 0:n], wglu[:, k, P * m:P * m + P], yT[:, k, c0:c0 + n], start=(k == 0), stop=(k == 3))
                last.then_inc(sem("glu_done"), 1)

        def channel_mean(src, b):
            for j in range(2):
                last = mm(B[1 + b][:, 0:389], onesm[:, :], src[:, j, 389 * b:389 * b + 389], start=(j == 0), stop=(j == 1))
            last.then_inc(sem("channels_meant"), 1)

        glu_tile(0)
        mod_turn(2, B[1])
        pe.wait_ge(sem("mod_evac"), 3)
        pe.wait_ge(sem("gate_evac"), 4)
        pe.wait_ge(sem("conv_made"), 2)
        for b in range(NB):
            channel_mean(cacc, b)
        glu_tile(1)
        for b in range(NB):
            pe.wait_ge(sem("dev_squared"), 2 * (b + 1))
            channel_mean(lnw, b)
        glu_tile(2)
        glu_tile(3)
        def h2_turn(i):
            pe.wait_ge(sem("x2_normed"), i + 1)
            if i >= 2:
                pe.wait_ge(sem("h2_evac"), i - 1)
            for k in range(KT):
                last = tr(B[TB[i] + k // 4][:, P * (k % 4):P * (k % 4) + P], xn2[:, P * k:P * k + P], ident[:, :])
            last.then_inc(sem("h2_turned"), 1)

        pe.wait_ge(sem("wo_lo"), KT)
        pe.wait_ge(sem("gate_evac"), 4)
        ready = {4: ("y_part_pool", 2), 0: ("y_part_dve", 1), 1: ("y_part_dve", 2), 6: ("y_part_dve", 6), 2: ("y_part_pool", 3),
                 7: ("y_part_dve", 8), 3: ("y_part_pool", 4)}
        order = (4, 5, 0, 1, 6, 2, 7, 3)
        for i in range(NT):
            for h in range(2):
                c = 2 * i + h
                if c >= 4:
                    pe.wait_ge(sem("x2_made"), c - 3)
                for n, k in enumerate(order):
                    if c == 0 and k in ready:
                        pe.wait_ge(sem(ready[k][0]), ready[k][1])
                    last = three(B[4 + c % 4][:, :], y_hi[k][:, P * i:P * i + P], y_lo[k][:, P * i:P * i + P],
                                 wo_hi[k][:, 512 * h:512 * h + 512], wo_lo[k][:, 512 * h:512 * h + 512], n == 0, n == KT - 1)
                last.then_inc(sem("o_done"), 1)
                if c == 2 * NT - 2:
                    h2_turn(NT - 2)
            if 1 <= i < NT - 1:
                h2_turn(i - 1)
        def up(it, f, first, last_one=False):
            for n in range(NB):
                b = NB * f + n
                if first and f == 0:
                    if n == 1:
                        h2_turn(NT - 1)
                    pe.wait_ge(sem("h_split"), 3 * KT + 3 * (n + 1))
                    pe.wait_ge(sem("h2_evac"), 7)
                if last_one and b == 1:
                    pe.wait_ge(sem("acc_done"), 2 * NT * (NFB - 1))
                    gate_rows(2, 2, B[4:8])
                if not first or b >= 2:
                    pe.wait_ge(sem("silu_made"), 2 * NB * it + b - 1)
                    pe.wait_ge(sem("f_made"), 2 * NB * it + b - 1)
                for e in range(2):
                    if n == 0:
                        pe.wait_ge(sem("piece_lo"), 6 * it + 2 * f + e + 1)
                    for k in range(KT):
                        last = three(B[2 * e + b % 2][:, 0:BW], f13h[f][:, e, k, :], f13l[f][:, e, k, :],
                                     nt_hi[:, k, n * BW:(n + 1) * BW], nt_lo[:, k, n * BW:(n + 1) * BW], k == 0, k == KT - 1)
                    last.then_inc(sem("gate_done" if e == 0 else "up_done"), 1)

        def down(it, first, last_one=False):
            pe.wait_ge(sem("piece_lo"), 6 * it + 6)
            for i in range(NT):
                if last_one and i == 0:
                    pe.wait_ge(sem("gate_evac"), 8)
                if i % 3 == 0:
                    pe.wait_ge(sem("f_lo"), 2 * NB * it + NB + i // 3 + 1)
                for h in range(2):
                    c = 2 * i + h
                    if not first or c >= 4:
                        pe.wait_ge(sem("acc_done"), 2 * NT * it + c - 3)
                    for f in range(FB):
                        last = three(B[4 + c % 4][:, :], f_hi[:, f, P * i:P * i + P], f_lo[:, f, P * i:P * i + P],
                                     f2h[:, f, 512 * h:512 * h + 512], f2l[:, f, 512 * h:512 * h + 512], f == 0, f == FB - 1)
                    last.then_inc(sem("down_done"), 1)

        for f in range(FB):
            up(0, f, True)
        down(0, True)
        with pe.Fori(1, NFB - 1) as it:
            for f in range(FB):
                up(it, f, False)
            down(it, False)
        for f in range(FB):
            up(NFB - 1, f, False, True)
        down(NFB - 1, False, True)

    @block.scalar
    def _(act):
        A_ = nc.scalar.activation

        act.wait_ge(sem("pv_evac"), 2)
        for who, v in enumerate((V_CX, V_CC)):
            A_(condT[:, :, 16 * who:16 * who + 16], view(pv, v, [[1, KT], [0, 16]]), ACT.Silu).then_inc(sem("cond"), 1)
        A_(prm[:, 0, :], pv[:, X_DT:X_DT + Q], ACT.Exp).then_inc(sem("polar"), 1)
        act.wait_ge(sem("lam_dt"), 2)
        A_(prm[:, 3, :], prm[:, 1, :], ACT.Exp).then_inc(sem("polar"), 1)
        act.wait_ge(sem("angles"), 2)
        A_(prm[:, 8, :], prm[:, 5, :], ACT.Sin).then_inc(sem("polar"), 1)
        A_(prm[:, 9, :], prm[:, 7, :], ACT.Sin).then_inc(sem("polar"), 1)

        def mod_row_out(a, bank):
            act.wait_ge(sem("ada_bank"), a + 1)
            A_(arow[a][:, :], bank[:, :], ACT.Copy).then_inc(sem("ada_row"), 1)

        def mod_turn_out(a, bank):
            act.wait_ge(sem("mod_turned"), a + 1)
            A_(view(modc, 32 * a, [[2, 4], [8, 4], [1, 2]]), view(bank, 0, [[P, 4], [32, 4], [16, 2]]), ACT.Copy).then_inc(sem("mod_evac"), 1)

        def square_sums(g):
            for i in XG[g]:
                if i < 8:
                    act.wait_ge(sem("pos_half"), 2 * (i + 1))
                else:
                    act.wait_ge(sem("x8_in"), 16)
                for h in range(2):
                    if 2 * i + h >= 2:
                        act.wait_ge(sem("squares"), 2 * i + h - 1)
                    A_(B[6 + h][:, :], xt[i][:, 512 * h:512 * h + 512], ACT.Square, accum_out=ss[:, 2 * i + h:2 * i + h + 1]).then_inc(sem("squares"), 1)

        def normalise(g):
            i0, i1 = XG[g][0], XG[g][-1] + 1
            act.wait_ge(sem("inverse_ms"), g + 1)
            A_(rstd[:, i0:i1], var[:, i0:i1], ACT.Sqrt).then_inc(sem("rstd"), 1)
            act.wait_ge(sem("rstd"), g + 1)
            for i in XG[g]:
                A_(xt[i][:, :], xt[i][:, :], ACT.Copy, scale=rstd[:, i:i + 1]).then_inc(sem("x_normed"), 1)

        square_sums(0)
        normalise(0)
        act.wait_ge(sem("raws_turned"), 3)
        A_(view(cc, 0, [[1, HD], [HD, Q]]), B[2][:, :], ACT.Copy).then_inc(sem("cc_evac"), 1)
        act.wait_ge(sem("raws_turned"), 4)
        A_(view(cc, Q * HD, [[1, HD], [HD, Q]]), B[3][:, :], ACT.Copy, scale=-1.0).then_inc(sem("cc_evac"), 1)
        square_sums(1)
        mod_row_out(0, B[4])
        normalise(1)
        mod_turn_out(0, B[5])
        act.wait_ge(sem("gsc"), 1)
        act.wait_ge(sem("mod_evac"), 1)

        def w_high(i):
            act.wait_ge(sem(f"w_in{i % 2}_in"), 16 * (i // 2 + 1))
            if i < 2:
                act.wait_ge(sem("ada_tile"), 8)
            else:
                act.wait_ge(sem("z_done"), NB * (i - 1))
            nc.scalar.copy(w_hi[i % 2][:, :, :], wst[i % 2][:, :, :]).then_inc(sem("w_in_hi"), 1)

        n = 0
        for g, grp in enumerate(XG):
            if g >= 1:
                w_high(g - 1)
            if g == 1:
                square_sums(2)
                normalise(2)
            for k in range(KT):
                act.wait_ge(sem("xT_bank"), n + 1)
                if n >= 3:
                    act.wait_ge(sem("h_split"), n - 2)
                w = P * len(grp)
                who = 0 if g == 2 else 1
                A_(hf[n % 3][:, 0:w], B[n % 4][:, 0:w], ACT.Identity, scale=gsc[:, 0, k, who:who + 1],
                   bias=modc[:, k, who:who + 1]).then_inc(sem("h_evac"), 1)
                n += 1

        def z_out(i):
            for b in range(NB):
                src = B[ZB[b]]
                act.wait_ge(sem("z_done"), NB * i + b + 1)
                if i < 4 and b == 0 and i >= 2:
                    act.wait_ge(sem("z_out"), 16 * (i - 1))
                if i == 4 and b == 0:
                    act.wait_ge(sem("v_done"), 32)
                if i < 4:
                    parts = ((48 * b, 0, 48),) if b < 2 else ((96, 0, 32), (LC + 1, 256, 16))
                    for c0, o, m in parts:
                        last = A_(view(zp[i % 2], c0, [[1, m], [UC, CH]]), src[:, o:o + CH * m], ACT.Copy)
                else:
                    dst, pad = ((pu, PZ), (vp, PAD), (sig, 0))[(i - 4) // 2]
                    fn = ACT.Sigmoid if dst is sig else ACT.Copy
                    parts = ((BW * b, 0, BW),) if b < 2 else ((768, 0, 256), (LAT + pad, 256, CTX))
                    for c0, o, m in parts:
                        last = A_(dst[:, i % 2, pad + c0:pad + c0 + m], src[:, o:o + m], fn)
                last.then_inc(sem("z_evac"), 1)

        def wb_out(j):
            for d in range(2):
                for r in range(2):
                    c = 4 * j + 2 * d + r
                    if c == 0:
                        act.wait_ge(sem("raws_turned"), 4)
                    act.wait_ge(sem("wb_turned"), c + 1)
                    q0 = NPAIR * d + 4 * j
                    A_(wb[:, r, q0:q0 + 4, :], B[c % 2][:, :].rearrange("p (q n) -> p q n", n=P), ACT.Copy).then_inc(sem("wb_evac"), 1)

        def v_out(j):
            for d in range(2):
                for pp in range(4):
                    c = 8 * j + 4 * d + pp
                    q = NPAIR * d + 4 * j + pp
                    act.wait_ge(sem("v_done"), c + 1)
                    if c == 0:
                        for s in range(2):
                            act.wait_ge(sem(f"wc_out{s}"), 64)
                    A_(view(st, q * SLOTS + 1, [[Q * SLOTS, 2], [1, UC]]), view(B[VB[c % 3]], 0, [[UC, 2], [1, UC]]), ACT.Copy).then_inc(sem("v_evac"), 1)

        for i in range(10):
            if i == 4:
                v_out(2)
                v_out(3)
                act.wait_ge(sem("gaps"), 12)
            z_out(i)
            if i < 4:
                wb_out(i)
            if i == 3:
                v_out(0)
                v_out(1)
            if i + 2 < 10:
                w_high(i + 2)
        for n, c in enumerate(KC):
            act.wait_ge(sem("kb_done"), n + 1)
            bank = B[(7, 2)[n % 2]]
            w, o = (P, 7 * HD) if c < 4 else (7 * HD, 0)
            A_(view(kb, 4 * (c % 4) * 15 * HD + o, [[15 * HD, 4], [1, w]], 0, 32), view(bank, 0, [[P, 4], [1, w]], 0, 32), ACT.Copy).then_inc(sem("kb_evac"), 1)
        mod_row_out(1, B[0])
        for j in range(2):
            for b in range(NB):
                n = NB * j + b
                act.wait_ge(sem("pool_done"), n + 1)
                A_(ymp[:, j, b * BW:(b + 1) * BW], B[6 + n % 2][:, 0:BW], ACT.Copy, scale=pv[:, V_PS + j:V_PS + j + 1]).then_inc(sem("pool_evac"), 1)
        mod_turn_out(1, B[1])
        act.wait_ge(sem("fin_turned"), 1)
        for r in range(2):
            A_(fin[:, r, :], B[6][0:Q, P * r:P * r + P], ACT.Copy).then_inc(sem("fin_evac"), 1)
        for c in range(8):
            j = c // 2
            act.wait_ge(sem("y_done"), c + 1)
            if c % 2 == 0 and j >= 2:
                act.wait_ge(sem("y_out"), 128 * (j - 1))
            for par in range(2):
                A_(view(yb[j % 2], (4 * (c % 2) + par) * UC, [[2 * UC, 2], [1, UC]]),
                   view(B[(2, 4)[c % 2] + par], 0, [[UC, 2], [1, UC]]), ACT.Gelu_apprx_tanh).then_inc(sem("y_evac"), 1)
        def wo_high(n):
            act.wait_ge(sem(f"wo{n % 2}_in"), 16 * (n // 2 + 1))
            if n == 4:
                act.wait_ge(sem("ada_tile"), 3 * KT)
            if n == 6:
                act.wait_ge(sem("y_part_pool"), 2)
            nc.scalar.copy(wo_hi[OUT[n]][:, :], wos[n % 2][:, :]).then_inc(sem("wo_hi"), 1)

        def y_high(k, src):
            nc.scalar.copy(y_hi[k][:, :], src).then_inc(sem("y_part_act"), 1)

        act.wait_ge(sem("y_done"), 8)
        act.wait_ge(sem("pool_evac"), 6)
        for j in range(2):
            y_high(4 + j, ymp[:, j, :])
        for n in range(2):
            wo_high(n)
        act.wait_ge(sem("a8_copied"), 3)
        act.wait_ge(sem("wc_made"), 8)
        act.wait_ge(sem("wc_made_dve"), 8)
        mod_row_out(2, B[0])
        act.wait_ge(sem("gate_rows"), 1)
        for who in range(2):
            for h in range(2):
                A_(g1b[:, who, 512 * h:512 * h + 512], B[2 + 2 * who + h][:, :], ACT.Copy).then_inc(sem("gate_evac"), 1)

        def glu_gate(m):
            for b, (c0, n) in enumerate(GB):
                act.wait_ge(sem("glu_done"), NB * m + b + 1)
                if b == 0 and m >= 1:
                    act.wait_ge(sem("glu_made"), m)
                A_(gsig[:, c0:c0 + n], B[(6, 7, 0)[b]][:, 0:n], ACT.Sigmoid, bias=pv[:, V_GB + m:V_GB + m + 1]).then_inc(sem("glu_gate"), 1)

        def conv_silu(j):
            act.wait_ge(sem("ln_scaled"), j + 1)
            for dst, done in ((y_hi[6 + j], "y_part_act"), (cacc[:, j, :], "conv_out")):
                for c0, o, m in ((0, 0, LAT), (VCTX, LAT, CTX)):
                    out = dst[:, o:o + m] if done == "y_part_act" else dst[:, c0:c0 + m]
                    if done == "conv_out":
                        act.wait_ge(sem("y_part_act"), 4 + 2 * j + 2)
                    A_(out, cacc[:, j, c0:c0 + m], ACT.Silu, scale=pv[:, V_LG + j:V_LG + j + 1],
                       bias=pv[:, V_LB + j:V_LB + j + 1]).then_inc(sem(done), 1)

        glu_gate(0)
        mod_turn_out(2, B[1])
        for n in range(2, 4):
            wo_high(n)
        for b in range(NB):
            for j in range(2):
                act.wait_ge(sem("deviation"), 2 * b + j + 1)
                A_(lnw[:, j, 389 * b:389 * b + 389], cacc[:, j, 389 * b:389 * b + 389], ACT.Square).then_inc(sem("dev_squared"), 1)
        wo_high(4)
        glu_gate(1)
        act.wait_ge(sem("glu_made"), 1)
        y_high(0, ym[0][:, :])
        act.wait_ge(sem("ones"), 2)
        for b in range(NB):
            act.wait_ge(sem("channels_meant"), NB + b + 1)
            A_(view(sig, 389 * b, [[1, 389]]), B[1 + b][:, 0:389], ACT.Sqrt, bias=eps[:, 0:1]).then_inc(sem("ln_root"), 1)
        wo_high(5)
        glu_gate(2)
        act.wait_ge(sem("glu_made"), 2)
        y_high(1, ym[1][:, :])
        wo_high(6)
        wo_high(7)
        conv_silu(0)
        glu_gate(3)
        conv_silu(1)
        def piece_hi(n, c, after=None):
            act.wait_ge(sem(f"piece{c % 3}_in"), piece_count(n, c))
            if after is not None:
                act.wait_ge(*after)
            hi, _, src = piece(c)
            nc.scalar.copy(hi, src).then_inc(sem("piece_hi"), 1)

        def root_ms(scratch, x, s, v, i, n_squares, n_roots):
            A_(scratch[:, :], x, ACT.Square, accum_out=s[:, i:i + 1]).then_inc(sem("squares"), 1)
            act.wait_ge(sem("squares"), n_squares + i + 1)
            A_(v[:, i:i + 1], s[:, i:i + 1], ACT.Sqrt, scale=1.0 / D, bias=eps[:, 0:1]).then_inc(sem("rstd"), 1)

        act.wait_ge(sem("ones"), 2)
        for i in range(NT):
            who = 0 if i == 8 else 1
            if i >= 1:
                act.wait_ge(sem("h2_turned"), i)
            if i == NT - 1:
                act.wait_ge(sem("o_done"), 2 * NT)
                piece_hi(0, 0)
                piece_hi(1, 1)
            act.wait_ge(sem("x2_made"), 2 * i + 2)
            root_ms(xn2, xr[i % 3][:, :], ss2, var2, i, 2 * NT, 3)
            act.wait_ge(sem("inverse_ms"), 3 + i + 1)
            A_(xn2[:, :], xr[i % 3][:, :], ACT.Copy, scale=rstd2[:, i:i + 1]).then_inc(sem("x2_normed"), 1)
            act.wait_ge(sem("h2_turned"), i + 1)
            if i >= 1:
                act.wait_ge(sem("h_split"), 3 * KT + i)
            for k in range(KT):
                last = A_(h2f[:, k, :], B[TB[i] + k // 4][:, P * (k % 4):P * (k % 4) + P], ACT.Identity,
                          scale=gsc[:, 1, k, who:who + 1], bias=modc[:, 24 + k, who:who + 1])
            last.then_inc(sem("h2_evac"), 1)


        def hidden(it, f, first, n0=0, n1=NB):
            for n in range(n0, n1):
                b = NB * f + n
                g = 2 * NB * it + b
                act.wait_ge(sem("gate_done"), g + 1)
                if not first or b >= 2:
                    act.wait_ge(sem("f_made"), g - 1)
                A_(sa[b % 2][:, :], B[b % 2][:, 0:BW], ACT.Silu).then_inc(sem("silu_made"), 1)
                act.wait_ge(sem("f_made"), g + 1)
                if not first:
                    act.wait_ge(sem("down_done"), 2 * NT * (it - 1) + 6 * (n + 1))
                nc.scalar.copy(f_hi[:, f, n * BW:(n + 1) * BW], fv[b % 2][:, :]).then_inc(sem("f_hi"), 1)

        def iteration(it, first, last):
            n0 = 4 + 6 * it
            if first:
                hidden(0, 0, True, 0, 1)
                piece_hi(2, 2)
                piece_hi(3, 3)
                hidden(0, 0, True, 1, NB)
            for f in range(FB):
                piece_hi(n0 + f, 4 + f, None if first else (sem("down_done"), 2 * NT * it))
            for f in range(FB):
                if not (first and f == 0):
                    hidden(it, f, first)
                if last and f == 0:
                    act.wait_ge(sem("gate_rows"), 2)
                    act.wait_ge(sem("piece_lo"), n0)
                    for who in range(2):
                        for h in range(2):
                            A_(g2b[who][:, 512 * h:512 * h + 512], B[4 + 2 * who + h][:, :], ACT.Copy).then_inc(sem("gate_evac"), 1)
                if not last:
                    for e in range(2):
                        piece_hi(n0 + 2 + 2 * f + e, 6 + 2 * f + e, (sem("up_done"), 2 * NB * it + NB * (f + 1)))

        iteration(0, True, False)
        with act.Fori(1, NFB - 1) as it:
            iteration(it, False, False)
        iteration(NFB - 1, False, True)
        for i in range(NT):
            act.wait_ge(sem("end_sum"), i + 1)
            root_ms(sq, acc[:, i, :], ss, var, i, 3 * NT, 3 + NT)
            if i < NT - 1:
                act.wait_ge(sem("inverse_ms"), 3 + NT + i + 1)
                A_(acc[:, i, :], acc[:, i, :], ACT.Copy, scale=rstd[:, i:i + 1]).then_inc(sem("end_normed"), 1)

    @block.vector
    def _(dve):
        TT, TS, STT = nc.vector.tensor_tensor, nc.vector.tensor_scalar, nc.vector.scalar_tensor_tensor
        steps = [0]

        def step(ins):
            steps[0] += 1
            ins.then_inc(sem("dve_step"), 1)
            dve.wait_ge(sem("dve_step"), steps[0])

        dve.wait_ge(sem("log_dt_in"), 16)
        nc.vector.tensor_copy(view(rlam, 4 * P, [[NS, 2], [1, NS]], 0, Q), view(ldt, 0, [[1, 2], [0, NS]], 0, Q)).then_inc(sem("dt_rows"), 1)
        dve.wait_ge(sem("params_turned"), 1)
        nc.vector.tensor_copy(pv[:, :], B[6][:, 0:NPV]).then_inc(sem("pv_evac"), 1)
        nc.vector.tensor_copy(dcol[:, :], B[7][0:32, 0:NPAIR]).then_inc(sem("pv_evac"), 1)
        dve.wait_ge(sem("pv_evac"), 2)
        lre, lim = pv[:, X_LRE:X_LRE + Q], pv[:, X_LIM:X_LIM + Q]
        p_ = lambda i: prm[:, i, :]
        dve.wait_ge(sem("polar"), 1)
        TT(p_(1), lre, p_(0), ALU.mult).then_inc(sem("lam_dt"), 1)
        TT(p_(2), lim, p_(0), ALU.mult).then_inc(sem("lam_dt"), 1)
        dve.wait_ge(sem("lam_dt"), 2)
        for a, b, turn in ((4, 5, 0.0), (6, 7, 0.25)):
            step(TS(p_(a), p_(2), 1.0 / TWO_PI, turn, ALU.mult, ALU.add))
            step(TS(p_(a), p_(a), ROUND, None, ALU.add))
            step(TS(p_(a), p_(a), ROUND, None, ALU.subtract))
            step(STT(p_(b), p_(a), -TP1, p_(2), ALU.mult, ALU.add))
            step(STT(p_(b), p_(a), -TP2, p_(b), ALU.mult, ALU.add))
            step(STT(p_(b), p_(a), -TP3, p_(b), ALU.mult, ALU.add))
            if turn:
                step(TS(p_(b), p_(b), TWO_PI / 4, None, ALU.add))
            TS(p_(b), p_(b), 3.1415925, -3.1415925, ALU.min, ALU.max).then_inc(sem("angles"), 1)
        step(nc.vector.memset(powr[:, 0, :], 1.0))
        step(nc.vector.memset(powi[:, 0, :], 0.0))
        dve.wait_ge(sem("polar"), 4)
        TT(powr[:, 1, :], p_(3), p_(9), ALU.mult)
        step(TT(powi[:, 1, :], p_(3), p_(8), ALU.mult))
        step(TT(p_(10), lre, lre, ALU.mult))
        step(TT(p_(11), lim, lim, ALU.mult))
        step(TT(p_(10), p_(10), p_(11), ALU.add))
        step(nc.vector.reciprocal(p_(10), p_(10)))
        step(TS(p_(11), powr[:, 1, :], -1.0, None, ALU.add))
        step(TT(p_(12), p_(11), lre, ALU.mult))
        step(TT(p_(14), powi[:, 1, :], lim, ALU.mult))
        step(TT(p_(12), p_(12), p_(14), ALU.add))
        step(TT(p_(12), p_(12), p_(10), ALU.mult))
        step(TT(p_(13), powi[:, 1, :], lre, ALU.mult))
        step(TT(p_(14), p_(11), lim, ALU.mult))
        step(TT(p_(13), p_(13), p_(14), ALU.subtract))
        step(TT(p_(13), p_(13), p_(10), ALU.mult))
        for lo, n in ((1, 1), (2, 2), (4, 4)):
            br, bi = view(powr, lo * Q, [[0, n], [1, Q]]), view(powi, lo * Q, [[0, n], [1, Q]])
            sr, si = powr[:, 1:1 + n, :], powi[:, 1:1 + n, :]
            t0, t1 = wbt_tmp[0][:, 0:n, 0:Q], wbt_tmp[1][:, 0:n, 0:Q]
            dr, di = powr[:, lo + 1:lo + 1 + n, :], powi[:, lo + 1:lo + 1 + n, :]
            step(TT(t0, br, sr, ALU.mult))
            step(TT(t1, bi, si, ALU.mult))
            step(TT(dr, t0, t1, ALU.subtract))
            step(TT(t0, br, si, ALU.mult))
            step(TT(t1, bi, sr, ALU.mult))
            step(TT(di, t0, t1, ALU.add))
        dve.sem_inc(sem("powers"), 1)
        def inverse_ms(s, v, i0, i1, name, ready, count):
            dve.wait_ge(sem(ready), count)
            n = i1 - i0
            step(TT(v[:, i0:i1], view(s, 2 * i0, [[2, n]]), view(s, 2 * i0 + 1, [[2, n]]), ALU.add))
            step(TS(v[:, i0:i1], v[:, i0:i1], 1.0 / D, EPS, ALU.mult, ALU.add))
            nc.vector.reciprocal(v[:, i0:i1], v[:, i0:i1]).then_inc(sem(name), 1)

        inverse_ms(ss, var, XG[0][0], XG[0][-1] + 1, "inverse_ms", "squares", 2 * (XG[0][-1] + 1))
        dve.wait_ge(sem("raws_turned"), 2)
        qre, qim = view(prm, 12 * Q, [[0, HD], [1, Q]]), view(prm, 13 * Q, [[0, HD], [1, Q]])
        bank = lambda b: B[b][:, :].rearrange("p (h q) -> p h q", q=Q)
        bout = lambda r: view(bb, r * Q * HD, [[1, HD], [HD, Q]])
        tv = [view(wbt_tmp[i], 0, [[1, HD], [HD, Q]]) for i in range(2)]
        step(TT(bout(0), bank(0), qre, ALU.mult))
        step(TT(tv[0], bank(1), qim, ALU.mult))
        step(TT(bout(1), bank(1), qre, ALU.mult))
        step(TT(tv[1], bank(0), qim, ALU.mult))
        TT(bout(0), bout(0), tv[0], ALU.subtract).then_inc(sem("bb_made"), 1)
        TT(bout(1), bout(1), tv[1], ALU.add).then_inc(sem("bb_made"), 1)
        dve.wait_ge(sem("ident"), 1)
        step(TT(dsel[:, 0, :], ident[0:32, 0:16], ident[0:32, 16:32], ALU.add))
        step(nc.vector.tensor_copy(view(dsel, HD, [[HD, NPAIR - 1], [1, HD]], 0, 32), view(dsel, 0, [[0, NPAIR - 1], [1, HD]], 0, 32)))
        TT(dsel[:, :, :], dsel[:, :, :], view(dcol, 0, [[1, NPAIR], [0, HD]], 0, 32), ALU.mult).then_inc(sem("dsel"), 1)


        dve.wait_ge(sem("cc_evac"), 2)
        dve.wait_ge(sem("raws_turned"), 4)
        for n in range(4):
            lr, li, cr, ci, v3 = wc_views(n)
            slot, tmp = wcd[n], wcd_tmp
            TT(v3(slot[0]), lr, cr, ALU.mult)
            step(TT(v3(tmp[0]), li, ci, ALU.mult))
            TT(v3(slot[1]), lr, ci, ALU.mult)
            step(TT(v3(tmp[1]), li, cr, ALU.mult))
            TT(slot[0][:, :, :], slot[0][:, :, :], tmp[0][:, :, :], ALU.add).then_inc(sem("wc_made_dve"), 1)
            TT(slot[1][:, :, :], slot[1][:, :, :], tmp[1][:, :, :], ALU.subtract).then_inc(sem("wc_made_dve"), 1)
            dve.wait_ge(sem("wc_made_dve"), 2 * (n + 1))

        def w_low(i):
            dve.wait_ge(sem("w_in_hi"), i + 1)
            TT(w_lo[i % 2][:, :, :], wst[i % 2][:, :, :], w_hi[i % 2][:, :, :].bitcast(F32), ALU.subtract).then_inc(low_ready(i)[0], 1)

        inverse_ms(ss, var, XG[1][0], XG[1][-1] + 1, "inverse_ms", "squares", 2 * (XG[1][-1] + 1))
        dve.wait_ge(sem("mod_evac"), 1)
        STT(gsc[:, 0, :, :], modc[:, 8:16, :], 1.0, view(pv, V_N1, [[1, KT], [0, 2]]), ALU.add, ALU.mult).then_inc(sem("gsc"), 1)
        dve.wait_ge(sem("wc_out2"), 128)
        def h_parts(n):
            grp, k = XG[n // KT], n % KT
            c0, w = P * grp[0], P * len(grp)
            return nt_hi[:, k, c0:c0 + w], nt_lo[:, k, c0:c0 + w], hf[n % 3][:, 0:w]

        def h_low(n):
            hi, lo, src = h_parts(n)
            dve.wait_ge(sem("h_hi"), n + 1)
            TT(lo, src, hi.bitcast(F32), ALU.subtract).then_inc(sem("h_split"), 1)

        for n in range(3 * KT):
            if n in (KT, 2 * KT):
                h_low(n - 1)
            if n == KT:
                w_low(0)
                inverse_ms(ss, var, XG[2][0], XG[2][-1] + 1, "inverse_ms", "squares", 2 * (XG[2][-1] + 1))
            if n == 2 * KT:
                w_low(1)
            hi, _, src = h_parts(n)
            dve.wait_ge(sem("h_evac"), n + 1)
            nc.vector.tensor_copy(hi, src).then_inc(sem("h_hi"), 1)
            if n % KT:
                h_low(n - 1)
        h_low(3 * KT - 1)

        def wbt_piece(j, d):
            n = 2 * j + d
            q0 = NPAIR * d + 4 * j
            step_, base = (-Q, (CH - 1) * Q) if d == 0 else (Q, 0)
            lr = view(powr, base + q0, [[1, 4], [step_, CH], [0, HD]])
            li = view(powi, base + q0, [[1, 4], [step_, CH], [0, HD]])
            br = view(bb, q0 * HD, [[HD, 4], [0, CH], [1, HD]])
            bi = view(bb, (Q + q0) * HD, [[HD, 4], [0, CH], [1, HD]])
            v3 = lambda t: view(t, 0, [[P, 4], [HD, CH], [1, HD]])
            out, tmp = wbt[d], wbt_tmp
            if n == 0:
                dve.wait_ge(sem("bb_made"), 2)
            if j >= 1:
                dve.wait_ge(sem("wb_turned"), 4 * (j - 1) + 2 * d + 2)
            if n >= 1:
                dve.wait_ge(sem("wbt_made"), 2 * n)
            TT(v3(out[0]), lr, br, ALU.mult).then_inc(sem("wbt_terms"), 1)
            TT(v3(tmp[0]), li, bi, ALU.mult).then_inc(sem("wbt_terms"), 1)
            TT(v3(out[1]), lr, bi, ALU.mult).then_inc(sem("wbt_terms"), 1)
            TT(v3(tmp[1]), li, br, ALU.mult).then_inc(sem("wbt_terms"), 1)
            dve.wait_ge(sem("wbt_terms"), 4 * n + 2)
            TT(out[0][:, :, :], out[0][:, :, :], tmp[0][:, :, :], ALU.subtract).then_inc(sem("wbt_made"), 1)
            dve.wait_ge(sem("wbt_terms"), 4 * n + 4)
            TT(out[1][:, :, :], out[1][:, :, :], tmp[1][:, :, :], ALU.add).then_inc(sem("wbt_made"), 1)

        for j in range(4):
            wbt_piece(j, 0)
            wbt_piece(j, 1)
            w_low(j + 2)
        dve.wait_ge(sem("wbt_made"), 16)
        nc.vector.tensor_copy(a8r[:, :], powr[:, CH, :]).then_inc(sem("a8_copied"), 1)
        TS(a8i[:, 0, :], powi[:, CH, :], -1.0, None, ALU.mult).then_inc(sem("a8_copied"), 1)
        nc.vector.tensor_copy(a8i[:, 1, :], powi[:, CH, :]).then_inc(sem("a8_copied"), 1)
        dve.wait_ge(sem("a8_copied"), 3)
        dve.wait_ge(sem("v_evac"), 32)
        for r, x in enumerate((X_HRE, X_HIM)):
            nc.vector.tensor_copy(view(st, r * Q * SLOTS, [[SLOTS, NPAIR]]), pv[:, x:x + NPAIR]).then_inc(sem("h0"), 1)
            nc.vector.tensor_copy(view(st, (r * Q + NPAIR) * SLOTS + BSH, [[SLOTS, NPAIR]]), pv[:, x + NPAIR:x + Q]).then_inc(sem("h0"), 1)
            nc.vector.memset(view(st, (r * Q + NPAIR) * SLOTS, [[SLOTS, NPAIR]]), 0.0).then_inc(sem("h0"), 1)
        dve.wait_ge(sem("h0"), 6)
        DL = NPAIR * SLOTS + BSH
        DC = NPAIR * SLOTS - (LC + 1)
        count = [0]

        def state(base, dstep, k, flip=False):
            rs = -Q * SLOTS if flip else Q * SLOTS
            return view(st, base + k + (Q * SLOTS if flip else 0), [[rs, 2], [dstep, 2], [SLOTS, NPAIR]])

        ar = view(a8r, 0, [[0, 2], [NPAIR, 2], [1, NPAIR]])
        ai = view(a8i, 0, [[Q, 2], [NPAIR, 2], [1, NPAIR]])
        tt = lambda t, i: view(t, i * 2 * Q, [[Q, 2], [NPAIR, 2], [1, NPAIR]])

        def scan_step(chains):
            for name, t, base, dstep, k in chains:
                TT(tt(t, 0), ar, state(base, dstep, k), ALU.mult).then_inc(sem(name), 1)
                TT(tt(t, 1), ai, state(base, dstep, k, True), ALU.mult).then_inc(sem(name), 1)
            for name, t, base, dstep, k in chains:
                dve.wait_ge(sem(name), 4 * k + 1)
                TT(tt(t, 2), tt(t, 0), state(base, dstep, k + 1), ALU.add).then_inc(sem(name), 1)
            for name, t, base, dstep, k in chains:
                dve.wait_ge(sem(name), 4 * k + 3)
                TT(state(base, dstep, k + 1), tt(t, 2), tt(t, 1), ALU.add).then_inc(sem(name), 1)
            for name, t, base, dstep, k in chains:
                dve.wait_ge(sem(name), 4 * k + 4)

        for k in range(LC):
            chains = [("latent_step", scT, 0, DL, k)]
            if k < CC:
                chains.append(("context_step", scC, LC + 1, DC, k))
            scan_step(chains)
        nc.vector.tensor_copy(tt(scT, 0), state(UC, NPAIR * SLOTS - LC - 1, 0)).then_inc(sem("scan_done"), 1)

        dve.wait_ge(sem("gated"), 4)
        for tap in range(TAPS):
            for j in range(2):
                w = pv[:, X_TAP + 2 * tap + j:X_TAP + 2 * tap + j + 1]
                src = vp[:, j, tap:tap + VO]
                if tap == 0:
                    TS(cacc[:, j, :], src, w, pv[:, V_CB + j:V_CB + j + 1], ALU.mult, ALU.add).then_inc(sem("tap_done"), 1)
                else:
                    dve.wait_ge(sem("tap_done"), 2 * tap + j - 1)
                    STT(cacc[:, j, :], src, w, cacc[:, j, :], ALU.mult, ALU.add).then_inc(sem("tap_done" if tap < TAPS - 1 else "conv_made"), 1)
        def glu_out(m):
            dve.wait_ge(sem("glu_gate"), NB * (m + 1))
            if m >= 2:
                dve.wait_ge(sem("y_part_dve"), m - 1)
            for c0, o, n in ((0, 0, LC), (LC + 1, LAT, CC)):
                last = TT(view(ym[m % 2], o, [[1, CH], [CH, n]]), view(yT, m * CH * UC + c0, [[UC, CH], [1, n]]),
                          view(gsig, c0, [[UC, CH], [1, n]]), ALU.mult)
            last.then_inc(sem("glu_made"), 1)

        def y_low(k, src, dst):
            TT(dst, src, y_hi[k][:, :].bitcast(F32), ALU.subtract).then_inc(sem("y_part_dve"), 1)

        glu_out(0)
        dve.wait_ge(sem("conv_made"), 2)
        for b in range(NB):
            dve.wait_ge(sem("channels_meant"), b + 1)
            for j in range(2):
                TT(cacc[:, j, 389 * b:389 * b + 389], cacc[:, j, 389 * b:389 * b + 389], B[1 + b][:, 0:389], ALU.subtract).then_inc(sem("deviation"), 1)
        glu_out(1)
        dve.wait_ge(sem("y_part_act"), 3)
        y_low(0, ym[0][:, :], y_lo[0][:, :])
        dve.wait_ge(sem("deviation"), 6)
        for b in range(NB):
            dve.wait_ge(sem("ln_root"), b + 1)
            step(nc.vector.reciprocal(view(sig, 389 * b, [[1, 389]]), view(sig, 389 * b, [[1, 389]])))
        glu_out(2)
        for j in range(2):
            TT(cacc[:, j, :], cacc[:, j, :], view(sig, 0, [[1, VO]]), ALU.mult).then_inc(sem("ln_scaled"), 1)
        dve.wait_ge(sem("y_part_act"), 4)
        dve.wait_ge(sem("glu_made"), 2)
        y_low(1, ym[1][:, :], y_lo[1][:, :])
        glu_out(3)
        dve.wait_ge(sem("glu_made"), 4)
        dve.wait_ge(sem("glu_done"), 12)
        for m in (2, 3):
            nc.vector.tensor_copy(y_hi[m][:, :], ym[m % 2][:, :]).then_inc(sem("y_part_dve"), 1)
        for j in range(2):
            dve.wait_ge(sem("conv_out"), 2 * j + 2)
            for c0, o, m in ((0, 0, LAT), (VCTX, LAT, CTX)):
                TT(y_lo[6 + j][:, o:o + m], cacc[:, j, c0:c0 + m], y_hi[6 + j][:, o:o + m].bitcast(F32), ALU.subtract).then_inc(sem("y_part_dve"), 1)
        dve.wait_ge(sem("y_part_dve"), 8)
        dve.wait_ge(sem("mod_evac"), 3)
        STT(gsc[:, 1, :, :], modc[:, 32:40, :], 1.0, view(pv, V_N2, [[1, KT], [0, 2]]), ALU.add, ALU.mult).then_inc(sem("gsc"), 1)
        dve.wait_ge(sem("gate_evac"), 4)
        dve.wait_ge(sem("ln_scaled"), 2)

        def inverse_root(r, v, i, n_roots):
            dve.wait_ge(sem("rstd"), n_roots + i + 1)
            nc.vector.reciprocal(r[:, i:i + 1], v[:, i:i + 1]).then_inc(sem("inverse_ms"), 1)

        def h2_split(i):
            dve.wait_ge(sem("h2_evac"), i + 1)
            hi, lo = nt_hi[:, :, P * i:P * i + P], nt_lo[:, :, P * i:P * i + P]
            nc.vector.tensor_copy(hi, h2f[:, :, :]).then_inc(sem("h_hi"), 1)
            dve.wait_ge(sem("h_hi"), 3 * KT + i + 1)
            TT(lo, h2f[:, :, :], hi.bitcast(F32), ALU.subtract).then_inc(sem("h_split"), 1)

        for i in range(NT):
            who = 0 if i == 8 else 1
            if i < 8:
                dve.wait_ge(sem("pos_half"), 2 * (8 + i + 1))
            else:
                dve.wait_ge(sem("xr2_in"), 48)
            for h in range(2):
                c = 2 * i + h
                dve.wait_ge(sem("o_done"), c + 1)
                if c >= 1:
                    dve.wait_ge(sem("x2_made"), c)
                step(TT(tg[:, :], B[4 + c % 4][:, :], g1b[:, who, 512 * h:512 * h + 512], ALU.mult))
                TT(xr[i % 3][:, 512 * h:512 * h + 512], xr[i % 3][:, 512 * h:512 * h + 512], tg[:, :], ALU.add).then_inc(sem("x2_made"), 1)
            inverse_root(rstd2, var2, i, 3)
            if i >= 1:
                h2_split(i - 1)
        h2_split(NT - 1)

        def hidden_block(it, f, n, first):
            b = NB * f + n
            g = 2 * NB * it + b
            dve.wait_ge(sem("silu_made"), g + 1)
            dve.wait_ge(sem("up_done"), g + 1)
            if not first or b >= 2:
                dve.wait_ge(sem("f_lo"), g - 1)
            TT(fv[b % 2][:, :], sa[b % 2][:, :], B[2 + b % 2][:, 0:BW], ALU.mult).then_inc(sem("f_made"), 1)

        def hidden(it, first):
            for f in range(FB):
                for n in range(NB):
                    hidden_block(it, f, n, first)

        def gather(it, first):
            if first:
                for s in range(3):
                    dve.wait_ge(sem(f"tile_out{s}"), 48)
            if not first:
                dve.wait_ge(sem("acc_done"), 2 * NT * it)
            for c in range(2 * NT):
                a = acc[:, c // 2, 512 * (c % 2):512 * (c % 2) + 512]
                dve.wait_ge(sem("down_done"), 2 * NT * it + c + 1)
                if first:
                    nc.vector.tensor_copy(a, B[4 + c % 4][:, :]).then_inc(sem("acc_done"), 1)
                else:
                    TT(a, a, B[4 + c % 4][:, :], ALU.add).then_inc(sem("acc_done"), 1)

        hidden(0, True)
        gather(0, True)
        with dve.Fori(1, NFB - 1) as it:
            hidden(it, False)
            gather(it, False)
        def gate_sum(i):
            if i == 0:
                dve.wait_ge(sem("gate_evac"), 8)
                dve.wait_ge(sem("acc_done"), 2 * NT * (NFB - 1))
            step(TT(acc[:, i, :], acc[:, i, :], g2b[0 if i == 8 else 1][:, :], ALU.mult))

        def add_residual(i):
            dve.wait_ge(sem(f"x{i}_in"), 48 if i < 8 else 32)
            TT(acc[:, i, :], acc[:, i, :], xe[i % 4][:, :], ALU.add).then_inc(sem("x2_added"), 1)

        for b in range(2 * NB):
            hidden_block(NFB - 1, b // NB, b % NB, False)
            for i in {2: range(0, 5), 3: range(5, NT)}.get(b, ()):
                gate_sum(i)
            for i in {3: range(0, 2), 4: range(2, 6), 5: range(6, NT)}.get(b, ()):
                add_residual(i)
        for i in range(NT):
            if i >= 2:
                dve.wait_ge(sem("end_sum"), i - 1)
            for h in range(2):
                c = 2 * i + h
                dve.wait_ge(sem("down_done"), 2 * NT * (NFB - 1) + c + 1)
                TT(te[i % 2][:, 512 * h:512 * h + 512], B[4 + c % 4][:, :], g2b[0 if i == 8 else 1][:, 512 * h:512 * h + 512], ALU.mult).then_inc(sem("acc_done"), 1)
            if i >= 1:
                inverse_root(rstd, var, i - 1, 3 + NT)
            dve.wait_ge(sem("acc_done"), 2 * NT * (NFB - 1) + 2 * i + 2)
            dve.wait_ge(sem("x2_added"), i + 1)
            TT(acc[:, i, :], acc[:, i, :], te[i % 2][:, :], ALU.add).then_inc(sem("end_sum"), 1)
        inverse_root(rstd, var, NT - 1, 3 + NT)
        dve.wait_ge(sem("final_g_in"), 16)
        dve.wait_ge(sem("inverse_ms"), 3 + 2 * NT)
        dve.wait_ge(sem("end_sum"), NT)
        STT(acc[:, NT - 1, :], acc[:, NT - 1, :], rstd[:, NT - 1:NT], fgb[:, :], ALU.mult, ALU.mult).then_inc(sem("last_y_made"), 1)

    ctx.close()


_INS = ['x_prompt', 'x_sample', 'state_ssm_re', 'state_ssm_im', 'c', 'c_ctx', 'ada_w', 'ada_b', 'norm1_g', 'w_in',
        'ssm_lam_re', 'ssm_lam_im', 'ssm_log_dt', 'ssm_b_re', 'ssm_b_im', 'ssm_c_re', 'ssm_c_im', 'ssm_d',
        'ssm_w_glu', 'ssm_b_glu', 'pool_w', 'pool_scale', 'conv_dw_w', 'conv_dw_b', 'conv_ln_g', 'conv_ln_b',
        'w_out', 'norm2_g', 'ffn_w1', 'ffn_w3', 'ffn_w2', 'final_g']
_OUTS = [(1, 128, 1024), (1, 1024, 1024), (1, 1, 2, 32, 64), (1, 1, 2, 32, 64)]


def shape_constants():
    quarter = D // 4
    omega = (1.0 / (10000.0 ** (np.arange(quarter, dtype=np.float32) / np.float32(quarter)))).astype(np.float32)

    def waves(n):
        a = np.arange(n, dtype=np.float32)[:, None] * omega[None]
        return np.concatenate([np.sin(a), np.cos(a)], axis=1).astype(np.float32)

    edges = np.ones((P, 34), np.float32)
    for g, w in enumerate((2, 4, 8, 16)):
        p0, j = 64 * (g % 2), g // 2
        edges[p0:p0 + 64, j] = 1.0 / w
        for i in range(8):
            edges[p0:p0 + 64, 2 + 16 * j + i] = w / (min(i + w // 2, LAT) - max(i - w // 2, 0))
            t = LAT - 8 + i
            edges[p0:p0 + 64, 2 + 16 * j + 8 + i] = w / (min(t + w // 2, LAT) - max(t - w // 2, 0))
    return {"pos_rows": waves(LAT // GRID_W), "pos_cols": waves(GRID_W), "pool_edges": edges}


def kernel(**inputs):
    import concourse.bacc as bacc
    from concourse.bass_utils import run_bass_kernel_spmd

    nc = bacc.Bacc("TRN2", target_bir_lowering=False, num_devices=1)
    arrays = {name: np.ascontiguousarray(inputs[name]) for name in _INS}
    arrays.update(shape_constants())
    ins = {name: nc.dram_tensor(f"in_{name}", a.shape, mybir.dt.from_np(a.dtype), kind="ExternalInput").ap() for name, a in arrays.items()}
    outs = [nc.dram_tensor(f"out_{i}", shape, F32, kind="ExternalOutput").ap() for i, shape in enumerate(_OUTS)]
    build(nc, ins, outs)
    r = run_bass_kernel_spmd(nc, [{f"in_{name}": a for name, a in arrays.items()}], core_ids=[0])
    return tuple(r.results[0][f"out_{i}"] for i in range(len(_OUTS)))
```
